# Optimizing a Trainium2 kernel written in Bass

```python
import math
import jax
import jax.numpy as jnp
from jax import lax
import numpy as np
import jax, jax.numpy as jnp

D_MODEL = 1024
BATCH = 1
SEQ = 256
DEPTH = 1

N_META = 16
D_MIX = 2 * D_MODEL
EPS = 1e-6
HG_WIDTH = D_MIX // 2
HG_DK = 128
HG_HEADS = HG_WIDTH // 128
HG_DV = HG_WIDTH // HG_HEADS
HG_KEY = HG_HEADS * HG_DK
HG_CHUNK = 16
M2_WIDTH = D_MIX - HG_WIDTH
M2_HEADDIM = 64
M2_HEADS = M2_WIDTH // M2_HEADDIM
M2_STATE = 128
M2_GROUPS = 2
M2_HPG = M2_HEADS // M2_GROUPS
M2_GN = M2_GROUPS * M2_STATE
M2_XBC = M2_WIDTH + 2 * M2_GN
M2_CONV = 4
M2_CHUNK = 64
DT_MIN = 1e-3
DT_MAX = 1e-1
D_FF = 2816
FFN_CONV = 3
PROJ_SIZES = (HG_KEY, HG_KEY, HG_WIDTH, HG_WIDTH, M2_WIDTH, M2_XBC, M2_HEADS)
D_PROJ = sum(PROJ_SIZES)
PROJ_SPLITS = tuple(int(v) for v in np.cumsum(PROJ_SIZES)[:-1])


def rmsnorm(x, w):
    xf = x.astype(jnp.float32)
    y = xf * lax.rsqrt(jnp.mean(xf * xf, axis=-1, keepdims=True) + EPS)
    return (y * w.astype(jnp.float32)).astype(x.dtype)

def causal_dwconv(x, w, b):
    k_taps, length = w.shape[0], x.shape[1]
    xp = jnp.pad(x, ((0, 0), (k_taps - 1, 0), (0, 0)))
    y = b + xp[:, 0:length] * w[0]
    for k in range(1, k_taps):
        y = y + xp[:, k:k + length] * w[k]
    return y

def front_pad(t, n):
    return jnp.pad(t, ((0, 0), (n, 0)) + ((0, 0),) * (t.ndim - 2))

def to_chunks(t, c):
    return t.reshape((t.shape[0], t.shape[1] // c, c) + t.shape[2:])

def hgrn2_mixer(q, f_pre, i_in, g, lb, norm_w):
    bsz, length, _ = q.shape
    f32 = jnp.float32
    f = lb + (1.0 - lb) * jax.nn.sigmoid(f_pre.astype(f32))
    k = 1.0 - f
    log_f = jnp.log(f)
    qa = jax.nn.silu(q.astype(f32))
    pad = (-N_META) % HG_CHUNK
    lp = length + pad

    def prep(t, d):
        return to_chunks(front_pad(t, pad).reshape(bsz, lp, HG_HEADS, d), HG_CHUNK)

    qc, kc, gc = prep(qa, HG_DK), prep(k, HG_DK), prep(log_f, HG_DK)
    vc = prep(i_in.astype(f32), HG_DV)
    bcum = jnp.cumsum(gc, axis=2)
    blast = bcum[:, :, -1]
    q_dec = qc * jnp.exp(bcum)
    k_inv = kc * jnp.exp(-bcum)
    k_end = kc * jnp.exp(blast[:, :, None] - bcum)
    causal = jnp.tril(jnp.ones((HG_CHUNK, HG_CHUNK), dtype=bool))
    scores = jnp.einsum('bnrhk,bnshk->bnhrs', q_dec, k_inv)
    scores = jnp.where(causal, scores, 0.0)
    o_intra = jnp.einsum('bnhrs,bnshv->bnrhv', scores, vc)

    def step(state, inp):
        q_n, k_n, v_n, d_n = inp
        o_n = jnp.einsum('brhk,bhkv->brhv', q_n, state)
        state = d_n[..., None] * state + jnp.einsum('brhk,brhv->bhkv', k_n, v_n)
        return state, o_n

    s0 = jnp.zeros((bsz, HG_HEADS, HG_DK, HG_DV), f32)
    xs = (jnp.moveaxis(q_dec, 1, 0), jnp.moveaxis(k_end, 1, 0),
          jnp.moveaxis(vc, 1, 0), jnp.moveaxis(jnp.exp(blast), 1, 0))
    _, o_inter = lax.scan(step, s0, xs)
    o = o_intra + jnp.moveaxis(o_inter, 0, 1)
    o = o.reshape(bsz, lp, HG_HEADS, HG_DV)[:, pad:]
    o = o * lax.rsqrt(jnp.mean(o * o, axis=-1, keepdims=True) + EPS)
    o = o.reshape(bsz, length, HG_WIDTH) * norm_w.astype(f32)
    return (o * jax.nn.silu(g.astype(f32))).astype(q.dtype)

def mamba2_mixer(z, xbc, dt_pre, conv_w, conv_b, dt_bias, a_log, d_skip, norm_w):
    bsz, length, _ = z.shape
    f32 = jnp.float32
    xbc = jax.nn.silu(causal_dwconv(xbc, conv_w, conv_b).astype(f32))
    x_in = xbc[..., :M2_WIDTH].reshape(bsz, length, M2_GROUPS, M2_HPG, M2_HEADDIM)
    b_in = xbc[..., M2_WIDTH:M2_WIDTH + M2_GN].reshape(bsz, length, M2_GROUPS, M2_STATE)
    c_in = xbc[..., M2_WIDTH + M2_GN:].reshape(bsz, length, M2_GROUPS, M2_STATE)
    dt = jax.nn.softplus(dt_pre.astype(f32) + dt_bias.astype(f32))
    dt = dt.reshape(bsz, length, M2_GROUPS, M2_HPG)
    a = -jnp.exp(a_log.astype(f32)).reshape(M2_GROUPS, M2_HPG)
    da = dt * a
    xdt = x_in * dt[..., None]
    pad = (-N_META) % M2_CHUNK
    lp = length + pad
    xc = to_chunks(front_pad(xdt, pad), M2_CHUNK)
    ac = to_chunks(front_pad(da, pad), M2_CHUNK)
    bc = to_chunks(front_pad(b_in, pad), M2_CHUNK)
    cc = to_chunks(front_pad(c_in, pad), M2_CHUNK)
    a_cum = jnp.cumsum(ac, axis=2)
    causal = jnp.tril(jnp.ones((M2_CHUNK, M2_CHUNK), dtype=bool))
    seg = a_cum[:, :, :, None] - a_cum[:, :, None, :]
    l_mat = jnp.exp(jnp.where(causal[:, :, None, None], seg, -jnp.inf))
    cb = jnp.einsum('bnigs,bnjgs->bnijg', cc, bc)
    y_diag = jnp.einsum('bnijgh,bnjghp->bnighp', cb[..., None] * l_mat, xc)
    decay_to_end = jnp.exp(a_cum[:, :, -1:] - a_cum)
    u = jnp.einsum('bnjgs,bnjghp->bnghps', bc, xc * decay_to_end[..., None])
    chunk_decay = jnp.exp(a_cum[:, :, -1])

    def step(state, inp):
        c_n, e_n, u_n, d_n = inp
        y_n = jnp.einsum('bigs,bghps->bighp', c_n, state) * e_n[..., None]
        state = d_n[..., None, None] * state + u_n
        return state, y_n

    s0 = jnp.zeros((bsz, M2_GROUPS, M2_HPG, M2_HEADDIM, M2_STATE), f32)
    xs = (jnp.moveaxis(cc, 1, 0), jnp.moveaxis(jnp.exp(a_cum), 1, 0),
          jnp.moveaxis(u, 1, 0), jnp.moveaxis(chunk_decay, 1, 0))
    _, y_off = lax.scan(step, s0, xs)
    y = y_diag + jnp.moveaxis(y_off, 0, 1)
    y = y.reshape(bsz, lp, M2_GROUPS, M2_HPG, M2_HEADDIM)[:, pad:]
    y = y + d_skip.astype(f32).reshape(M2_GROUPS, M2_HPG, 1) * x_in
    y = y.reshape(bsz, length, M2_WIDTH) * jax.nn.silu(z.astype(f32))
    yg = y.reshape(bsz, length, M2_GROUPS, M2_WIDTH // M2_GROUPS)
    yg = yg * lax.rsqrt(jnp.mean(yg * yg, axis=-1, keepdims=True) + EPS)
    y = yg.reshape(bsz, length, M2_WIDTH) * norm_w.astype(f32)
    return y.astype(z.dtype)

def conv_glu_ffn(h, w_up, conv_w, conv_b, w_down):
    u = causal_dwconv(h @ w_up, conv_w, conv_b)
    gate, val = jnp.split(u, 2, axis=-1)
    return (jax.nn.silu(gate) * val) @ w_down

def first_inputs(seed: int = 0) -> dict:
    key = jax.random.key(seed)
    ks = jax.random.split(key, 20)
    f32 = jnp.float32

    def nrm(k, shape, scale):
        return scale * jax.random.normal(k, shape, f32)

    def gain(k, shape):
        return 1.0 + 0.05 * jax.random.normal(k, shape, f32)

    dt0 = jnp.exp(jax.random.uniform(ks[8], (DEPTH, M2_HEADS), f32,
                                     minval=math.log(DT_MIN), maxval=math.log(DT_MAX)))
    dt_bias = dt0 + jnp.log(-jnp.expm1(-dt0))
    a_log = jnp.log(jax.random.uniform(ks[9], (DEPTH, M2_HEADS), f32, minval=1.0, maxval=16.0))
    return {
        'x': nrm(ks[0], (BATCH, SEQ, D_MODEL), 1.0),
        'meta_tokens': nrm(ks[1], (N_META, D_MODEL), 1.0),
        'norm1_w': gain(ks[2], (DEPTH, D_MODEL)),
        'w_in': nrm(ks[3], (DEPTH, D_MODEL, D_PROJ), D_MODEL ** -0.5),
        'hg_lb_logits': nrm(ks[4], (DEPTH + 1, HG_KEY), 0.1),
        'hg_norm_w': gain(ks[5], (DEPTH, HG_WIDTH)),
        'm2_conv_w': nrm(ks[6], (DEPTH, M2_CONV, M2_XBC), M2_CONV ** -0.5),
        'm2_conv_b': nrm(ks[7], (DEPTH, M2_XBC), 0.02),
        'm2_dt_bias': dt_bias,
        'm2_a_log': a_log,
        'm2_d': gain(ks[10], (DEPTH, M2_HEADS)),
        'm2_norm_w': gain(ks[11], (DEPTH, M2_WIDTH)),
        'w_out': nrm(ks[12], (DEPTH, D_MIX, D_MODEL), D_MIX ** -0.5),
        'norm2_w': gain(ks[13], (DEPTH, D_MODEL)),
        'ffn_w_up': nrm(ks[14], (DEPTH, D_MODEL, 2 * D_FF), D_MODEL ** -0.5),
        'ffn_conv_w': nrm(ks[15], (DEPTH, FFN_CONV, 2 * D_FF), FFN_CONV ** -0.5),
        'ffn_conv_b': nrm(ks[16], (DEPTH, 2 * D_FF), 0.02),
        'ffn_w_down': nrm(ks[17], (DEPTH, D_FF, D_MODEL), D_FF ** -0.5),
        'final_norm_w': gain(ks[18], (D_MODEL,)),
    }

def first_block(x, meta_tokens, norm1_w, w_in, hg_lb_logits, hg_norm_w, m2_conv_w, m2_conv_b,
              m2_dt_bias, m2_a_log, m2_d, m2_norm_w, w_out, norm2_w, ffn_w_up, ffn_conv_w,
              ffn_conv_b, ffn_w_down, final_norm_w):
    bsz = x.shape[0]
    meta = jnp.broadcast_to(meta_tokens.astype(x.dtype)[None], (bsz, N_META, D_MODEL))
    h = jnp.concatenate([meta, x], axis=1)
    lbs = jnp.cumsum(jax.nn.softmax(hg_lb_logits.astype(jnp.float32), axis=0), axis=0)
    for l in range(DEPTH):
        u = rmsnorm(h, norm1_w[l])
        proj = u @ w_in[l]
        hg_q, hg_f, hg_i, hg_g, m2_z, m2_xbc, m2_dt = jnp.split(proj, PROJ_SPLITS, axis=-1)
        out_a = hgrn2_mixer(hg_q, hg_f, hg_i, hg_g, lbs[l], hg_norm_w[l])
        out_b = mamba2_mixer(m2_z, m2_xbc, m2_dt, m2_conv_w[l], m2_conv_b[l], m2_dt_bias[l],
                             m2_a_log[l], m2_d[l], m2_norm_w[l])
        h = h + jnp.concatenate([out_a, out_b], axis=-1) @ w_out[l]
        h = h + conv_glu_ffn(rmsnorm(h, norm2_w[l]), ffn_w_up[l], ffn_conv_w[l],
                             ffn_conv_b[l], ffn_w_down[l])
    y = rmsnorm(h, final_norm_w)
    return y[:, N_META:, :]


GRID_W = 64
CTX_LEN = 256
CONV_WIDTH = D_MODEL // 2
RET_HEADS = 4
RET_HEAD_DIM = (D_MODEL - CONV_WIDTH) // RET_HEADS
RET_WIDTH = RET_HEADS * RET_HEAD_DIM
MIX_WIDTH = CONV_WIDTH + RET_WIDTH
RET_CHUNK = 128
ROPE_BASE = 10000.0
N_EXPERTS = 16
EC_CAPACITY_FACTOR = 2
D_EXPERT = 2 * D_MODEL
RMS_EPS = 1e-6
GN_EPS = 1e-6
SPLITS = (CONV_WIDTH, CONV_WIDTH, CONV_WIDTH, RET_WIDTH, RET_WIDTH, RET_WIDTH, RET_WIDTH)
IN_COLS = sum(SPLITS)
SPLIT_IDX = tuple(int(s) for s in np.cumsum(SPLITS)[:-1])


def _rms_norm(x, g):
    xf = x.astype(jnp.float32)
    y = xf * lax.rsqrt(jnp.mean(xf * xf, axis=-1, keepdims=True) + RMS_EPS)
    return (y * g.astype(jnp.float32)).astype(x.dtype)

def _modulation(cond, w_ada, b_ada):
    m = jax.nn.silu(cond) @ w_ada + b_ada
    return jnp.split(m[:, None, :], 6, axis=-1)

def _rotary(t, pos):
    half = t.shape[-1] // 2
    inv = 1.0 / (ROPE_BASE ** (jnp.arange(half, dtype=jnp.float32) / half))
    ang = pos[:, None] * inv[None, :]
    cos = jnp.cos(ang)[None, :, None, :]
    sin = jnp.sin(ang)[None, :, None, :]
    t1, t2 = t[..., :half], t[..., half:]
    return jnp.concatenate([t1 * cos - t2 * sin, t1 * sin + t2 * cos], axis=-1)

def _ret_qkv(q, k, v, pos):
    b, n, _ = q.shape
    shp = (b, n, RET_HEADS, RET_HEAD_DIM)
    q = _rotary(q.reshape(shp).astype(jnp.float32), pos)
    k = _rotary(k.reshape(shp).astype(jnp.float32), pos) * (RET_HEAD_DIM ** -0.5)
    v = v.reshape(shp).astype(jnp.float32)
    return q, k, v

def _retention_scan(q, k, v, log_g, s0, include_self):
    b, n, h, d = q.shape
    nc = n // RET_CHUNK
    qc = q.reshape(b, nc, RET_CHUNK, h, d)
    kc = k.reshape(b, nc, RET_CHUNK, h, d)
    vc = v.reshape(b, nc, RET_CHUNK, h, d)
    idx = jnp.arange(RET_CHUNK, dtype=jnp.float32)
    rel = idx[:, None] - idx[None, :]
    mask = (rel >= 0) if include_self else (rel > 0)
    decay = jnp.where(mask[None], jnp.exp(log_g[:, None, None] * jnp.where(mask, rel, 0.0)[None]), 0.0)
    scores = jnp.einsum('bcihd,bcjhd->bchij', qc, kc) * decay[None, None]
    intra = jnp.einsum('bchij,bcjhd->bcihd', scores, vc)
    zeta = jnp.exp(log_g[None, :] * (RET_CHUNK - 1.0 - idx)[:, None])
    u = jnp.einsum('bcjhd,bcjhe->bchde', kc * zeta[None, None, :, :, None], vc)
    g_chunk = jnp.exp(log_g * RET_CHUNK)[None, :, None, None]

    def step(s, u_c):
        return g_chunk * s + u_c, s

    s_final, s_prev = lax.scan(step, s0, jnp.moveaxis(u, 1, 0))
    s_prev = jnp.moveaxis(s_prev, 0, 1)
    xi = jnp.exp(log_g[None, :] * (idx + 1.0)[:, None])
    inter = jnp.einsum('bcihd,bchde->bcihe', qc, s_prev) * xi[None, None, :, :, None]
    return (intra + inter).reshape(b, n, h, d), s_final

def _bidir_retention(q, k, v, log_gf, log_gb, s0_f, s0_b):
    y_f, s_f = _retention_scan(q, k, v, log_gf, s0_f, True)
    flip = lambda t: jnp.flip(t, axis=1)
    y_b, s_b = _retention_scan(flip(q), flip(k), flip(v), log_gb, s0_b, False)
    return y_f + flip(y_b), s_f, s_b

def _context_states(k, v, log_gf, log_gb):
    n = k.shape[1]
    pos = jnp.arange(n, dtype=jnp.float32)
    wf = jnp.exp(log_gf[None, :] * (n - 1.0 - pos)[:, None])
    wb = jnp.exp(log_gb[None, :] * pos[:, None])
    s_f = jnp.einsum('bnhd,nh,bnhe->bhde', k, wf, v)
    s_b = jnp.einsum('bnhd,nh,bnhe->bhde', k, wb, v)
    return s_f, s_b

def _ret_out(y, g, norm_g):
    b, n, _, _ = y.shape
    mu = jnp.mean(y, axis=-1, keepdims=True)
    var = jnp.mean(jnp.square(y - mu), axis=-1, keepdims=True)
    yn = ((y - mu) * lax.rsqrt(var + GN_EPS)).reshape(b, n, RET_WIDTH) * norm_g.astype(jnp.float32)
    return (jax.nn.silu(g.astype(jnp.float32)) * yn).astype(g.dtype)

def _conv_branch(gate_b, gate_c, u_in, w, bias, rows, width):
    bsz, n, ch = u_in.shape
    u = (gate_c * u_in).reshape(bsz, rows, width, ch)
    up = jnp.pad(u, ((0, 0), (0, 0), (1, 1), (0, 0)))
    y = up[:, :, :-2] * w[0] + up[:, :, 1:-1] * w[1] + up[:, :, 2:] * w[2] + bias
    return gate_b * y.reshape(bsz, n, ch)

def _expert_choice_ffn(h, w_router, b_router, w_gate, w_up, w_down):
    b, n, d = h.shape
    cap = max(1, EC_CAPACITY_FACTOR * n // N_EXPERTS)
    logits = h.astype(jnp.float32) @ w_router.astype(jnp.float32) + b_router.astype(jnp.float32)
    aff = jax.nn.softmax(logits, axis=-1)
    gate, idx = lax.top_k(jnp.swapaxes(aff, 1, 2), cap)
    xs = jax.vmap(lambda hb, ib: hb[ib])(h, idx)
    a = jnp.einsum('becd,edf->becf', xs, w_gate)
    u = jnp.einsum('becd,edf->becf', xs, w_up)
    y = jnp.einsum('becf,efd->becd', jax.nn.silu(a) * u, w_down) * gate[..., None].astype(h.dtype)
    return jax.vmap(lambda yb, ib: jnp.zeros((n, d), yb.dtype).at[ib.reshape(-1)].add(yb.reshape(-1, d)))(y, idx)

def second_inputs(seed: int = 0) -> dict:
    key = jax.random.key(seed)
    ks = jax.random.split(key, 22)
    f32 = jnp.float32

    def nrm(k, shape, scale):
        return jax.random.normal(k, shape, f32) * scale

    decay_base = jnp.log(2.0 ** (5.0 + jnp.arange(RET_HEADS, dtype=f32)) - 1.0)
    return {
        "x": nrm(ks[0], (BATCH, SEQ, D_MODEL), 1.0),
        "c": nrm(ks[1], (BATCH, D_MODEL), 1.0),
        "ctx": nrm(ks[2], (BATCH, CTX_LEN, D_MODEL), 1.0),
        "c_ctx": nrm(ks[3], (D_MODEL,), 1.0),
        "w_ada": nrm(ks[4], (DEPTH, D_MODEL, 6 * D_MODEL), 0.5 * D_MODEL ** -0.5),
        "b_ada": nrm(ks[5], (DEPTH, 6 * D_MODEL), 0.02),
        "pre_mix_g": 1.0 + nrm(ks[6], (DEPTH, D_MODEL), 0.05),
        "post_mix_g": 1.0 + nrm(ks[7], (DEPTH, D_MODEL), 0.05),
        "pre_ffn_g": 1.0 + nrm(ks[8], (DEPTH, D_MODEL), 0.05),
        "post_ffn_g": 1.0 + nrm(ks[9], (DEPTH, D_MODEL), 0.05),
        "w_in": nrm(ks[10], (DEPTH, D_MODEL, IN_COLS), D_MODEL ** -0.5),
        "conv_w": nrm(ks[11], (DEPTH, 3, CONV_WIDTH), 3.0 ** -0.5),
        "conv_b": nrm(ks[12], (DEPTH, CONV_WIDTH), 0.02),
        "ret_decay_logit": decay_base[None, None, :] + nrm(ks[13], (DEPTH, 2, RET_HEADS), 0.1),
        "ret_norm_g": 1.0 + nrm(ks[14], (DEPTH, RET_WIDTH), 0.05),
        "w_out": nrm(ks[15], (DEPTH, MIX_WIDTH, D_MODEL), MIX_WIDTH ** -0.5),
        "w_router": nrm(ks[16], (DEPTH, D_MODEL, N_EXPERTS), D_MODEL ** -0.5),
        "b_router": nrm(ks[17], (DEPTH, N_EXPERTS), 0.01),
        "w_gate": nrm(ks[18], (DEPTH, N_EXPERTS, D_MODEL, D_EXPERT), D_MODEL ** -0.5),
        "w_up": nrm(ks[19], (DEPTH, N_EXPERTS, D_MODEL, D_EXPERT), D_MODEL ** -0.5),
        "w_down": nrm(ks[20], (DEPTH, N_EXPERTS, D_EXPERT, D_MODEL), D_EXPERT ** -0.5),
    }

def second_block(x, c, ctx, c_ctx, w_ada, b_ada, pre_mix_g, post_mix_g, pre_ffn_g, post_ffn_g,
              w_in, conv_w, conv_b, ret_decay_logit, ret_norm_g, w_out,
              w_router, b_router, w_gate, w_up, w_down):
    n_lat = x.shape[1]
    ctx_len = ctx.shape[1]
    rows = n_lat // GRID_W
    pos_ctx = jnp.arange(ctx_len, dtype=jnp.float32)
    pos_lat = ctx_len + jnp.arange(n_lat, dtype=jnp.float32)
    bsz = x.shape[0]
    zero_state = jnp.zeros((bsz, RET_HEADS, RET_HEAD_DIM, RET_HEAD_DIM), jnp.float32)

    for i in range(DEPTH):
        last = i == DEPTH - 1
        sh1, sc1, g1, sh2, sc2, g2 = _modulation(c, w_ada[i], b_ada[i])
        csh1, csc1, cg1, csh2, csc2, cg2 = _modulation(c_ctx[None, :], w_ada[i], b_ada[i])
        log_gf = jax.nn.log_sigmoid(ret_decay_logit[i, 0].astype(jnp.float32))
        log_gb = jax.nn.log_sigmoid(ret_decay_logit[i, 1].astype(jnp.float32))

        hc = _rms_norm(ctx, pre_mix_g[i]) * (1.0 + csc1) + csh1
        c_b, c_c, c_x, c_q, c_k, c_v, c_g = jnp.split(hc @ w_in[i], SPLIT_IDX, axis=-1)
        qc, kc, vc = _ret_qkv(c_q, c_k, c_v, pos_ctx)
        if last:
            s_f, s_b = _context_states(kc, vc, log_gf, log_gb)
            ctx_next = ctx
        else:
            yc, s_f, s_b = _bidir_retention(qc, kc, vc, log_gf, log_gb, zero_state, zero_state)
            mix_c = jnp.concatenate([
                _conv_branch(c_b, c_c, c_x, conv_w[i], conv_b[i], 1, ctx_len),
                _ret_out(yc, c_g, ret_norm_g[i])], axis=-1) @ w_out[i]
            ctx_mid = ctx + cg1 * _rms_norm(mix_c, post_mix_g[i])
            hc2 = _rms_norm(ctx_mid, pre_ffn_g[i]) * (1.0 + csc2) + csh2
            ffn_c = _expert_choice_ffn(hc2, w_router[i], b_router[i], w_gate[i], w_up[i], w_down[i])
            ctx_next = ctx_mid + cg2 * _rms_norm(ffn_c, post_ffn_g[i])

        hx = _rms_norm(x, pre_mix_g[i]) * (1.0 + sc1) + sh1
        x_b, x_c, x_x, x_q, x_k, x_v, x_g = jnp.split(hx @ w_in[i], SPLIT_IDX, axis=-1)
        qx, kx, vx = _ret_qkv(x_q, x_k, x_v, pos_lat)
        yx, _, _ = _bidir_retention(qx, kx, vx, log_gf, log_gb, s_f, s_b)
        mix_x = jnp.concatenate([
            _conv_branch(x_b, x_c, x_x, conv_w[i], conv_b[i], rows, GRID_W),
            _ret_out(yx, x_g, ret_norm_g[i])], axis=-1) @ w_out[i]
        x = x + g1 * _rms_norm(mix_x, post_mix_g[i])
        hx2 = _rms_norm(x, pre_ffn_g[i]) * (1.0 + sc2) + sh2
        ffn_x = _expert_choice_ffn(hx2, w_router[i], b_router[i], w_gate[i], w_up[i], w_down[i])
        x = x + g2 * _rms_norm(ffn_x, post_ffn_g[i])
        ctx = ctx_next
    return x


def setup_inputs(seed=0):
    out = dict(first_inputs(seed))
    for name, value in second_inputs(seed + 1).items():
        if name != "x":
            out[name + "_2"] = value
    return out


def reference(
    x, meta_tokens, norm1_w, w_in, hg_lb_logits, hg_norm_w, m2_conv_w, m2_conv_b, m2_dt_bias,
    m2_a_log, m2_d, m2_norm_w, w_out, norm2_w, ffn_w_up, ffn_conv_w, ffn_conv_b, ffn_w_down,
    final_norm_w, c_2, ctx_2, c_ctx_2, w_ada_2, b_ada_2, pre_mix_g_2, post_mix_g_2, pre_ffn_g_2,
    post_ffn_g_2, w_in_2, conv_w_2, conv_b_2, ret_decay_logit_2, ret_norm_g_2, w_out_2,
    w_router_2, b_router_2, w_gate_2, w_up_2, w_down_2,
):
    x = first_block(
        x, meta_tokens, norm1_w, w_in, hg_lb_logits, hg_norm_w, m2_conv_w, m2_conv_b,
        m2_dt_bias, m2_a_log, m2_d, m2_norm_w, w_out, norm2_w, ffn_w_up, ffn_conv_w, ffn_conv_b,
        ffn_w_down, final_norm_w,
    )
    return second_block(
        x, c_2, ctx_2, c_ctx_2, w_ada_2, b_ada_2, pre_mix_g_2, post_mix_g_2, pre_ffn_g_2,
        post_ffn_g_2, w_in_2, conv_w_2, conv_b_2, ret_decay_logit_2, ret_norm_g_2, w_out_2,
        w_router_2, b_router_2, w_gate_2, w_up_2, w_down_2,
    )


_drawn_inputs = setup_inputs


def setup_inputs(seed=0):
    import zlib

    import numpy as np

    out = dict(_drawn_inputs(seed))
    spreads = {}
    factors = {'hg_lb_logits': 4.429,
     'post_ffn_g_2': 4.024,
     'conv_b_2': 3.062,
     'ret_norm_g_2': 3.85,
     'b_router_2': 4.817}
    for name, (base, spread) in spreads.items():
        noise = np.random.default_rng([zlib.crc32(name.encode()), seed]).standard_normal(out[name].shape)
        drawn = base * np.exp(spread * noise) if base else spread * noise
        out[name] = jnp.asarray(drawn.astype(out[name].dtype))
    for name, factor in factors.items():
        out[name] = (out[name] * factor).astype(out[name].dtype)
    return out
```

```python
from contextlib import ExitStack

import numpy as np
import concourse.bass as bass
from concourse import mybir

F32 = mybir.dt.float32
U32 = mybir.dt.uint32
ACT = mybir.ActivationFunctionType
ALU = mybir.AluOpType
AX = mybir.AxisListType.X

P = 128
D = 1024
KT = D // P
META, SEQ = 16, 256
T = META + SEQ
WINDOWS = [(0, 128), (128, 128), (256, 16)]
LEVELS = [16, 32, 64, 128]
HEADS = 8
M2H, M2P, M2G = 16, 64, 2
FF = 2816
FT = FF // P
L = 256
RH = 4
NE, CAP, DE = 16, 32, 2048
RING = 6
UNIT = 4096
TB = 6
BIG = 8

TQ, TF_, TI, TG, TZ, TX, TBM, TCM = 0, 8, 16, 24, 32, 40, 48, 50
NPROJ = 52


def par_rows():
    plan = [
        [("norm1", 8), ("lb0", 8), ("lb1", 8), ("hgn", 8), ("m2cw", 48), ("m2cb", 12), ("m2n", 8),
         ("norm2", 8), ("fin", 8)],
        [("ffw01", 88), ("prem", 8), ("postm", 8), ("pref", 8), ("postf", 8)],
        [("ffw2", 44), ("ffb", 44), ("cw2", 12), ("cb2", 4), ("retn", 4), ("c", 8), ("cctx", 8)],
        [("bada", 48)],
    ]
    where = {}
    for b, names in enumerate(plan):
        at = 0
        for name, n in names:
            where[name] = (b, at, n)
            at += n
    return where


PAR = par_rows()

CST = {}
_at = 0
for _name, _n in [("ident", P), ("rot", P), ("causal", P), ("mask", 4 * P), ("reset", 4 * T), ("sel2", 2),
                  ("slot", CAP), ("cos", 2 * L), ("sin", 2 * L)]:
    CST[_name] = (_at, _n)
    _at += _n
NCST = _at
NDIST = 8 * L


def constants():
    c = np.zeros((P, NCST), np.float32)

    def put(name, a):
        at, n = CST[name]
        c[:, at:at + n] = a

    i = np.arange(P)
    put("ident", np.eye(P))
    rot = np.zeros((P, P), np.float32)
    rot[i[64:], i[:64]] = -1.0
    rot[i[:64], i[64:]] = 1.0
    put("rot", rot)
    s, r = i[:, None], i[None, :]
    put("causal", s <= r)
    masks = [(s // 16 == r // 16) & (s <= r)]
    for w in LEVELS[1:]:
        masks.append((s // w == r // w) & (s % w < w // 2) & (r % w >= w // 2))
    put("mask", np.concatenate(masks, 1))
    t = np.arange(T)
    put("reset", np.tile(np.concatenate([t % w != 0 for w in LEVELS])[None], (P, 1)))
    put("sel2", (i[:, None] % 32) == np.arange(2)[None])
    put("slot", np.tile(np.arange(1, CAP + 1, dtype=np.float32)[None], (P, 1)))
    inv = (1.0 / (np.float32(10000.0) ** (np.arange(64, dtype=np.float32) / np.float32(64)))).astype(np.float32)
    pos = np.concatenate([L + np.arange(L), np.arange(L)]).astype(np.float32)
    ang = (pos[None, :] * inv[:, None]).astype(np.float32)
    n = np.arange(L)[None, :]
    lat = [np.maximum(n - (128 * k + s), 0) for k in range(2)] + [np.maximum((128 * k + s) - n, 0) for k in range(2)]
    ctx = [L + n - (128 * k + s) for k in range(2)] + [L - n + (128 * k + s) for k in range(2)]
    dist = np.concatenate(lat + ctx + [np.tile(f(ang), (2, 1)) for f in (np.cos, np.sin)], 1).astype(np.float32)
    return c, dist


class Steps:

    def __init__(self, engine, sem):
        self.engine, self.sem, self.n, self.turn = engine, sem, 0, 0

    def __call__(self, ins):
        self.n += 1
        ins.then_inc(self.sem, 1)

    def wait(self):
        self.engine.wait_ge(self.sem, self.turn + self.n)

    def link(self, ins):
        self(ins)
        self.wait()

    def loop(self, i, steps):
        self.turn = self.turn + i * steps
        self.start = self.n

    def close(self, turns, steps):
        assert self.n - self.start == steps, (self.n - self.start, steps)
        self.turn = 0
        self.n += (turns - 1) * steps


def build(nc, a, out, stop=99):
    with ExitStack() as ctx:
        def sb(name, shape, dt=F32):
            return ctx.enter_context(nc.sbuf_tensor(name, shape, dt))

        sems = {}

        def ev(name):
            if name not in sems:
                sems[name] = ctx.enter_context(nc.semaphore("s_" + name))
            return sems[name]

        ring = sb("ring", [P, RING, UNIT])
        cst = sb("cst", [P, NCST])
        hT = sb("hT", [P, KT, T])
        uT = sb("uT", [P, KT, T])
        par = sb("par", [P, 4 * P])
        mod = sb("mod", [P, 48, 2])
        cond = sb("cond", [P, KT, 32])
        ones = sb("ones", [P, P])
        ones4 = sb("ones4", [P, P])
        ones1 = sb("ones1", [P, P])
        bc = sb("bc", [P, 3, 2 * L])
        small = sb("small", [P, 256])
        wsm = sb("wsm", [P, 2, KT, 16])
        arena = sb("arena", [P, 19500])
        ps = ctx.enter_context(nc.psum_tensor("ps", [P, 8, 512], F32))

        class Arena:
            def __init__(self, at):
                self.at = at

            def take(self, *shape):
                n = int(np.prod(shape))
                v = arena[:, self.at:self.at + n]
                self.at += n
                assert self.at <= 19500, self.at
                if len(shape) == 2:
                    v = v.rearrange("p (a b) -> p a b", a=shape[0])
                if len(shape) == 3:
                    v = v.rearrange("p (a b c) -> p a b c", a=shape[0], b=shape[1])
                return v

        def cs(name, rows=P):
            at, n = CST[name]
            return cst[0:rows, at:at + n]

        ident = cs("ident")

        def pc(name, i=0, n=1):
            b, at, rows = PAR[name]
            return par[:, b * P + at + i:b * P + at + i + n]

        A = Arena(0)
        proj = A.take(NPROJ, T)
        x_at = A.at
        tok = A.take(3, D)
        prow = A.take(4, P)
        A = Arena(0)
        mrow = Arena(x_at + 3 * D + 4 * P).take(512)
        A = Arena(x_at)
        hg_B = A.take(4, T)
        hg_D = A.take(4, 256)
        hg_K0 = A.take(T)
        hg_f = A.take(T)
        hg_k = A.take(T)
        hg_lf = A.take(T)
        hg_v = A.take(3, P)
        hg_ke = A.take(2, P)
        hg_P = A.take(2, P)
        hg_P2 = A.take(16)
        hg_S = A.take(2, P)
        hg_sq = A.take(T)
        hg_o = A.take(T)
        A = Arena(x_at)
        m2_t = A.take(2, T)
        m2_x = A.take(3, D)
        m2_b = A.take(2, 2, P)
        m2_cb = A.take(2, 2, P)
        m2_cb2 = A.take(2, 16)
        m2_seg = A.take(1, 4 * P)
        dia = proj[:, TF_:TF_ + 16, :]
        m2_S = arena[:, TG * T:TG * T + 2 * D].rearrange("p (w c) -> p w c", w=2)
        m2_xe = uT[:].rearrange("p a b -> p (a b)")[:, 0:2 * D].rearrange("p (w c) -> p w c", w=2)

        chan_ones = sb("chan_ones", [16, P])[:]
        chan = sb("chan", [16, 2, T])

        def ch(row):
            return chan[:, row, :] if row < 2 else m2_x[0:16].rearrange("p a b -> p (a b)")[:, (row - 2) * T:(row - 1) * T]

        tkq = sb("tkq", [P, 3, 3, 16])
        bcast8 = sb("bcast8", [P, 40])
        m2_flat = uT[:].rearrange("p a b -> p (a b)")
        m2P0 = m2_flat[:, 0:512].rearrange("p (h t) -> p h t", h=4)
        m2P1 = m2_flat[:, 512:1024].rearrange("p (h t) -> p h t", h=4)
        m2P2 = m2_flat[0:16, 1024:1088].rearrange("p (h t) -> p h t", h=4)
        m2C = m2_flat[:, 1088:1664].rearrange("p (h t) -> p h t", h=4)

        A = Arena(0)
        act_ = A.take(FT, T)
        fc = A.take(2, 2, T)
        A = Arena(0)
        dist = A.take(12, L)
        ctok = A.take(2, D)
        hx = A.take(KT, 2 * L)
        pb = A.take(4, L)
        pcg = A.take(4, L)
        pu = A.take(4, L)
        pq = A.take(4, L)
        pk = A.take(4, 2 * L)
        pv = A.take(4, 2 * L)
        pg = A.take(4, L)
        A = Arena(12 * L + 2 * D)
        vtok = A.take(4, 4, P)
        rD = A.take(4, L)
        rP = A.take(4, L)
        A = Arena(12 * L)
        ry = A.take(4, L)
        rt = A.take(2, 2 * L)
        A = Arena(0)
        h2 = A.take(KT, L)
        h2tok = A.take(2, D)
        sel = A.take(2, NE, CAP)
        selg = A.take(2, NE, CAP)
        aff = A.take(2, NE)
        rtk = A.take(8, L)
        sg4 = A.take(2, 4, CAP)
        Gt = A.take(L)
        xs = A.take(KT, CAP)
        sa = A.take(512)
        he = A.take(512)
        heT = A.take(4, P)
        ye = A.take(D)
        A = Arena(15400)
        mx = A.take(KT, L)
        otok = A.take(2, D)

        def slot(u):
            return ring[:, u % RING, :]

        units = []

        def unit(pieces):
            units.append(pieces)
            return len(units) - 1

        def kview(w):
            return w.rearrange("(k p) c -> p k c", p=P)

        def cols(w, c0, k0=0, k1=KT, n=512):
            u = len(units)
            return unit([(slot(u)[:, 0:(k1 - k0) * n].rearrange("p (k c) -> p k c", c=n),
                          kview(w)[:, k0:k1, c0:c0 + n])])

        w_in, w_ada = a["w_in"][0], a["w_ada_2"][0]
        u_in, u_ada = [], []
        for n in range(13):
            u_in.append(cols(w_in, 512 * n))
            if n < 12:
                u_ada.append(cols(w_ada, 512 * n))
        u_out = [[cols(a["w_out"][0], 512 * cb, 8 * kh, 8 * kh + 8) for kh in range(2)] for cb in range(2)]
        u_up = []
        for i in range(11):
            v = slot(len(units)).rearrange("p (k s c) -> p k s c", k=KT, s=2)
            w = kview(a["ffn_w_up"][0])
            u_up.append(unit([(v[:, :, s, :], w[:, :, FF * s + 256 * i:FF * s + 256 * i + 256]) for s in range(2)]))
        DK = [(0, 8), (8, 16), (16, 22)]
        u_dn = [[cols(a["ffn_w_down"][0], 512 * cb, k0, k1) for k0, k1 in DK] for cb in range(2)]
        u_in2 = [cols(a["w_in_2"][0], 512 * n) for n in range(7)]
        u_out2 = [cols(a["w_out_2"][0], 512 * n) for n in range(2)]
        U0 = len(units)
        slot_count = [0] * RING
        ready_at = []
        for u, pieces in enumerate(units):
            slot_count[u % RING] += 16 * len(pieces)
            ready_at.append(slot_count[u % RING])

        def slot_ready(u):
            return ev(f"slot{u % RING}_loaded")

        n_in = [0]
        block = ctx.enter_context(nc.Block())

        @block.sync
        def _(sp):
            def load(dst, src, sem, **kw):
                sp.dma_start(dst, src, **kw).then_inc(ev(sem), 16)

            sp.wait_ge(ev("tok_cleared"), 1)
            load(cst[:], a["cst"], "cst_loaded")
            load(tok[0:16, 0, :], a["meta_tokens"], "tok_loaded")
            load(tok[16:128, 0, :], a["x"][0, 0:112], "tok_loaded")
            load(tok[:, 1, :], a["x"][0, 112:240], "tok_loaded")
            load(tok[0:16, 2, :], a["x"][0, 240:256], "tok_loaded")

            def rows(name, src, at=0):
                b, r, n = PAR[name]
                n = src.shape[0]
                load(prow[r + at:r + at + n, b, :], src, "par_loaded")
                n_in[0] += 1

            def r1(w):
                return w.rearrange("o (k p) -> (o k) p", p=P)

            rows("norm1", r1(a["norm1_w"]))
            rows("lb0", r1(a["hg_lb_logits"][0:1]))
            rows("lb1", r1(a["hg_lb_logits"][1:2]))
            rows("hgn", r1(a["hg_norm_w"]))
            rows("m2cw", r1(a["m2_conv_w"][0]))
            rows("m2cb", r1(a["m2_conv_b"]))
            rows("m2n", r1(a["m2_norm_w"]))
            rows("norm2", r1(a["norm2_w"]))
            rows("fin", a["final_norm_w"].rearrange("(k p) -> k p", p=P))
            rows("ffw01", r1(a["ffn_conv_w"][0, 0:2]))
            rows("prem", r1(a["pre_mix_g_2"]))
            rows("postm", r1(a["post_mix_g_2"]))
            rows("pref", r1(a["pre_ffn_g_2"]))
            rows("postf", r1(a["post_ffn_g_2"]))
            rows("ffw2", r1(a["ffn_conv_w"][0, 2:3]))
            rows("ffb", r1(a["ffn_conv_b"]))
            rows("cw2", r1(a["conv_w_2"][0]))
            rows("cb2", r1(a["conv_b_2"]))
            rows("retn", r1(a["ret_norm_g_2"]))
            rows("c", r1(a["c_2"]))
            rows("cctx", a["c_ctx_2"].rearrange("(k p) -> k p", p=P))
            rows("bada", r1(a["b_ada_2"]))
            load(ch(0)[:, 0:1], a["m2_dt_bias"].rearrange("o h -> h o"), "small_loaded")
            load(ch(0)[:, 1:2], a["m2_a_log"].rearrange("o h -> h o"), "small_loaded")
            for half in range(2):
                load(bcast8[64 * half:64 * half + 64, 0:8],
                     a["m2_d"].rearrange("o (k two) -> o two k", two=2)[:, half, :].to_broadcast([64, 8]), "small_loaded",
                     allow_slow_non_contiguous=True)
            load(bcast8[:, 8:24], a["b_router_2"].to_broadcast([P, 16]), "small_loaded")
            load(bcast8[:, 24:32], a["ret_decay_logit_2"].rearrange("o d h -> o (d h)").to_broadcast([P, 8]), "small_loaded")
            load(wsm[:, 0], kview(w_in)[:, :, 6656:6672], "small_loaded")
            load(wsm[:, 1], kview(a["w_router_2"][0]), "small_loaded")

            def stream(u):
                if u >= RING:
                    sp.wait_ge(ev("units_used"), u - RING + 1)
                for dst, src in units[u]:
                    sp.dma_start(dst, src).then_inc(slot_ready(u), 16)

            last = {1: 0, 2: 25, 3: 25, 4: 25, 5: 29, 6: 46}.get(stop, U0)
            for u in range(last):
                stream(u)
                if u == u_dn[1][2]:
                    sp.wait_ge(ev("ffn_down_done"), 1)
                    load(dist[:].rearrange("p a b -> p (a b)"), a["dist"], "ctx_loaded")
                    load(ctok[:], a["ctx_2"][0].rearrange("(w p) c -> p w c", p=P), "ctx_loaded")
            if stop < 9:
                sp.wait_ge(ev("small_loaded"), 128)
                for u in range(max(0, last - RING), last):
                    sp.wait_ge(slot_ready(u), ready_at[u])
                if last > u_dn[1][2]:
                    sp.wait_ge(ev("ctx_loaded"), 32)
            if stop >= 9:
                turns = [slot_count[(U0 + i) % RING] for i in range(RING)]
                with sp.Fori(0, NE) as e:
                    for i in range(12):
                        s = (U0 + i) % RING
                        sp.wait_ge(ev("units_used"), e * 12 + (U0 + i - RING + 1))
                        if i < 8:
                            w = a["w_gate_2" if i < 4 else "w_up_2"][0, e]
                            src = kview(w)[:, 2 * (i % 4):2 * (i % 4) + 2, :]
                            dst = ring[:, s, :].rearrange("p (k c) -> p k c", k=2)
                        else:
                            src = a["w_down_2"][0, e].rearrange("(j b p) c -> b p j c", b=4, p=P)[i - 8]
                            dst = ring[:, s, :].rearrange("p (j c) -> p j c", j=4)
                        sp.dma_start(dst, src).then_inc(ev(f"slot{s}_loaded"), 16)
                sp.wait_ge(ev("out_ready"), 1)
                sp.dma_start(out[0].rearrange("(w p) c -> p w c", p=P), otok[:]).then_inc(ev("stored"), 16)
                sp.wait_ge(ev("stored"), 16)

        n_par = 22

        @block.tensor
        def _(pe):
            tile = [0]

            def bank():
                return ps[:, tile[0] % TB, :]

            def open_tile():
                if tile[0] >= TB:
                    pe.wait_ge(ev("tiles_freed"), tile[0] - TB + 1)
                tile[0] += 1
                return ps[:, (tile[0] - 1) % TB, :]

            def weights(u):
                pe.wait_ge(slot_ready(u), ready_at[u])

            def group(pairs, o, **kw):
                for i, (l, r) in enumerate(pairs):
                    mm = pe.matmul(o, l, r, start=i == 0, stop=i == len(pairs) - 1, **kw)
                return mm

            def sum_tiles(src, n, o, w):
                return group([(w[:], src[:, k, :]) for k in range(n)], o)

            pe.wait_ge(ev("cst_loaded"), 16)
            pe.wait_ge(ev("par_loaded"), 16 * n_par)
            for b in range(4):
                mm = pe.transpose(ps[:, 6, b * P:b * P + P], prow[:, b, :], ident)
            mm.then_inc(ev("par_turned"), 1)
            pe.wait_ge(ev("tok_loaded"), 64)
            for k in range(KT):
                o = open_tile()
                for w, (t0, n) in enumerate(WINDOWS):
                    mm = pe.transpose(o[:, t0:t0 + n], tok[0:n, w, k * P:k * P + P], ident[0:n, 0:n])
                mm.then_inc(ev("tiles_done"), 1)
            pe.wait_ge(ev("sq"), 1)
            sum_tiles(uT, KT, ps[:, 7, 0:T], ones).then_inc(ev("mean"), 1)
            if stop <= 1:
                return
            pe.wait_ge(ev("u1"), 1)
            def turn_mod(n):
                pe.wait_ge(ev("mod_row"), n + 1)
                if n:
                    pe.wait_ge(ev("mod_done"), n)
                for b in range(4):
                    mm = pe.matmul(ps[:, 7, 2 * b:2 * b + 2], mrow[:, b * P:b * P + P], cs("sel2"), start=True, stop=True)
                mm.then_inc(ev("mod_turned"), 1)

            pe.wait_ge(ev("cond_ready"), 1)
            for n in range(13):
                u = u_in[n]
                weights(u)
                w = slot(u).rearrange("p (k c) -> p k c", k=KT)
                for m in range(4):
                    o = open_tile()
                    group([(w[:, k, m * P:m * P + P], uT[:, k, :]) for k in range(KT)], o[:, 0:T]).then_inc(ev("tiles_done"), 1)
                pe.wait_ge(ev("tiles_done"), tile[0])
                pe.nop().then_inc(ev("units_used"), 1)
                if n >= 1:
                    turn_mod(n - 1)
                if n < 12:
                    u = u_ada[n]
                    weights(u)
                    if n:
                        pe.wait_ge(ev("mod_row"), n)
                    w = slot(u).rearrange("p (k c) -> p k c", k=KT)
                    for k in range(KT):
                        j = k % 4
                        mm = pe.matmul(ps[32 * j:32 * j + 32, 6, :], cond[:, k, :], w[:, k, :], start=k < 4, stop=k >= 4)
                    mm.then_inc(ev("units_used"), 1)
            o = open_tile()
            pe.wait_ge(ev("small_loaded"), 16 * 8)
            group([(wsm[:, 0, k, :], uT[:, k, :]) for k in range(KT)], o[0:16, 0:T]).then_inc(ev("tiles_done"), 1)
            if stop <= 2:
                return
            pe.wait_ge(ev("tiles_freed"), tile[0])
            pe.wait_ge(ev("mod_done"), 12)
            with pe.Fori(0, HEADS) as h:
                pe.wait_ge(ev("hg_staged"), h + 1)
                for w, (t0, n) in enumerate(WINDOWS):
                    mm = pe.transpose(ps[0:n, 6, w * P:w * P + P], hg_o[:, t0:t0 + n], ident)
                for w in range(2):
                    mm = pe.transpose(ps[:, 7, w * P:w * P + P], hg_D[:, 3, w * P:w * P + P], ident)
                mm.then_inc(ev("hg_turned"), 1)
                keys = [hg_K0, hg_D[:, 0, :], hg_D[:, 1, :], hg_D[:, 2, :]]
                for l in range(4):
                    q = hg_B[:, max(l - 1, 0), :]
                    for w in range(2):
                        s = slice(w * P, w * P + P)
                        mm = pe.matmul(ps[:, l // 2, (l % 2) * 256 + w * P:(l % 2) * 256 + w * P + P],
                                       keys[l][:, s], q[:, s], start=True, stop=True)
                mm = pe.matmul(ps[0:16, 2, 0:16], hg_K0[:, 256:T], hg_B[:, 0, 256:T], start=True, stop=True)
                mm.then_inc(ev("hg_scores"), 1)
                pe.wait_ge(ev("hg_vk"), h + 1)
                for w in range(2):
                    mm = pe.matmul(ps[:, 3, w * P:w * P + P], hg_ke[:, w, :], hg_v[:, w, :], start=True, stop=True)
                mm.then_inc(ev("hg_update"), 1)
                pe.wait_ge(ev("hg_masked"), h + 1)
                pe.matmul(ps[:, 4, 0:128], hg_v[:, 0, :], hg_P[:, 0, :], start=True, stop=True)
                group([(hg_v[:, 1, :], hg_P[:, 1, :]), (hg_S[:, 0, :], hg_B[:, 3, 128:256])], ps[:, 4, 128:256])
                pe.matmul(ps[:, 4, 256:T], hg_v[0:16, 2, :], hg_P2[0:16, :], start=True, stop=False)
                pe.matmul(ps[:, 4, 256:T], hg_S[:, 1, :], hg_B[:, 3, 256:T], start=False, stop=True).then_inc(ev("hg_out"), 1)
                pe.wait_ge(ev("hg_squared"), h + 1)
                pe.matmul(ps[:, 5, 0:T], ones1[:], hg_sq[:], start=True, stop=True).then_inc(ev("hg_mean"), 1)
            if stop <= 3:
                return
            pe.wait_ge(ev("m2_rows"), 1)
            for i, row in enumerate((1, 2, 3)):
                for w, (t0, n) in enumerate(WINDOWS):
                    mm = pe.transpose(ps[0:n, 0, (w * 3 + i) * 16:(w * 3 + i) * 16 + 16], ch(row)[:, t0:t0 + n], ident[0:16, 0:16])
            mm.then_inc(ev("m2_rows_turned"), 1)
            pe.wait_ge(ev("m2_conv"), 12)
            for w, (t0, n) in enumerate(WINDOWS):
                for half in range(2):
                    b = 1 + (2 * w + half) % 4
                    if 2 * w + half >= 4:
                        pe.wait_ge(ev("m2_x_copied"), 2 * w + half - 3)
                    for c in range(4):
                        mm = pe.transpose(ps[0:n, b, c * P:c * P + P], proj[:, TX + 4 * half + c, t0:t0 + n], ident)
                    mm.then_inc(ev("m2_x_turned"), 1)
            for w in range(2):
                for g in range(2):
                    mm = pe.transpose(ps[:, 5, (2 * w + g) * P:(2 * w + g) * P + P], proj[:, TBM + g, w * P:w * P + P], ident)
            mm.then_inc(ev("m2_b_turned"), 1)
            for g in range(2):
                for w in range(2):
                    s = slice(w * P, w * P + P)
                    pe.matmul(ps[:, 6, (2 * g + w) * P:(2 * g + w) * P + P], proj[:, TBM + g, s], proj[:, TCM + g, s], start=True, stop=True)
                mm = pe.matmul(ps[0:16, 7, g * 16:g * 16 + 16], proj[:, TBM + g, 256:T], proj[:, TCM + g, 256:T], start=True, stop=True)
            mm.then_inc(ev("m2_cb"), 1)
            pe.wait_ge(ev("m2_xe"), 1)
            for w in range(2):
                for g in range(2):
                    mm = pe.matmul(ps[:, 1 + 2 * w + g, :], m2_b[:, w, g, :], m2_xe[:, w, g * 512:g * 512 + 512], start=True, stop=True)
            mm.then_inc(ev("m2_update"), 1)
            pe.wait_ge(ev("m2_dia"), 1)
            pe.wait_ge(ev("m2_cbm"), 1)
            for q in range(4):
                if q:
                    pe.wait_ge(ev("m2_seg"), 3 * q)
                    pe.wait_ge(ev("m2_ea"), 2 * q)
                for w, (t0, n) in enumerate(WINDOWS):
                    mm = pe.matmul(ps[:, 5 + w, 0:4 * n], chan_ones, dia[0:16, 4 * q:4 * q + 4, t0:t0 + n], start=True, stop=True)
                mm.then_inc(ev("m2_a"), 1)
                pe.wait_ge(ev("m2_pc"), q + 1)
                if q:
                    pe.wait_ge(ev("m2_gated"), 2 * q)
                for pair in range(2):
                    for hh in range(2):
                        j = 2 * pair + hh
                        hc = (4 * q + j) * M2P
                        o = ps[64 * hh:64 * hh + 64, 0 if pair == 0 else 1, :]
                        if q == 0 and pair == 1 and hh == 0:
                            pe.wait_ge(ev("m2_S_copied"), 1)
                        pe.matmul(o[:, 0:128], m2_x[:, 0, hc:hc + M2P], m2P0[:, j, :], start=True, stop=True)
                        pe.matmul(o[:, 128:256], m2_x[:, 1, hc:hc + M2P], m2P1[:, j, :], start=True, stop=False)
                        pe.matmul(o[:, 128:256], m2_S[:, 0, hc:hc + M2P], m2C[:, j, 0:128], start=False, stop=True)
                        pe.matmul(o[:, 256:T], m2_x[0:16, 2, hc:hc + M2P], m2P2[0:16, j, :], start=True, stop=False)
                        mm = pe.matmul(o[:, 256:T], m2_S[:, 1, hc:hc + M2P], m2C[:, j, 128:144], start=False, stop=True)
                    mm.then_inc(ev("m2_y"), 1)
            for g in range(2):
                pe.wait_ge(ev("m2_sq"), g + 1)
                sum_tiles(uT, 4, ps[:, 2 + g, 0:T], ones4).then_inc(ev("m2_mean"), 1)
            if stop <= 4:
                return
            pe.wait_ge(ev("mix_ready"), 1)

            def block_products(us, ks, rhs, n):
                outs = [open_tile() for _ in range(4)]
                k0 = 0
                for i, (u, nk) in enumerate(zip(us, ks)):
                    weights(u)
                    w = slot(u)[:, 0:nk * 512].rearrange("p (k c) -> p k c", k=nk)
                    lastu = i == len(us) - 1
                    for m in range(4):
                        for k in range(nk):
                            mm = pe.matmul(outs[m][:, 0:n], w[:, k, m * P:m * P + P], rhs(k0 + k),
                                           start=(i == 0 and k == 0), stop=(lastu and k == nk - 1))
                        if lastu:
                            mm.then_inc(ev("tiles_done"), 1)
                    if lastu:
                        pe.wait_ge(ev("tiles_done"), tile[0])
                        pe.nop().then_inc(ev("units_used"), 1)
                    else:
                        mm.then_inc(ev("units_used"), 1)
                    k0 += nk

            for cb in range(2):
                block_products(u_out[cb], (8, 8), lambda k: proj[:, k if k < 8 else TZ + k - 8, :], T)
            pe.wait_ge(ev("sq"), 2)
            sum_tiles(uT, KT, ps[:, 7, 0:T], ones).then_inc(ev("mean"), 1)
            if stop <= 5:
                return
            pe.wait_ge(ev("u2"), 1)
            for i in range(11):
                u = u_up[i]
                weights(u)
                w = slot(u).rearrange("p (k s c) -> p k s c", k=KT, s=2)
                for m in range(2):
                    for s in range(2):
                        o = open_tile()
                        group([(w[:, k, s, m * P:m * P + P], uT[:, k, :]) for k in range(KT)], o[:, 0:T]).then_inc(ev("tiles_done"), 1)
                pe.wait_ge(ev("tiles_done"), tile[0])
                pe.nop().then_inc(ev("units_used"), 1)
            pe.wait_ge(ev("ffn_act"), FT)
            for cb in range(2):
                block_products(u_dn[cb], (8, 8, 6), lambda k: act_[:, k, :], T)
            pe.wait_ge(ev("sq"), 3)
            pe.nop().then_inc(ev("ffn_down_done"), 1)
            sum_tiles(uT, KT, ps[:, 7, 0:T], ones).then_inc(ev("mean"), 1)
            if stop <= 6:
                return
            pe.wait_ge(ev("ctx_loaded"), 32)
            for k in range(KT):
                o = open_tile()
                for w in range(2):
                    mm = pe.transpose(o[:, w * P:w * P + P], ctok[:, w, k * P:k * P + P], ident)
                mm.then_inc(ev("tiles_done"), 1)
            pe.wait_ge(ev("sq"), 4)
            sum_tiles(hx, KT, ps[:, 7, :], ones).then_inc(ev("mean"), 1)
            pe.wait_ge(ev("hx_ready"), 1)
            for n in range(7):
                u = u_in2[n]
                weights(u)
                w = slot(u).rearrange("p (k c) -> p k c", k=KT)
                width = 2 * L if n in (4, 5) else L
                for m in range(4):
                    o = open_tile()
                    group([(w[:, k, m * P:m * P + P], hx[:, k, 0:width]) for k in range(KT)], o[:, 0:width]).then_inc(ev("tiles_done"), 1)
                pe.wait_ge(ev("tiles_done"), tile[0])
                pe.nop().then_inc(ev("units_used"), 1)
            for j in range(2 * RH):
                src = pq[:, j, :] if j < RH else pk[:, j - RH, :]
                width = L if j < RH else 2 * L
                if j == 0:
                    pe.wait_ge(ev("p2_done"), 28)
                o = open_tile()
                pe.matmul(o[:, 0:width], cs("rot"), src, start=True, stop=True).then_inc(ev("tiles_done"), 1)
            for h in range(RH):
                o = open_tile()
                for t in range(4):
                    mm = pe.transpose(o[:, t * P:t * P + P], pv[:, h, t * P:t * P + P], ident)
                mm.then_inc(ev("tiles_done"), 1)
            pe.wait_ge(ev("tiles_freed"), tile[0])
            for h in range(RH):
                if h:
                    pe.wait_ge(ev("ret_p"), h)
                for t in range(4):
                    mm = pe.matmul(ps[:, t // 2, (t % 2) * L:(t % 2) * L + L], pk[:, h, t * P:t * P + P], pq[:, h, :], start=True, stop=True)
                mm.then_inc(ev("ret_s"), 1)
                pe.wait_ge(ev("ret_p"), h + 1)
                if h:
                    pe.wait_ge(ev("ret_y"), h)
                group([(vtok[:, h, t, :], rP[:, t, :]) for t in range(4)], ps[:, 2, 0:L]).then_inc(ev("ret_o"), 1)
            pe.wait_ge(ev("ret_y"), RH)
            for h in range(RH):
                mm = pe.matmul(ps[:, 3 + h // 2, (h % 2) * L:(h % 2) * L + L], ones1[:], ry[:, h, :], start=True, stop=True)
            mm.then_inc(ev("ret_mu"), 1)
            pe.wait_ge(ev("ret_sq"), 1)
            for h in range(RH):
                mm = pe.matmul(ps[:, h // 2, (h % 2) * L:(h % 2) * L + L], ones1[:], rD[:, h, :], start=True, stop=True)
            mm.then_inc(ev("ret_var"), 1)
            if stop <= 7:
                return
            pe.wait_ge(ev("mix2_ready"), 1)
            for cb in range(2):
                block_products([u_out2[cb]], (8,), lambda k: pk[:].rearrange("p a b -> p (a b)")[:, k * L:k * L + L], L)
            pe.wait_ge(ev("sq"), 5)
            uflat = uT[:].rearrange("p a b -> p (a b)")[:, 0:KT * L].rearrange("p (k c) -> p k c", k=KT)
            sum_tiles(uflat, KT, ps[:, 7, 0:L], ones).then_inc(ev("mean"), 1)
            pe.wait_ge(ev("sq"), 6)
            sum_tiles(uflat, KT, ps[:, 7, 0:L], ones).then_inc(ev("mean"), 1)
            pe.wait_ge(ev("h2_ready"), 1)
            for w in range(2):
                mm = group([(h2[:, k, w * P:w * P + P], wsm[:, 1, k, :]) for k in range(KT)], ps[:, 6, w * 16:w * 16 + 16])
            mm.then_inc(ev("logits"), 1)
            pe.wait_ge(ev("tiles_freed"), tile[0])
            for w in range(2):
                for k in range(KT):
                    mm = pe.transpose(ps[:, 2 * w + k // 4, (k % 4) * P:(k % 4) * P + P], h2[:, k, w * P:w * P + P], ident)
            mm.then_inc(ev("h2_turned"), 1)
            pe.wait_ge(ev("aff_ready"), 1)
            for w in range(2):
                mm = pe.transpose(ps[0:16, 7, w * P:w * P + P], aff[:, w, :], ident)
            mm.then_inc(ev("aff_turned"), 1)
            pe.wait_ge(ev("rank_ready"), 1)
            for w in range(2):
                mm = pe.transpose(ps[:, 5, w * 16:w * 16 + 16], rtk[0:16, 3, w * P:w * P + P], ident[0:16, 0:16])
            mm.then_inc(ev("rank_turned"), 1)
            if stop <= 8:
                return
            pe.wait_ge(ev("sel_ready"), 1)
            pe.wait_ge(ev("zero_ready"), 1)
            for b in range(4):
                pe.matmul(ps[:, 4 + b, :], ident, uT[:].rearrange("p a b -> p (a b)")[:, 0:512], start=True, stop=False, skip_group_check=True)
            with pe.Fori(0, NE) as e:
                pe.wait_ge(ev("sg4_ready"), e + 1)
                for k in range(KT):
                    group([(h2tok[:, w, k * P:k * P + P], sel[:, w, e, :]) for w in range(2)], ps[:, 3, k * CAP:k * CAP + CAP])
                for w in range(2):
                    mm = pe.transpose(ps[:, 3, 256 + w * P:256 + w * P + P], sg4[:, w].rearrange("p j s -> p (j s)"), ident)
                mm.then_inc(ev("gathered"), 1)
                pe.wait_ge(ev("xs_ready"), e + 1)
                for half in range(2):
                    for i in range(4):
                        u = U0 + 4 * half + i
                        s = u % RING
                        base = slot_count[s]
                        pe.wait_ge(ev(f"slot{s}_loaded"), e * 32 + (base + 16 * (1 + (4 * half + i) // RING)))
                        w = ring[:, s, :].rearrange("p (k c) -> p k c", k=2)
                        for k in range(2):
                            for j in range(4):
                                kt = 2 * i + k
                                mm = pe.matmul(ps[32 * j:32 * j + 32, half, :], xs[:, kt, :], w[:, k, 512 * j:512 * j + 512],
                                               start=kt == 0, stop=kt == KT - 1)
                        mm.then_inc(ev("units_used"), 1)
                pe.wait_ge(ev("units_used"), e * 12 + (U0 + 8))
                pe.nop().then_inc(ev("up_done"), 1)
                pe.wait_ge(ev("hidden"), e + 1)
                for b in range(4):
                    mm = pe.transpose(ps[:, 2, b * P:b * P + P], he[:, b * P:b * P + P], ident)
                mm.then_inc(ev("hidden_turned"), 1)
                pe.wait_ge(ev("heT_ready"), e + 1)
                for i in range(4):
                    u = U0 + 8 + i
                    s = u % RING
                    pe.wait_ge(ev(f"slot{s}_loaded"), e * 32 + (slot_count[s] + 16 * (1 + (8 + i) // RING)))
                    w = ring[:, s, :].rearrange("p (j c) -> p j c", j=4)
                    for half in range(2):
                        for j in range(4):
                            mm = pe.matmul(ps[32 * j:32 * j + 32, half, :], heT[:, i, 32 * j:32 * j + 32], w[:, j, 512 * half:512 * half + 512],
                                           start=i == 0, stop=i == 3)
                    mm.then_inc(ev("units_used"), 1)
                pe.wait_ge(ev("y_ready"), e + 1)
                for k in range(KT):
                    mm = pe.matmul(ps[:, 4 + k // 2, (k % 2) * L:(k % 2) * L + L], ye[:, k * P:k * P + P], Gt, start=False, stop=False, skip_group_check=True)
                mm.then_inc(ev("scattered"), 1)
            for b in range(4):
                mm = pe.matmul(ps[:, 4 + b, :], ident, uT[:].rearrange("p a b -> p (a b)")[:, 0:512], start=False, stop=True, skip_group_check=True)
            mm.then_inc(ev("experts_done"), 1)
            pe.wait_ge(ev("sq"), 7)
            sum_tiles(uflat, KT, ps[:, 0, 0:L], ones).then_inc(ev("mean"), 1)
            pe.wait_ge(ev("y_final"), 1)
            for w in range(2):
                for k in range(KT):
                    mm = pe.transpose(ps[:, 4 + 2 * w + k // 4, (k % 4) * P:(k % 4) * P + P], hT[:, k, w * P:w * P + P], ident)
            mm.then_inc(ev("y_turned"), 1)

        @block.scalar
        def _(act):
            st = Steps(act, ev("act_steps"))
            tile = [0]

            def root(i, n):
                act.wait_ge(ev("var"), i)
                act.activation(bc[:, 1, 0:n], bc[:, 0, 0:n], ACT.Sqrt).then_inc(ev("root"), 1)

            act.wait_ge(ev("par_ready"), 1)
            act.wait_ge(ev("cond_cleared"), 1)
            st(act.activation(cond[:, :, 0], pc("c", 0, 8), ACT.Silu))
            act.activation(cond[:, :, 1], pc("cctx", 0, 8), ACT.Silu).then_inc(ev("cond_act"), 1)
            st.wait()
            act.wait_ge(ev("cond_act"), 1)
            act.nop().then_inc(ev("cond_ready"), 1)
            act.wait_ge(ev("lb_shift"), 1)
            act.activation(small[:, 0:16], small[:, 0:16], ACT.Exp).then_inc(ev("lb_exp"), 1)
            root(1, T)
            if stop <= 1:
                return
            tile[0] = 8

            def leave(dst, n, fn):
                t = tile[0]
                act.wait_ge(ev("tiles_done"), t + 1)
                act.activation(dst, ps[:, t % TB, 0:n], fn).then_inc(ev("tiles_freed"), 1)
                tile[0] += 1

            act.wait_ge(ev("tok_free"), 1)
            for m in range(NPROJ):
                fn = {0: ACT.Silu, 1: ACT.Sigmoid, 2: ACT.Copy, 3: ACT.Silu, 4: ACT.Silu}.get(m // 8, ACT.Copy)
                leave(proj[:, m, :], T, fn)
            act.wait_ge(ev("tiles_freed"), tile[0])
            act.nop().then_inc(ev("proj_ready"), 1)
            if stop <= 2:
                return
            SA = 4
            with act.Fori(0, HEADS) as h:
                st.loop(h, SA)
                act.wait_ge(ev("hg_f"), h + 1)
                act.activation(hg_lf, hg_f, ACT.Ln).then_inc(ev("hg_log"), 1)
                act.wait_ge(ev("hg_b"), h + 1)
                st(act.activation(hg_K0, hg_B[:, 0, :], ACT.Exp, scale=-1.0))
                st(act.activation(hg_D, hg_D, ACT.Exp))
                st.wait()
                act.activation(hg_B, hg_B, ACT.Exp).then_inc(ev("hg_exp"), 1)
                st(act.nop())
                act.wait_ge(ev("hg_turned"), h + 1)
                act.activation(hg_ke[:], ps[:, 7, 0:256].rearrange("p (w c) -> p w c", w=2), ACT.Copy).then_inc(ev("hg_ke_copied"), 1)
                act.wait_ge(ev("hg_out"), h + 1)
                act.activation(hg_sq, ps[:, 4, 0:T], ACT.Square).then_inc(ev("hg_squared"), 1)
                act.wait_ge(ev("hg_eps"), h + 1)
                st(act.activation(bc[:, 1, 0:T], bc[:, 0, 0:T], ACT.Sqrt))
                st.wait()
                act.nop().then_inc(ev("hg_root"), 1)
            st.close(HEADS, SA)
            if stop <= 3:
                return
            for t in range(12):
                act.wait_ge(ev("m2_conv_sum"), t + 1)
                act.activation(proj[:, TX + t, :], m2_t[:, t % 2, :], ACT.Silu).then_inc(ev("m2_conv"), 1)
            act.wait_ge(ev("dt_abs"), 1)
            act.activation(ch(6)[:, :], ch(5)[:, :], ACT.Exp, scale=-1.0).then_inc(ev("dt_exp"), 1)
            act.wait_ge(ev("dt_one"), 1)
            act.activation(ch(8)[:, :], ch(7)[:, :], ACT.Ln).then_inc(ev("dt_log"), 1)
            act.wait_ge(ev("small_loaded"), 16 * 8)
            act.activation(ch(0)[:, 2:3], ch(0)[:, 1:2], ACT.Exp).then_inc(ev("a_exp"), 1)
            act.wait_ge(ev("m2_end"), 1)
            act.activation(ch(3)[:, 0:256], ch(4)[:, 0:256], ACT.Exp).then_inc(ev("m2_end_exp"), 1)
            for q in range(4):
                act.wait_ge(ev("m2_a"), q + 1)
                if q:
                    act.wait_ge(ev("m2_y"), 2 * q)
                act.activation(m2C[:, :, 0:128], ps[:, 6, :].rearrange("p (h t) -> p h t", h=4), ACT.Exp).then_inc(ev("m2_ea"), 1)
                act.activation(m2C[:, :, 128:144], ps[:, 7, 0:64].rearrange("p (h t) -> p h t", h=4), ACT.Exp).then_inc(ev("m2_ea"), 1)
                for w, (buf, n) in enumerate(((m2P0[:], P), (m2P1[:], P), (m2P2[:], 16))):
                    act.wait_ge(ev("m2_seg"), 3 * q + w + 1)
                    act.activation(buf, buf, ACT.Exp).then_inc(ev("m2_seg_exp"), 1)
            for g in range(2):
                act.wait_ge(ev("m2_eps"), g + 1)
                act.activation(bc[:, 1, 0:T], bc[:, 0, 0:T], ACT.Sqrt).then_inc(ev("m2_root"), 1)
            if stop <= 4:
                return
            root(2, T)
            if stop <= 5:
                return
            tile[0] = 8 + NPROJ + 1 + 8
            for i in range(FT):
                for s in range(2):
                    m = s * FT + i
                    t = tile[0]
                    act.wait_ge(ev("tiles_done"), t + 1)
                    if i >= 2:
                        act.wait_ge(ev("ffn_act"), i - 1)
                    act.activation(fc[:, i % 2, s, :], ps[:, t % TB, 0:T], ACT.Identity, scale=pc("ffw2", m),
                                   bias=pc("ffb", m)).then_inc(ev("ffn_tap"), 1)
                    tile[0] += 1
                act.wait_ge(ev("ffn_conv"), 2 * i + 1)
                act.activation(fc[:, i % 2, 0, :], fc[:, i % 2, 0, :], ACT.Silu).then_inc(ev("ffn_silu"), 1)
            root(3, T)
            if stop <= 6:
                return
            root(4, 2 * L)
            tile[0] = 8 + NPROJ + 1 + 8 + 44 + 8 + 8
            act.wait_ge(ev("hx_ready"), 1)
            for n in range(7):
                for m in range(4):
                    width = 2 * L if n in (4, 5) else L
                    dst = (pb, pcg, pu, pq, pk, pv, pg)[n][:, m, :]
                    leave(dst, width, ACT.Silu if n == 6 else ACT.Copy)
            act.wait_ge(ev("tiles_freed"), tile[0])
            act.nop().then_inc(ev("p2_done"), 28)
            act.wait_ge(ev("lg_abs"), 1)
            act.activation(small[:, 40:48], small[:, 32:40], ACT.Exp, scale=-1.0).then_inc(ev("lg_exp"), 1)
            act.wait_ge(ev("lg_one"), 1)
            act.activation(small[:, 56:64], small[:, 48:56], ACT.Ln).then_inc(ev("lg_log"), 1)
            for h in range(RH):
                act.wait_ge(ev("ret_arg"), h + 1)
                st(act.activation(rD[:, 0:2, :], rD[:, 0:2, :], ACT.Exp))
                act.wait_ge(ev("lg_ready"), 1)
                st(act.activation(rD[:, 2:4, :], dist[:, 4:6, :], ACT.Exp, scale=small[:, 80 + h:81 + h]))
                act.activation(rt[:, :, :].rearrange("p a b -> p (a b)")[:, 0:512], dist[:, 6:8, :].rearrange("p a b -> p (a b)"), ACT.Exp,
                               scale=small[:, 84 + h:85 + h]).then_inc(ev("ret_pow"), 1)
                st.wait()
                act.wait_ge(ev("ret_pow"), h + 1)
                act.nop().then_inc(ev("ret_d"), 1)
            act.wait_ge(ev("ret_eps"), 1)
            act.activation(rD[:], rD[:], ACT.Sqrt).then_inc(ev("ret_root"), 1)
            if stop <= 7:
                return
            root(5, L)
            root(6, L)
            act.wait_ge(ev("soft_shift"), 1)
            act.activation(aff[:], aff[:], ACT.Exp).then_inc(ev("soft_exp"), 1)
            if stop <= 8:
                return
            SE = 1
            with act.Fori(0, NE) as e:
                act.wait_ge(ev("up_done"), e + 1)
                act.activation(sa, ps[:, 0, :], ACT.Silu).then_inc(ev("gate_silu"), 1)
                act.wait_ge(ev("hidden_turned"), e + 1)
                act.activation(heT[:], ps[:, 2, :].rearrange("p (b c) -> p b c", b=4), ACT.Copy).then_inc(ev("heT_ready"), 1)
                act.wait_ge(ev("units_used"), e * 12 + (U0 + 12))
                act.activation(ye[:, 0:512], ps[:, 0, :], ACT.Copy).then_inc(ev("y_half"), 1)
            root(7, L)

        @block.vector
        def _(dve):
            st = Steps(dve, ev("dve_steps"))
            tile = [0]
            tt, ts, stt = dve.tensor_tensor, dve.tensor_scalar, dve.scalar_tensor_tensor

            def inverse_root(i, n, src):
                dve.wait_ge(ev("mean"), i)
                ts(bc[:, 0, 0:n], src, 1e-6, None, ALU.add).then_inc(ev("var"), 1)
                dve.wait_ge(ev("root"), i)
                st.link(dve.reciprocal(bc[:, 2, 0:n], bc[:, 1, 0:n]))

            st(dve.memset(ones[:], 1.0 / D))
            st(dve.memset(ones4[:], 1.0 / 512))
            st(dve.memset(ones1[:], 1.0 / P))
            dve.memset(cond[:], 0.0).then_inc(ev("cond_cleared"), 1)
            dve.memset(prow, 0.0).then_inc(ev("tok_cleared"), 1)
            dve.wait_ge(ev("par_turned"), 1)
            dve.tensor_copy(par[:], ps[:, 6, :]).then_inc(ev("par_ready"), 1)
            dve.wait_ge(ev("par_ready"), 1)
            st.link(tt(small[:, 16:24], pc("lb0", 0, 8), pc("lb1", 0, 8), ALU.max))
            st(tt(small[:, 0:8], pc("lb0", 0, 8), small[:, 16:24], ALU.subtract))
            tt(small[:, 8:16], pc("lb1", 0, 8), small[:, 16:24], ALU.subtract).then_inc(ev("lb_shift"), 1)
            for k in range(KT):
                dve.wait_ge(ev("tiles_done"), k + 1)
                dve.tensor_copy(hT[:, k, :], ps[:, k % TB, 0:T]).then_inc(ev("tiles_freed"), 1)
            dve.wait_ge(ev("tiles_freed"), 8)
            dve.nop().then_inc(ev("tok_free"), 1)
            st.link(tt(uT[:], hT[:], hT[:], ALU.mult))
            dve.nop().then_inc(ev("sq"), 1)
            dve.wait_ge(ev("lb_exp"), 1)
            st.link(tt(small[:, 16:24], small[:, 0:8], small[:, 8:16], ALU.add))
            st.link(dve.reciprocal(small[:, 24:32], small[:, 16:24]))
            lb, oml = small[:, 96:104], small[:, 104:112]
            st.link(tt(lb, small[:, 0:8], small[:, 24:32], ALU.mult))
            st.link(ts(oml, lb, -1.0, 1.0, ALU.mult, ALU.add))

            def normed(i, name, event):
                inverse_root(i, T, ps[:, 7, 0:T])
                for k in range(KT):
                    st(stt(uT[:, k, :], hT[:, k, :], pc(name, k), bc[:, 2, 0:T], ALU.mult, ALU.mult))
                st.wait()
                dve.nop().then_inc(ev(event), 1)

            normed(1, "norm1", "u1")
            if stop <= 1:
                return
            for n in range(12):
                dve.wait_ge(ev("units_used"), 2 * n + 2)
                if n:
                    dve.wait_ge(ev("mod_turned"), n)
                dve.tensor_copy(mrow, ps[:, 6, :]).then_inc(ev("mod_row"), 1)
                dve.wait_ge(ev("mod_turned"), n + 1)
                tt(mod[:, 4 * n:4 * n + 4, :], ps[:, 7, 0:8].rearrange("p (b c) -> p b c", c=2),
                   pc("bada", 4 * n, 4).unsqueeze(2).to_broadcast([P, 4, 2]), ALU.add).then_inc(ev("mod_done"), 1)
            t = 8 + NPROJ
            dve.wait_ge(ev("tiles_done"), t + 1)
            dve.wait_ge(ev("small_loaded"), 16 * 8)
            dve.wait_ge(ev("proj_ready"), 1)
            ts(ch(1)[:, :], ps[0:16, t % TB, 0:T], ch(0)[:, 0:1], None, ALU.add).then_inc(ev("tiles_freed"), 1)
            if stop <= 2:
                return
            st(dve.memset(hg_P, 0.0))
            st.link(dve.memset(hg_P2, 0.0))
            dve.wait_ge(ev("mod_done"), 12)
            reset = cs("reset").rearrange("p (l t) -> p l t", l=4)
            mask = cs("mask").bitcast(U32).rearrange("p (l r) -> p l r", l=4)
            SD = 29
            with dve.Fori(0, HEADS) as h:
                st.loop(h, SD)
                st.link(ts(hg_f, proj[:, h + TF_, :], small[:, bass.ds(h + 104, 1)], small[:, bass.ds(h + 96, 1)], ALU.mult, ALU.add))
                dve.nop().then_inc(ev("hg_f"), 1)
                st(ts(hg_k, hg_f, -1.0, 1.0, ALU.mult, ALU.add))
                dve.wait_ge(ev("hg_log"), h + 1)
                for l in range(4):
                    st(dve.tensor_tensor_scan(hg_B[:, l, :], reset[:, l, :], hg_lf, 0.0, ALU.mult, ALU.add))
                st.wait()
                for l, w in enumerate(LEVELS):
                    b = hg_B[:, l, 0:256].rearrange("p (c w) -> p c w", w=w)
                    st(tt(hg_D[:, l, :].rearrange("p (c w) -> p c w", w=w),
                          b[:, :, w - 1:w].to_broadcast([P, 256 // w, w]), b, ALU.subtract))
                st.wait()
                dve.nop().then_inc(ev("hg_b"), 1)
                dve.wait_ge(ev("hg_exp"), h + 1)
                st(dve.tensor_copy(small[:, 120:121], hg_B[:, 3, 255:256]))
                st(tt(hg_K0, hg_K0, hg_k, ALU.mult))
                st(tt(hg_D, hg_D, hg_k[:, 0:256].unsqueeze(1).to_broadcast([P, 4, 256]), ALU.mult))
                st.wait()
                st(tt(hg_B, hg_B, proj[:, h + TQ, :].unsqueeze(1).to_broadcast([P, 4, T]), ALU.mult))
                st(dve.tensor_copy(hg_o, proj[:, h + TI, :]))
                st.wait()
                dve.nop().then_inc(ev("hg_staged"), 1)
                dve.wait_ge(ev("hg_turned"), h + 1)
                st(dve.tensor_copy(hg_v[:, 0:2, :], ps[:, 6, 0:256].rearrange("p (w c) -> p w c", w=2)))
                st(dve.tensor_copy(hg_v[0:16, 2, :], ps[0:16, 6, 256:384]))
                st.wait()
                dve.wait_ge(ev("hg_ke_copied"), h + 1)
                dve.nop().then_inc(ev("hg_vk"), 1)
                dve.wait_ge(ev("hg_scores"), h + 1)
                for l in range(4):
                    st(dve.memset(small[:, 122:123], 0.0))
                    st.link(dve.copy_predicated(hg_P, mask[:, l, :].unsqueeze(1).to_broadcast([P, 2, P]),
                                           ps[:, l // 2, (l % 2) * 256:(l % 2) * 256 + 256].rearrange("p (w r) -> p w r", w=2)))
                st(dve.memset(small[:, 122:123], 0.0))
                st(dve.copy_predicated(hg_P2[0:16, :], mask[0:16, 0, 0:16], ps[0:16, 2, 0:16]))
                dve.wait_ge(ev("hg_update"), h + 1)
                st.link(dve.tensor_copy(hg_S[:, 0, :], ps[:, 3, 0:128]))
                st.link(stt(hg_S[:, 1, :], hg_S[:, 0, :], small[:, 120:121], ps[:, 3, 128:256], ALU.mult, ALU.add))
                dve.nop().then_inc(ev("hg_masked"), 1)
                dve.wait_ge(ev("hg_mean"), h + 1)
                ts(bc[:, 0, 0:T], ps[:, 5, 0:T], 1e-6, None, ALU.add).then_inc(ev("hg_eps"), 1)
                dve.wait_ge(ev("hg_root"), h + 1)
                dve.reciprocal(bc[:, 2, 0:T], bc[:, 1, 0:T]).then_inc(ev("hg_inv"), 1)
                dve.wait_ge(ev("hg_inv"), h + 1)
                b_, r_, _n = PAR["hgn"]
                stt(hg_o, ps[:, 4, 0:T], par[:, bass.ds(h + (b_ * P + r_), 1)], bc[:, 2, 0:T], ALU.mult, ALU.mult).then_inc(ev("hg_scaled"), 1)
                dve.wait_ge(ev("hg_scaled"), h + 1)
                tt(proj[:, h + TQ, :], hg_o, proj[:, h + TG, :], ALU.mult).then_inc(ev("hg_head"), 1)
                dve.wait_ge(ev("hg_head"), h + 1)
            st.close(HEADS, SD)
            if stop <= 3:
                return
            for t in range(12):
                x, o = proj[:, TX + t, :], m2_t[:, t % 2, :]
                if t >= 2:
                    dve.wait_ge(ev("m2_conv"), t - 1)
                st.link(ts(o, x, pc("m2cw", 36 + t), pc("m2cb", t), ALU.mult, ALU.add))
                for s in (1, 2, 3):
                    ins = stt(o[:, s:T], x[:, 0:T - s], pc("m2cw", 12 * (3 - s) + t), o[:, s:T], ALU.mult, ALU.add)
                    if s < 3:
                        st.link(ins)
                ins.then_inc(ev("m2_conv_sum"), 1)

            def log1p_of_exp(u, e, one, lg, tmp, ev_abs, ev_exp, ev_one, ev_log):
                st.link(stt(tmp, u, -1.0, u, ALU.mult, ALU.max))
                dve.nop().then_inc(ev(ev_abs), 1)
                dve.wait_ge(ev(ev_exp), 1)
                st.link(ts(one, e, 1.0, None, ALU.add))
                dve.nop().then_inc(ev(ev_one), 1)
                dve.wait_ge(ev(ev_log), 1)
                st.link(tt(lg, lg, e, ALU.mult))
                st.link(ts(tmp, one, -1.0, 1e-30, ALU.add, ALU.max))
                st.link(dve.reciprocal(tmp, tmp))
                st.link(tt(lg, lg, tmp, ALU.mult))
                st.link(ts(tmp, one, 1.0, None, ALU.is_equal))
                st.link(tt(tmp, tmp, e, ALU.mult))
                st.link(tt(lg, lg, tmp, ALU.add))

            log1p_of_exp(ch(1)[:, :], ch(6)[:, :], ch(7)[:, :], ch(8)[:, :], ch(5)[:, :], "dt_abs", "dt_exp", "dt_one", "dt_log")
            st.link(stt(ch(1)[:, :], ch(1)[:, :], 0.0, ch(8)[:, :], ALU.max, ALU.add))
            dve.wait_ge(ev("a_exp"), 1)
            st.link(ts(ch(4)[:, :], ch(1)[:, :], ch(0)[:, 2:3], -1.0, ALU.mult, ALU.mult))
            st.link(dve.tensor_tensor_scan(ch(2)[:, :], cs("reset", 16)[:, 3 * T:4 * T], ch(4)[:, :], 0.0, ALU.mult, ALU.add))
            for w in range(2):
                s = slice(w * P, w * P + P)
                st(tt(ch(4)[:, s], ch(2)[:, w * P + 127:w * P + 128].to_broadcast([16, P]), ch(2)[:, s], ALU.subtract))
            st(dve.memset(ch(3)[:, 256:T], 1.0))
            st(tt(dia[0:16], ch(2)[:, :].unsqueeze(1).to_broadcast([16, 16, T]),
                  ident[0:16, 0:16].unsqueeze(2).to_broadcast([16, 16, T]), ALU.mult))
            st(dve.memset(chan_ones, 1.0))
            st.wait()
            dve.nop().then_inc(ev("m2_end"), 1)
            dve.nop().then_inc(ev("m2_dia"), 1)
            dve.wait_ge(ev("m2_end_exp"), 1)
            dve.nop().then_inc(ev("m2_rows"), 1)
            dve.wait_ge(ev("m2_rows_turned"), 1)
            pr = ps[:, 0, 0:144].rearrange("p (w i h) -> p w i h", w=3, i=3)
            st(dve.tensor_copy(tkq[:, 0:2], pr[:, 0:2]))
            st(dve.tensor_copy(tkq[0:16, 2], pr[0:16, 2]))
            st.wait()
            for w, (t0, n) in enumerate(WINDOWS):
                for half in range(2):
                    i = 2 * w + half
                    dve.wait_ge(ev("m2_x_turned"), i + 1)
                    dst = m2_x[0:n, w, 512 * half:512 * half + 512].rearrange("p (h c) -> p h c", h=8)
                    tt(dst, ps[0:n, 1 + i % 4, :].rearrange("p (h c) -> p h c", h=8),
                       tkq[0:n, w, 0, 8 * half:8 * half + 8].unsqueeze(2).to_broadcast([n, 8, 64]), ALU.mult).then_inc(ev("m2_x_copied"), 1)
            dve.wait_ge(ev("m2_x_copied"), 6)
            for w in range(2):
                st(tt(m2_xe[:, w, :].rearrange("p (h c) -> p h c", h=16), m2_x[:, w, :].rearrange("p (h c) -> p h c", h=16),
                      tkq[:, w, 2, :].unsqueeze(2).to_broadcast([P, 16, 64]), ALU.mult))
            dve.wait_ge(ev("m2_b_turned"), 1)
            st(dve.tensor_copy(m2_b, ps[:, 5, :].rearrange("p (w g c) -> p w g c", w=2, g=2)))
            st.wait()
            dve.nop().then_inc(ev("m2_xe"), 1)
            dve.wait_ge(ev("m2_cb"), 1)
            st(tt(m2_cb.rearrange("p g w c -> p (g w) c"), ps[:, 6, :].rearrange("p (g c) -> p g c", g=4),
                  cs("causal").unsqueeze(1).to_broadcast([P, 4, P]), ALU.mult))
            st(tt(m2_cb2[0:16], ps[0:16, 7, 0:32].rearrange("p (g c) -> p g c", g=2),
                  cs("causal", 16)[:, 0:16].unsqueeze(1).to_broadcast([16, 2, 16]), ALU.mult))
            st.wait()
            dve.nop().then_inc(ev("m2_cbm"), 1)
            dve.wait_ge(ev("m2_update"), 1)
            for g in range(2):
                st(dve.tensor_copy(m2_S[:, 0, 512 * g:512 * g + 512], ps[:, 1 + g, :]))
                st(dve.tensor_copy(m2_S[:, 1, 512 * g:512 * g + 512], ps[:, 3 + g, :]))
            st.wait()
            dve.nop().then_inc(ev("m2_S_copied"), 1)
            for q in range(4):
                g = q // 2
                dve.wait_ge(ev("m2_a"), q + 1)
                if q:
                    dve.wait_ge(ev("m2_y"), 2 * q)
                bufs = ((m2P0[:], P), (m2P1[:], P), (m2P2[:], 16))
                for w, (buf, n) in enumerate(bufs):
                    if w:
                        dve.wait_ge(ev("m2_ea"), 2 * q + w)
                    st.link(tt(buf, ps[0:n, 5 + w, 0:4 * n].rearrange("p (h t) -> p h t", h=4),
                               tkq[0:n, w, 1, 4 * q:4 * q + 4].unsqueeze(2).to_broadcast([n, 4, n]), ALU.subtract))
                    ts(buf, buf, 0.0, None, ALU.min).then_inc(ev("m2_seg"), 1)
                dve.wait_ge(ev("m2_ea"), 2 * q + 2)
                hs = slice(256 * q, 256 * q + 256)
                s0 = m2_S[:, 0, hs].rearrange("p (h c) -> p h c", h=4)
                s1 = m2_S[:, 1, hs].rearrange("p (h c) -> p h c", h=4)
                tmp = m2_seg[:, 0, 0:256].rearrange("p (h c) -> p h c", h=4)
                st.link(tt(tmp, s0, m2C[:, :, 127:128].to_broadcast([P, 4, 64]), ALU.mult))
                st.link(tt(s1, s1, tmp, ALU.add))
                st(tt(m2C[:], m2C[:], proj[:, TCM + g, 128:T].unsqueeze(1).to_broadcast([P, 4, 144]), ALU.mult))
                for w, (buf, n) in enumerate(bufs):
                    dve.wait_ge(ev("m2_seg_exp"), 3 * q + w + 1)
                    cb = m2_cb[:, g, w, :] if w < 2 else m2_cb2[0:16, g, :]
                    st(tt(buf, buf, cb.unsqueeze(1).to_broadcast([n, 4, n]), ALU.mult))
                st.wait()
                dve.nop().then_inc(ev("m2_pc"), 1)
                for pair in range(2):
                    c = 2 * q + pair
                    dve.wait_ge(ev("m2_y"), c + 1)
                    st.link(stt(m2_t[:, pair, :], proj[:, TX + c, :], bcast8[:, c:c + 1], ps[:, pair, 0:T], ALU.mult, ALU.add))
                    tt(proj[:, TZ + c, :], m2_t[:, pair, :], proj[:, TZ + c, :], ALU.mult).then_inc(ev("m2_gated"), 1)
            dve.wait_ge(ev("m2_gated"), 8)
            for g in range(2):
                st.link(tt(uT[:, 0:4, :], proj[:, TZ + 4 * g:TZ + 4 * g + 4, :], proj[:, TZ + 4 * g:TZ + 4 * g + 4, :], ALU.mult))
                dve.nop().then_inc(ev("m2_sq"), 1)
                dve.wait_ge(ev("m2_mean"), g + 1)
                ts(bc[:, 0, 0:T], ps[:, 2 + g, 0:T], 1e-6, None, ALU.add).then_inc(ev("m2_eps"), 1)
                dve.wait_ge(ev("m2_root"), g + 1)
                st.link(dve.reciprocal(bc[:, 2, 0:T], bc[:, 1, 0:T]))
                for k in range(4):
                    m = TZ + 4 * g + k
                    st(stt(proj[:, m, :], proj[:, m, :], pc("m2n", 4 * g + k), bc[:, 2, 0:T], ALU.mult, ALU.mult))
                st.wait()
            dve.nop().then_inc(ev("mix_ready"), 1)
            if stop <= 4:
                return
            tile[0] = 8 + NPROJ + 1

            def add_tile(k, n=T):
                t = tile[0]
                dve.wait_ge(ev("tiles_done"), t + 1)
                tt(hT[:, k, 0:n], hT[:, k, 0:n], ps[:, t % TB, 0:n], ALU.add).then_inc(ev("tiles_freed"), 1)
                tile[0] += 1

            for k in range(KT):
                add_tile(k)
            dve.wait_ge(ev("tiles_freed"), tile[0])
            st.link(tt(uT[:], hT[:], hT[:], ALU.mult))
            dve.nop().then_inc(ev("sq"), 1)
            normed(2, "norm2", "u2")
            if stop <= 5:
                return
            for i in range(FT):
                for s in range(2):
                    t = tile[0]
                    m = s * FT + i
                    dve.wait_ge(ev("ffn_tap"), 2 * i + s + 1)
                    o, x = fc[:, i % 2, s, :], ps[:, t % TB, :]
                    st.link(stt(o[:, 1:T], x[:, 0:T - 1], pc("ffw01", 44 + m), o[:, 1:T], ALU.mult, ALU.add))
                    st.link(stt(o[:, 2:T], x[:, 0:T - 2], pc("ffw01", m), o[:, 2:T], ALU.mult, ALU.add))
                    dve.nop().then_inc(ev("tiles_freed"), 1)
                    dve.nop().then_inc(ev("ffn_conv"), 1)
                    tile[0] += 1
                dve.wait_ge(ev("ffn_silu"), i + 1)
                tt(act_[:, i, :], fc[:, i % 2, 0, :], fc[:, i % 2, 1, :], ALU.mult).then_inc(ev("ffn_act"), 1)
            for k in range(KT):
                add_tile(k)
            dve.wait_ge(ev("tiles_freed"), tile[0])
            st.link(tt(uT[:], hT[:], hT[:], ALU.mult))
            dve.nop().then_inc(ev("sq"), 1)
            inverse_root(3, T, ps[:, 7, 0:T])
            for k in range(KT):
                st(stt(uT[:, k, :], hT[:, k, :], pc("fin", k), bc[:, 2, 0:T], ALU.mult, ALU.mult))
            st.wait()
            st.link(dve.tensor_copy(hT[:, :, 0:L], uT[:, :, META:T]))
            if stop <= 6:
                return
            cstream = uT[:].rearrange("p a b -> p (a b)")[:, 0:KT * L].rearrange("p (k c) -> p k c", k=KT)
            for k in range(KT):
                t = tile[0]
                dve.wait_ge(ev("tiles_done"), t + 1)
                dve.tensor_copy(cstream[:, k, :], ps[:, t % TB, 0:L]).then_inc(ev("tiles_freed"), 1)
                tile[0] += 1
            dve.wait_ge(ev("tiles_freed"), tile[0])
            st(tt(hx[:, :, 0:L], hT[:, :, 0:L], hT[:, :, 0:L], ALU.mult))
            st(tt(hx[:, :, L:2 * L], cstream, cstream, ALU.mult))
            st.wait()
            dve.nop().then_inc(ev("sq"), 1)
            gain = small[:, 128:144].rearrange("p (k c) -> p k c", c=2)

            def scaled_gain(dst, name, first, c):
                st(stt(dst, mod[:, first:first + 8, c], 1.0, pc(name, 0, 8), ALU.add, ALU.mult))

            scaled_gain(gain[:, :, 0], "prem", 8, 0)
            scaled_gain(gain[:, :, 1], "prem", 8, 1)
            inverse_root(4, 2 * L, ps[:, 7, :])
            for c in range(2):
                src = (hT[:, :, 0:L], cstream)[c]
                for k in range(KT):
                    st(stt(hx[:, k, c * L:c * L + L], src[:, k, :], gain[:, k, c:c + 1], bc[:, 2, c * L:c * L + L], ALU.mult, ALU.mult))
            st.wait()
            for c in range(2):
                st(tt(hx[:, :, c * L:c * L + L], hx[:, :, c * L:c * L + L],
                      mod[:, 0:8, c:c + 1].to_broadcast([P, KT, L]), ALU.add))
            st.wait()
            dve.nop().then_inc(ev("hx_ready"), 1)
            lgt = bcast8[:, 24:32]
            log1p_of_exp(lgt, small[:, 40:48], small[:, 48:56], small[:, 56:64], small[:, 32:40], "lg_abs", "lg_exp", "lg_one", "lg_log")
            st.link(stt(small[:, 80:88], lgt, 0.0, small[:, 56:64], ALU.min, ALU.subtract))
            dve.nop().then_inc(ev("lg_ready"), 1)
            tile[0] += 28
            dve.wait_ge(ev("p2_done"), 28)
            for j in range(2 * RH):
                n = L if j < RH else 2 * L
                src = pq[:, j, :] if j < RH else pk[:, j - RH, :]
                t = tile[0]
                dve.wait_ge(ev("tiles_done"), t + 1)
                st.link(tt(rt[:, 0, 0:n], ps[:, t % TB, 0:n], dist[:, 10:12, :].rearrange("p a b -> p (a b)")[:, 0:n], ALU.mult))
                dve.nop().then_inc(ev("tiles_freed"), 1)
                st.link(tt(src, src, dist[:, 8:10, :].rearrange("p a b -> p (a b)")[:, 0:n], ALU.mult))
                st.link(tt(src, src, rt[:, 0, 0:n], ALU.add))
                tile[0] += 1
            for h in range(RH):
                t = tile[0]
                dve.wait_ge(ev("tiles_done"), t + 1)
                st.link(dve.tensor_copy(vtok[:, h], ps[:, t % TB, :].rearrange("p (a b) -> p a b", a=4)))
                if h == 0:
                    dve.wait_ge(ev("tiles_done"), t + 1)
                dve.nop().then_inc(ev("tiles_freed"), 1)
                tile[0] += 1
            for h in range(RH):
                st.link(ts(rD[:, 0:2, :], dist[:, 0:2, :], small[:, 80 + h:81 + h], None, ALU.mult))
                st.link(stt(rD[:, 0:2, :], dist[:, 2:4, :], small[:, 84 + h:85 + h], rD[:, 0:2, :], ALU.mult, ALU.add))
                dve.nop().then_inc(ev("ret_arg"), 1)
                dve.wait_ge(ev("ret_d"), h + 1)
                st.link(tt(rD[:, 2:4, :], rD[:, 2:4, :], rt[:, :, :].rearrange("p a b -> p (a b)")[:, 0:512].rearrange("p (a b) -> p a b", a=2), ALU.add))
                dve.wait_ge(ev("ret_s"), h + 1)
                for b in range(2):
                    st(stt(rP[:, 2 * b:2 * b + 2, :], ps[:, b, :].rearrange("p (a b) -> p a b", a=2), float(P) ** -0.5,
                           rD[:, 2 * b:2 * b + 2, :], ALU.mult, ALU.mult))
                st.wait()
                dve.nop().then_inc(ev("ret_p"), 1)
                dve.wait_ge(ev("ret_o"), h + 1)
                st.link(dve.tensor_copy(ry[:, h, :], ps[:, 2, 0:L]))
                dve.nop().then_inc(ev("ret_y"), 1)
            dve.wait_ge(ev("ret_mu"), 1)
            for b in range(2):
                st(tt(ry[:, 2 * b:2 * b + 2, :], ry[:, 2 * b:2 * b + 2, :], ps[:, 3 + b, :].rearrange("p (a b) -> p a b", a=2), ALU.subtract))
            st.wait()
            st.link(tt(rD[:], ry, ry, ALU.mult))
            dve.nop().then_inc(ev("ret_sq"), 1)
            dve.wait_ge(ev("ret_var"), 1)
            for b in range(2):
                st(ts(rD[:, 2 * b:2 * b + 2, :], ps[:, b, :].rearrange("p (a b) -> p a b", a=2), 1e-6, None, ALU.add))
            st.wait()
            dve.nop().then_inc(ev("ret_eps"), 1)
            dve.wait_ge(ev("ret_root"), 1)
            st.link(dve.reciprocal(rP[:], rD[:]))
            m2x = pk[:].rearrange("p a b -> p (a b)").rearrange("p (k c) -> p k c", k=8)
            for h in range(RH):
                st(stt(ry[:, h, :], ry[:, h, :], pc("retn", h), rP[:, h, :], ALU.mult, ALU.mult))
            st.wait()
            st(tt(m2x[:, 4:8, :], ry, pg, ALU.mult))
            st.link(tt(pu, pu, pcg, ALU.mult))
            for k in range(4):
                st(ts(m2x[:, k, :], pu[:, k, :], pc("cw2", 4 + k), pc("cb2", k), ALU.mult, ALU.add))
            st.wait()
            for k in range(4):
                o = m2x[:, k, :].rearrange("p (r c) -> p r c", c=64)
                x = pu[:, k, :].rearrange("p (r c) -> p r c", c=64)
                st.link(stt(o[:, :, 1:64], x[:, :, 0:63], pc("cw2", k), o[:, :, 1:64], ALU.mult, ALU.add))
                st.link(stt(o[:, :, 0:63], x[:, :, 1:64], pc("cw2", 8 + k), o[:, :, 0:63], ALU.mult, ALU.add))
            st.link(tt(m2x[:, 0:4, :], m2x[:, 0:4, :], pb, ALU.mult))
            dve.nop().then_inc(ev("mix2_ready"), 1)
            if stop <= 7:
                return
            uflat = cstream

            for k in range(KT):
                t = tile[0]
                dve.wait_ge(ev("tiles_done"), t + 1)
                dve.tensor_copy(mx[:, k, :], ps[:, t % TB, 0:L]).then_inc(ev("tiles_freed"), 1)
                tile[0] += 1
            dve.wait_ge(ev("tiles_freed"), tile[0])

            def post(i, name, gate, src):
                st.link(tt(uflat, src, src, ALU.mult))
                dve.nop().then_inc(ev("sq"), 1)
                st(tt(small[:, 128:136], mod[:, gate:gate + 8, 0], pc(name, 0, 8), ALU.mult))
                inverse_root(i, L, ps[:, 7 if i < 7 else 0, 0:L])
                for k in range(KT):
                    st(stt(uflat[:, k, :], src[:, k, :], small[:, 128 + k:129 + k], bc[:, 2, 0:L], ALU.mult, ALU.mult))
                st.wait()
                st.link(tt(hT[:, :, 0:L], hT[:, :, 0:L], uflat, ALU.add))

            post(5, "postm", 16, mx)
            st.link(tt(uflat, hT[:, :, 0:L], hT[:, :, 0:L], ALU.mult))
            dve.nop().then_inc(ev("sq"), 1)
            st(stt(small[:, 144:152], mod[:, 32:40, 0], 1.0, pc("pref", 0, 8), ALU.add, ALU.mult))
            inverse_root(6, L, ps[:, 7, 0:L])
            for k in range(KT):
                st(stt(h2[:, k, :], hT[:, k, 0:L], small[:, 144 + k:145 + k], bc[:, 2, 0:L], ALU.mult, ALU.mult))
            st.wait()
            st.link(tt(h2, h2, mod[:, 24:32, 0:1].to_broadcast([P, KT, L]), ALU.add))
            dve.nop().then_inc(ev("h2_ready"), 1)
            dve.wait_ge(ev("logits"), 1)
            st.link(tt(aff, ps[:, 6, 0:32].rearrange("p (w e) -> p w e", w=2), bcast8[:, 8:24].unsqueeze(1).to_broadcast([P, 2, NE]), ALU.add))
            st.link(dve.tensor_reduce(small[:, 160:162], aff, AX, ALU.max))
            st.link(tt(aff, aff, small[:, 160:162].unsqueeze(2).to_broadcast([P, 2, NE]), ALU.subtract))
            dve.nop().then_inc(ev("soft_shift"), 1)
            dve.wait_ge(ev("soft_exp"), 1)
            st.link(dve.tensor_reduce(small[:, 162:164], aff, AX, ALU.add))
            st.link(dve.reciprocal(small[:, 164:166], small[:, 162:164]))
            st.link(tt(aff, aff, small[:, 164:166].unsqueeze(2).to_broadcast([P, 2, NE]), ALU.mult))
            dve.nop().then_inc(ev("aff_ready"), 1)
            dve.wait_ge(ev("aff_turned"), 1)
            st.link(dve.tensor_copy(rtk[0:16, 0, :], ps[0:16, 7, 0:L]))
            for i in range(4):
                st.link(dve.max(rtk[0:16, 4, 8 * i:8 * i + 8], rtk[0:16, i % 2, :]))
                st.link(dve.match_replace(rtk[0:16, (i + 1) % 2, :], rtk[0:16, 4, 8 * i:8 * i + 8], rtk[0:16, i % 2, :], -1.0))
            st.link(ts(rtk[0:16, 1, :], rtk[0:16, 0, :], 0.0, None, ALU.is_lt))
            st.link(dve.memset(rtk[0:16, 5, :], 1.0))
            st.link(dve.tensor_tensor_scan(rtk[0:16, 2, :], rtk[0:16, 5, :], rtk[0:16, 1, :], 0.0, ALU.mult, ALU.add))
            st.link(tt(rtk[0:16, 3, :], rtk[0:16, 2, :], rtk[0:16, 1, :], ALU.mult))
            dve.nop().then_inc(ev("rank_ready"), 1)
            dve.wait_ge(ev("h2_turned"), 1)
            for i in range(4):
                st(dve.tensor_copy(h2tok[:, i // 2, (i % 2) * 512:(i % 2) * 512 + 512], ps[:, i, :]))
            dve.wait_ge(ev("rank_turned"), 1)
            st.link(dve.tensor_copy(small[:, 168:200], ps[:, 5, 0:32]))
            for w in range(2):
                st(tt(sel[:, w], small[:, 168 + 16 * w:184 + 16 * w].unsqueeze(2).to_broadcast([P, NE, CAP]),
                      cs("slot").unsqueeze(1).to_broadcast([P, NE, CAP]), ALU.is_equal))
            st.wait()
            for w in range(2):
                st(tt(selg[:, w], sel[:, w], aff[:, w, :].unsqueeze(2).to_broadcast([P, NE, CAP]), ALU.mult))
            st(dve.memset(uT[:], 0.0))
            st.wait()
            dve.nop().then_inc(ev("sel_ready"), 1)
            dve.nop().then_inc(ev("zero_ready"), 1)
            if stop <= 8:
                return
            SX = 4
            with dve.Fori(0, NE) as e:
                st.loop(e, SX)
                for w in range(2):
                    st(dve.tensor_copy(sg4[:, w], selg[:, w, e, :].unsqueeze(1).to_broadcast([P, 4, CAP])))
                st.wait()
                dve.nop().then_inc(ev("sg4_ready"), 1)
                dve.wait_ge(ev("gathered"), e + 1)
                st(dve.tensor_copy(xs, ps[:, 3, 0:256].rearrange("p (k s) -> p k s", k=KT)))
                st(dve.tensor_copy(Gt, ps[:, 3, 256:512]))
                st.wait()
                dve.nop().then_inc(ev("xs_ready"), 1)
                dve.wait_ge(ev("gate_silu"), e + 1)
                tt(he, sa, ps[:, 1, :], ALU.mult).then_inc(ev("hidden"), 1)
                dve.wait_ge(ev("units_used"), e * 12 + (U0 + 12))
                dve.tensor_copy(ye[:, 512:1024], ps[:, 1, :]).then_inc(ev("y_other"), 1)
                dve.wait_ge(ev("y_other"), e + 1)
                dve.wait_ge(ev("y_half"), e + 1)
                dve.nop().then_inc(ev("y_ready"), 1)
                dve.wait_ge(ev("scattered"), e + 1)
            st.close(NE, SX)
            dve.wait_ge(ev("experts_done"), 1)
            for b in range(4):
                st(dve.tensor_copy(mx[:, 2 * b:2 * b + 2, :], ps[:, 4 + b, :].rearrange("p (a c) -> p a c", a=2)))
            st.wait()
            post(7, "postf", 40, mx)
            dve.nop().then_inc(ev("y_final"), 1)
            dve.wait_ge(ev("y_turned"), 1)
            for i in range(4):
                st(dve.tensor_copy(otok[:, i // 2, (i % 2) * 512:(i % 2) * 512 + 512], ps[:, 4 + i, :]))
            st.wait()
            dve.nop().then_inc(ev("out_ready"), 1)


NAMES = ["x", "meta_tokens", "norm1_w", "w_in", "hg_lb_logits", "hg_norm_w", "m2_conv_w", "m2_conv_b", "m2_dt_bias",
         "m2_a_log", "m2_d", "m2_norm_w", "w_out", "norm2_w", "ffn_w_up", "ffn_conv_w", "ffn_conv_b", "ffn_w_down",
         "final_norm_w", "c_2", "ctx_2", "c_ctx_2", "w_ada_2", "b_ada_2", "pre_mix_g_2", "post_mix_g_2", "pre_ffn_g_2",
         "post_ffn_g_2", "w_in_2", "conv_w_2", "conv_b_2", "ret_decay_logit_2", "ret_norm_g_2", "w_out_2",
         "w_router_2", "b_router_2", "w_gate_2", "w_up_2", "w_down_2"]


def kernel(**inputs):
    import concourse.bacc as bacc
    from concourse.bass_utils import run_bass_kernel_spmd

    nc = bacc.Bacc("TRN2", target_bir_lowering=False, num_devices=1, dynamic_dma_scratch_size=1024)
    arrays = {n: np.ascontiguousarray(inputs[n]) for n in NAMES}
    arrays["cst"], arrays["dist"] = constants()
    aps = {n: nc.dram_tensor("in_" + n, v.shape, mybir.dt.from_np(v.dtype), kind="ExternalInput").ap() for n, v in arrays.items()}
    out = nc.dram_tensor("out_y", (1, SEQ, D), F32, kind="ExternalOutput").ap()
    build(nc, aps, out)
    r = run_bass_kernel_spmd(nc, [{"in_" + n: v for n, v in arrays.items()}], core_ids=[0])
    return r.results[0]["out_y"]
```

```python
from contextlib import ExitStack

import numpy as np
import concourse.bass as bass
from concourse import mybir

F32 = mybir.dt.float32
U32 = mybir.dt.uint32
ACT = mybir.ActivationFunctionType
ALU = mybir.AluOpType
AX = mybir.AxisListType.X

P = 128
D = 1024
KT = D // P
META, SEQ = 16, 256
T = META + SEQ
WINDOWS = [(0, 128), (128, 128), (256, 16)]
LEVELS = [16, 32, 64, 128]
HEADS = 8
M2H, M2P, M2G = 16, 64, 2
FF = 2816
FT = FF // P
L = 256
RH = 4
NE, CAP, DE = 16, 32, 2048
RING = 6
UNIT = 4096
TB = 3
WORDS = 21900

TQ, TF_, TI, TG, TZ, TX, TBM, TCM = 0, 8, 16, 24, 32, 40, 48, 50
NPROJ = 52


def par_rows():
    plan = [
        [("norm1", 8), ("lb0", 8), ("lb1", 8), ("hgn", 8), ("m2cw", 48), ("m2cb", 12), ("m2n", 8),
         ("norm2", 8), ("fin", 8)],
        [("ffw01", 88), ("prem", 8), ("postm", 8), ("pref", 8), ("postf", 8)],
        [("ffw2", 44), ("ffb", 44), ("cw2", 12), ("cb2", 4), ("retn", 4), ("c", 8), ("cctx", 8)],
        [("bada", 48)],
    ]
    where = {}
    for b, names in enumerate(plan):
        at = 0
        for name, n in names:
            where[name] = (b, at, n)
            at += n
    return where


PAR = par_rows()

CST = {}
_at = 0
for _name, _n in [("ident", P), ("rot", P), ("causal", P), ("mask", 4 * P), ("reset", 4 * T), ("sel2", 2),
                  ("slot", CAP)]:
    CST[_name] = (_at, _n)
    _at += _n
NCST = _at
NDIST = 8 * L


def constants():
    c = np.zeros((P, NCST), np.float32)

    def put(name, a):
        at, n = CST[name]
        c[:, at:at + n] = a

    i = np.arange(P)
    put("ident", np.eye(P))
    rot = np.zeros((P, P), np.float32)
    rot[i[64:], i[:64]] = -1.0
    rot[i[:64], i[64:]] = 1.0
    put("rot", rot)
    s, r = i[:, None], i[None, :]
    put("causal", s <= r)
    masks = [(s // 16 == r // 16) & (s <= r)]
    for w in LEVELS[1:]:
        masks.append((s // w == r // w) & (s % w < w // 2) & (r % w >= w // 2))
    put("mask", np.concatenate(masks, 1))
    t = np.arange(T)
    put("reset", np.tile(np.concatenate([t % w != 0 for w in LEVELS])[None], (P, 1)))
    put("sel2", (i[:, None] % 32) == np.arange(2)[None])
    put("slot", np.tile(np.arange(1, CAP + 1, dtype=np.float32)[None], (P, 1)))
    inv = (1.0 / (np.float32(10000.0) ** (np.arange(64, dtype=np.float32) / np.float32(64)))).astype(np.float32)
    pos = np.concatenate([L + np.arange(L), np.arange(L)]).astype(np.float32)
    ang = (pos[None, :] * inv[:, None]).astype(np.float32)
    n = np.arange(L)[None, :]
    lat = [np.maximum(n - (128 * k + s), 0) for k in range(2)] + [np.maximum((128 * k + s) - n, 0) for k in range(2)]
    ctx = [L + n - (128 * k + s) for k in range(2)] + [L - n + (128 * k + s) for k in range(2)]
    dist = np.concatenate(lat + ctx + [np.tile(f(ang), (2, 1)) for f in (np.cos, np.sin)], 1).astype(np.float32)
    return c, dist


class Steps:

    def __init__(self, engine, sem):
        self.engine, self.sem, self.n, self.turn = engine, sem, 0, 0

    def __call__(self, ins):
        self.n += 1
        ins.then_inc(self.sem, 1)

    def wait(self):
        self.engine.wait_ge(self.sem, self.turn + self.n)

    def link(self, ins):
        self(ins)
        self.wait()

    def loop(self, i, steps):
        self.turn = self.turn + i * steps
        self.start = self.n

    def close(self, turns, steps):
        assert self.n - self.start == steps, (self.n - self.start, steps)
        self.turn = 0
        self.n += (turns - 1) * steps


def build(nc, a, out, stop=99):
    with ExitStack() as ctx:
        def sb(name, shape, dt=F32):
            return ctx.enter_context(nc.sbuf_tensor(name, shape, dt))

        sems = {}

        def ev(name):
            if name not in sems:
                sems[name] = ctx.enter_context(nc.semaphore("s_" + name))
            return sems[name]

        ring = sb("ring", [P, RING, UNIT])
        cst = sb("cst", [P, NCST])
        hT = sb("hT", [P, KT, T])
        uT = sb("uT", [P, KT, T])
        par = sb("par", [P, 4 * P])
        mod = sb("mod", [P, 48, 2])
        cond = sb("cond", [P, KT, 32])
        ones = sb("ones", [P, P])
        ones4 = sb("ones4", [P, P])
        ones1 = sb("ones1", [P, P])
        eps = sb("eps", [P, 1])
        bc = sb("bc", [P, 2, 2 * L])
        small = sb("small", [P, 256])
        wsm = sb("wsm", [P, 2, KT, 16])
        chan = sb("chan", [16, 2, T])
        tkq = sb("tkq", [P, 3, 3, 16])
        bcast8 = sb("bcast8", [P, 40])
        arena = sb("arena", [P, WORDS])
        ps = ctx.enter_context(nc.psum_tensor("ps", [P, 8, 512], F32))

        class Arena:

            def __init__(self, at):
                self.at = at

            def take(self, *shape):
                n = int(np.prod(shape))
                v = arena[:, self.at:self.at + n]
                self.at += n
                assert self.at <= WORDS, self.at
                if len(shape) == 2:
                    v = v.rearrange("p (a b) -> p a b", a=shape[0])
                if len(shape) == 3:
                    v = v.rearrange("p (a b c) -> p a b c", a=shape[0], b=shape[1])
                return v

        def cs(name, rows=P):
            at, n = CST[name]
            return cst[0:rows, at:at + n]

        ident = cs("ident")

        def pc(name, i=0, n=1):
            b, at, rows = PAR[name]
            return par[:, b * P + at + i:b * P + at + i + n]

        A = Arena(0)
        proj = A.take(NPROJ, T)
        mrow = A.take(512)
        x_at = A.at
        tok = A.take(3, D)
        prow = A.take(4, P)
        A = Arena(x_at)
        hg_B = A.take(2, 4, T)
        hg_D = A.take(2, 4, 256)
        hg_K0 = A.take(2, T)
        hg_f = A.take(T)
        hg_k = A.take(T)
        hg_lf = A.take(T)
        hg_v = A.take(3, P)
        hg_ke = A.take(2, P)
        hg_P = A.take(2, P)
        hg_P2 = A.take(16)
        hg_S = A.take(2, P)
        hg_sq = A.take(T)
        hg_o = hg_sq
        A = Arena(x_at)
        m2_t = A.take(2, T)
        rows_at = A.at
        m2_x = A.take(3, 512)
        m2_xe = A.take(2, 512)
        m2_b = A.take(2, P)
        m2_cb = A.take(2, P)
        m2_cb2 = A.take(16)
        m2_S = A.take(2, 512)
        m2_seg = A.take(256)
        m2P0 = A.take(4, P)
        m2P1 = A.take(4, P)
        m2P2 = A.take(4, 16)[0:16]
        m2C = A.take(4, 144)

        def ch(row):
            return chan[:, row, :] if row < 2 else arena[0:16, rows_at + (row - 2) * T:rows_at + (row - 1) * T]

        A = Arena(0)
        act_ = A.take(FT, T)
        fc = A.take(2, 2, T)
        dist = A.take(12, L)
        ctok = A.take(2, D)
        vtok = ctok.rearrange("p w (a b) -> p (w a) b", b=512).rearrange("p h (t c) -> p h t c", t=4)
        hx_at = A.at
        hx = A.take(KT, 2 * L)
        pcg = A.take(4, L)
        pu = A.take(4, L)
        pg = A.take(4, L)
        rD = A.take(2, 4, L)
        A = Arena(0)
        pq = A.take(4, L)
        pk = A.take(4, 2 * L)
        pv = A.take(4, 2 * L)
        pb = A.take(4, L)
        A = Arena(hx_at)
        mixed = A.take(KT, L)
        mx = A.take(KT, L)
        rr = cst[:, CST["mask"][0]:CST["mask"][0] + 4 * L].rearrange("p (a b) -> p a b", a=2)
        rP_ = uT[:].rearrange("p a b -> p (a b)")[:, 0:8 * L].rearrange("p (a b c) -> p a b c", a=2, b=4)
        ry = pq
        A = Arena(0)
        h2 = A.take(KT, L)
        h2tok = A.take(2, D)
        sel = A.take(2, NE, CAP)
        selg = A.take(2, NE, CAP)
        aff = A.take(2, NE)
        rtk = A.take(8, L)
        sg4 = A.take(2, 4, CAP)
        Gt = A.take(L)
        xs = A.take(KT, CAP)
        sa = A.take(512)
        he = A.take(512)
        heT = A.take(4, P)
        ye = A.take(D)
        assert A.at <= hx_at
        A = Arena(hx_at + 2 * KT * L)
        otok = A.take(2, D)

        def slot(u):
            return ring[:, u % RING, :]

        units = []

        def unit(pieces):
            units.append(pieces)
            return len(units) - 1

        def kview(w):
            return w.rearrange("(k p) c -> p k c", p=P)

        def cols(w, c0, k0=0, k1=KT, n=512):
            u = len(units)
            return unit([(slot(u)[:, 0:(k1 - k0) * n].rearrange("p (k c) -> p k c", c=n),
                          kview(w)[:, k0:k1, c0:c0 + n])])

        w_in, w_ada = a["w_in"][0], a["w_ada_2"][0]
        ORDER = [10, 11, 12, 2, 0, 4, 6, 3, 1, 5, 7, 8, 9]
        u_in, u_ada = [], []
        for n, blk in enumerate(ORDER):
            u_in.append(cols(w_in, 512 * blk))
            if n < 12:
                u_ada.append(cols(w_ada, 512 * n))
        u_out = [[cols(a["w_out"][0], 512 * cb, 8 * kh, 8 * kh + 8) for cb in range(2)] for kh in (1, 0)]
        u_up = []
        for i in range(11):
            v = slot(len(units)).rearrange("p (k s c) -> p k s c", k=KT, s=2)
            w = kview(a["ffn_w_up"][0])
            u_up.append(unit([(v[:, :, s, :], w[:, :, FF * s + 256 * i:FF * s + 256 * i + 256]) for s in range(2)]))
        DK = [(0, 8), (8, 16), (16, 22)]
        u_dn = [[cols(a["ffn_w_down"][0], 512 * cb, k0, k1) for k0, k1 in DK] for cb in range(2)]
        ORDER2 = [3, 4, 5, 6, 1, 2, 0]
        u_in2 = [cols(a["w_in_2"][0], 512 * n) for n in ORDER2]
        u_out2 = [cols(a["w_out_2"][0], 512 * n) for n in range(2)]
        U0 = len(units)
        slot_count = [0] * RING
        ready_at = []
        for u, pieces in enumerate(units):
            slot_count[u % RING] += 16 * len(pieces)
            ready_at.append(slot_count[u % RING])

        def slot_ready(u):
            return ev(f"slot{u % RING}_loaded")

        seq = [f"x{k}" for k in range(KT)] + ["n1"]
        for j in range(NPROJ):
            seq += ["dt"] * (j == 12) + ["mz0"] * (j == 50) + [f"p{j}"]
        seq += ["mz1"] + [f"ob{k}" for k in range(KT)] + [f"oa{k}" for k in range(KT)] + ["n2"]
        seq += [f"f{i}" for i in range(2 * FT)] + [f"d{k}" for k in range(KT)] + ["n3", "n4"]
        seq += [f"q{j}" for j in range(28)] + [f"w{k}" for k in range(KT)] + ["n5", "n6"]
        TN = {name: i for i, name in enumerate(seq)}

        def bank_of(name):
            return ps[:, TN[name] % TB, :]

        block = ctx.enter_context(nc.Block())
        PAR_LOADS = [9, 5, 7, 1]

        @block.sync
        def _(sp):
            def load(dst, src, sem, **kw):
                sp.dma_start(dst, src, **kw).then_inc(ev(sem), 16)

            load(cst[:], a["cst"], "cst_loaded")
            load(tok[0:16, 0, :], a["meta_tokens"], "tok_loaded")
            load(tok[16:128, 0, :], a["x"][0, 0:112], "tok_loaded")
            load(tok[:, 1, :], a["x"][0, 112:240], "tok_loaded")
            load(tok[0:16, 2, :], a["x"][0, 240:256], "tok_loaded")

            def stream(u):
                if u >= RING:
                    sp.wait_ge(ev("units_used"), u - RING + 1)
                for dst, src in units[u]:
                    sp.dma_start(dst, src).then_inc(slot_ready(u), 16)

            last = {1: 0, 2: 25, 4: 25, 5: 29, 6: 46}.get(stop, U0)
            for u in range(last):
                stream(u)
                if u == u_up[6]:
                    sp.wait_ge(ev("out_done"), 1)
                    load(dist[:].rearrange("p a b -> p (a b)"), a["dist"], "ctx_loaded")
                    load(ctok[:], a["ctx_2"][0].rearrange("(w p) c -> p w c", p=P), "ctx_loaded")
            if stop < 9:
                for u in range(max(0, last - RING), last):
                    sp.wait_ge(slot_ready(u), ready_at[u])
                if last > u_up[6]:
                    sp.wait_ge(ev("ctx_loaded"), 32)
            if stop >= 9:
                with sp.Fori(0, NE) as e:
                    for i in range(12):
                        s = (U0 + i) % RING
                        sp.wait_ge(ev("units_used"), e * 12 + (U0 + i - RING + 1))
                        if i < 8:
                            w = a["w_gate_2" if i < 4 else "w_up_2"][0, e]
                            src = kview(w)[:, 2 * (i % 4):2 * (i % 4) + 2, :]
                            dst = ring[:, s, :].rearrange("p (k c) -> p k c", k=2)
                        else:
                            src = a["w_down_2"][0, e].rearrange("(j b p) c -> b p j c", b=4, p=P)[i - 8]
                            dst = ring[:, s, :].rearrange("p (j c) -> p j c", j=4)
                        sp.dma_start(dst, src).then_inc(ev(f"slot{s}_loaded"), 16)
                for w in range(2):
                    sp.wait_ge(ev("out_ready"), w + 1)
                    sp.dma_start(out[0, w * P:w * P + P, :], otok[:, w, :]).then_inc(ev("stored"), 16)
                sp.wait_ge(ev("stored"), 32)

        @block.tensor
        def _(pe):
            opened = [0]

            def open_tile(name):
                assert TN[name] == opened[0], (name, opened[0])
                if opened[0] >= TB:
                    pe.wait_ge(ev("tiles_freed"), opened[0] - TB + 1)
                opened[0] += 1
                return bank_of(name)

            def done(mm):
                mm.then_inc(ev("tiles_done"), 1)

            def weights(u):
                pe.wait_ge(slot_ready(u), ready_at[u])

            def used(u_count=1):
                pe.wait_ge(ev("tiles_done"), opened[0])
                pe.nop().then_inc(ev("units_used"), u_count)

            def group(pairs, o):
                for i, (l, r) in enumerate(pairs):
                    mm = pe.matmul(o, l, r, start=i == 0, stop=i == len(pairs) - 1)
                return mm

            squares = [0]

            def norm_sum(name, n, src, w=ones, nk=KT):
                o = open_tile(name)
                for k in range(nk):
                    squares[0] += 1
                    pe.wait_ge(ev("squares"), squares[0])
                    mm = pe.matmul(o[:, 0:n], w[:], src(k), start=k == 0, stop=k == nk - 1)
                done(mm)

            pe.wait_ge(ev("cst_loaded"), 16)
            pe.wait_ge(ev("tok_loaded"), 64)
            for k in range(KT):
                o = open_tile(f"x{k}")
                for w, (t0, n) in enumerate(WINDOWS):
                    mm = pe.transpose(o[:, t0:t0 + n], tok[0:n, w, k * P:k * P + P], ident[0:n, 0:n])
                done(mm)
            pe.wait_ge(ev("par_loaded"), 16 * sum(PAR_LOADS))
            for b in range(4):
                mm = pe.transpose(ps[:, 3, b * P:b * P + P], prow[:, b, :], ident)
            mm.then_inc(ev("par_turned"), 1)
            norm_sum("n1", T, lambda k: uT[:, k, :])
            if stop <= 1:
                return

            def ada(n):
                weights(u_ada[n])
                if n:
                    pe.wait_ge(ev("mod_done"), n)
                else:
                    pe.wait_ge(ev("cond_ready"), 1)
                w = slot(u_ada[n]).rearrange("p (k c) -> p k c", k=KT)
                for k in range(KT):
                    j = k % 4
                    mm = pe.matmul(ps[32 * j:32 * j + 32, 3, :], cond[:, k, :], w[:, k, :], start=k < 4, stop=k >= 4)
                mm.then_inc(ev("units_used"), 1)

            def turn_mod(n):
                pe.wait_ge(ev("mod_row"), n + 1)
                for b in range(4):
                    mm = pe.matmul(ps[:, 3, 2 * b:2 * b + 2], mrow[:, b * P:b * P + P], cs("sel2"), start=True, stop=True)
                mm.then_inc(ev("mod_turned"), 1)

            def m2_turn_rows():
                pe.wait_ge(ev("m2_rows"), 1)
                for i, row in enumerate((1, 0, 3)):
                    for w, (t0, n) in enumerate(WINDOWS):
                        mm = pe.transpose(ps[0:n, 4, (w * 3 + i) * 16:(w * 3 + i) * 16 + 16], ch(row)[:, t0:t0 + n], ident[0:16, 0:16])
                mm.then_inc(ev("m2_rows_turned"), 1)

            def m2_turn(g):
                pe.wait_ge(ev("m2_conv"), 12)
                pe.wait_ge(ev("m2_tk"), 1)
                if g:
                    pe.wait_ge(ev("m2_out"), 4)
                for w, (t0, n) in enumerate(WINDOWS):
                    for c in range(4):
                        pe.transpose(ps[0:n, 4 + w, c * P:c * P + P], proj[:, TX + 4 * g + c, t0:t0 + n], ident)
                for w in range(2):
                    mm = pe.transpose(ps[:, 7, w * P:w * P + P], proj[:, TBM + g, w * P:w * P + P], ident)
                mm.then_inc(ev("m2_turned"), 1)

            def m2_states(g):
                pe.wait_ge(ev("m2_staged"), g + 1)
                for w in range(2):
                    s = slice(w * P, w * P + P)
                    pe.matmul(ps[:, 4, w * P:w * P + P], proj[:, TBM + g, s], proj[:, TCM + g, s], start=True, stop=True)
                pe.matmul(ps[0:16, 5, 0:16], proj[:, TBM + g, 256:T], proj[:, TCM + g, 256:T], start=True, stop=True)
                for w in range(2):
                    mm = pe.matmul(ps[:, 6 + w, :], m2_b[:, w, :], m2_xe[:, w, :], start=True, stop=True)
                mm.then_inc(ev("m2_update"), 1)

            def m2_spread(q):
                pe.wait_ge(ev("m2_group"), q // 2 + 1)
                pe.wait_ge(ev("m2_tk"), 1)
                if q % 2:
                    pe.wait_ge(ev("m2_out"), 2 * q)
                for w, (t0, n) in enumerate(WINDOWS):
                    for j in range(4):
                        hd = 4 * q + j
                        mm = pe.matmul(ps[:, (4, 5, 7)[w], j * n:j * n + n], ident[0:16, hd:hd + 1].to_broadcast([16, P]),
                                       ch(0)[:, t0:t0 + n], start=True, stop=True)
                mm.then_inc(ev("m2_a"), 1)

            def m2_heads(q):
                pe.wait_ge(ev("m2_pc"), q + 1)
                if q:
                    pe.wait_ge(ev("m2_out"), 2 * q)
                for pair in range(2):
                    for hh in range(2):
                        j = 2 * pair + hh
                        hc = (4 * (q % 2) + j) * M2P
                        o = ps[64 * hh:64 * hh + 64, 6 + pair, :]
                        pe.matmul(o[:, 0:128], m2_x[:, 0, hc:hc + M2P], m2P0[:, j, :], start=True, stop=True)
                        pe.matmul(o[:, 128:256], m2_x[:, 1, hc:hc + M2P], m2P1[:, j, :], start=True, stop=False)
                        pe.matmul(o[:, 128:256], m2_S[:, 0, hc:hc + M2P], m2C[:, j, 0:128], start=False, stop=True)
                        pe.matmul(o[:, 256:T], m2_x[0:16, 2, hc:hc + M2P], m2P2[:, j, :], start=True, stop=False)
                        mm = pe.matmul(o[:, 256:T], m2_S[:, 1, hc:hc + M2P], m2C[:, j, 128:144], start=False, stop=True)
                    mm.then_inc(ev("m2_y"), 1)

            def hg_turn(h):
                b = h % 2
                pe.wait_ge(ev("hg_staged"), h + 1)
                if h:
                    pe.wait_ge(ev("hg_head"), h)
                else:
                    pe.wait_ge(ev("m2_out"), 8)
                for w, (t0, n) in enumerate(WINDOWS):
                    pe.transpose(ps[0:n, 6, w * P:w * P + P], proj[:, TI + h, t0:t0 + n], ident)
                for w in range(2):
                    mm = pe.transpose(ps[:, 7, w * P:w * P + P], hg_D[:, b, 3, w * P:w * P + P], ident)
                mm.then_inc(ev("hg_turned"), 1)
                keys = [hg_K0[:, b], hg_D[:, b, 0, :], hg_D[:, b, 1, :], hg_D[:, b, 2, :]]
                for l in range(4):
                    q = hg_B[:, b, max(l - 1, 0), :]
                    for w in range(2):
                        s = slice(w * P, w * P + P)
                        pe.matmul(ps[:, 4 + l // 2, (l % 2) * 256 + w * P:(l % 2) * 256 + w * P + P], keys[l][:, s], q[:, s], start=True, stop=True)
                pe.wait_ge(ev("hg_v"), h + 1)
                pe.matmul(ps[0:16, 6, 384:400], hg_K0[:, b, 256:T], hg_B[:, b, 0, 256:T], start=True, stop=True).then_inc(ev("hg_scores"), 1)

            def hg_out(h):
                b = h % 2
                pe.wait_ge(ev("hg_ke"), h + 1)
                for w in range(2):
                    mm = pe.matmul(ps[:, 7, w * P:w * P + P], hg_ke[:, w, :], hg_v[:, w, :], start=True, stop=True)
                mm.then_inc(ev("hg_update"), 1)
                pe.wait_ge(ev("hg_masked"), h + 1)
                pe.matmul(ps[:, 6, 0:128], hg_v[:, 0, :], hg_P[:, 0, :], start=True, stop=True)
                group([(hg_v[:, 1, :], hg_P[:, 1, :]), (hg_S[:, 0, :], hg_B[:, b, 3, 128:256])], ps[:, 6, 128:256])
                pe.matmul(ps[:, 6, 256:T], hg_v[0:16, 2, :], hg_P2[0:16, :], start=True, stop=False)
                pe.matmul(ps[:, 6, 256:T], hg_S[:, 1, :], hg_B[:, b, 3, 256:T], start=False, stop=True).then_inc(ev("hg_out"), 1)

            def hg_mean(h):
                pe.wait_ge(ev("hg_squared"), h + 1)
                pe.matmul(ps[:, 7, 0:T], ones1[:], hg_sq, start=True, stop=True).then_inc(ev("hg_mean"), 1)

            def hgrn(j):
                h = (j - 32) // 3
                if j >= 32 and h < HEADS:
                    (hg_turn, hg_out, hg_mean)[(j - 32) % 3](h)

            for j in range(NPROJ):
                n, m = divmod(j, 4)
                if j == 12:
                    pe.wait_ge(ev("small_loaded"), 16 * 8)
                    o = open_tile("dt")
                    done(group([(wsm[:, 0, k, :], uT[:, k, :]) for k in range(KT)], o[0:16, 0:T]))
                if j == 16:
                    m2_turn_rows()
                if j in (17, 24):
                    m2_turn((17, 24).index(j))
                if j in (18, 25):
                    m2_states((18, 25).index(j))
                if j in (21, 23, 28, 30):
                    m2_heads((21, 23, 28, 30).index(j))
                if j in (19, 21, 26, 28):
                    m2_spread((19, 21, 26, 28).index(j))
                hgrn(j)
                if j == 50:
                    norm_sum("mz0", T, lambda k: proj[:, TX + k, :], ones4, 4)
                if m == 2 and n:
                    turn_mod(n - 1)
                o = open_tile(f"p{j}")
                if m == 0:
                    weights(u_in[n])
                w = slot(u_in[n]).rearrange("p (k c) -> p k c", k=KT)
                for k in range(KT):
                    if j == 0:
                        pe.wait_ge(ev("u_tiles"), k + 1)
                    mm = pe.matmul(o[:, 0:T], w[:, k, m * P:m * P + P], uT[:, k, :], start=k == 0, stop=k == KT - 1)
                done(mm)
                if m == 3:
                    used()
                    if n < 12:
                        ada(n)
            if stop <= 2:
                return
            hgrn(52)
            norm_sum("mz1", T, lambda k: proj[:, TX + 4 + k, :], ones4, 4)
            for half in range(2):
                for k in range(KT):
                    cb, m = divmod(k, 4)
                    if half == 0 and k:
                        hgrn(52 + k)
                    if half == 1 and k == 0:
                        pe.wait_ge(ev("hg_head"), HEADS)
                    o = open_tile(f"o{'ba'[half]}{k}")
                    u = u_out[half][cb]
                    if m == 0:
                        weights(u)
                    w = slot(u).rearrange("p (k c) -> p k c", k=KT)
                    for i in range(KT):
                        if half == 0 and k == 0 and i in (0, 4):
                            pe.wait_ge(ev("m2_normed"), 1 + i // 4)
                        src = proj[:, (TZ if half == 0 else TQ) + i, :]
                        mm = pe.matmul(o[:, 0:T], w[:, i, m * P:m * P + P], src, start=i == 0, stop=i == KT - 1)
                    done(mm)
                    if m == 3:
                        used()
            norm_sum("n2", T, lambda k: uT[:, k, :])
            pe.wait_ge(ev("tiles_freed"), opened[0] - 1)
            pe.nop().then_inc(ev("out_done"), 1)
            if stop <= 5:
                return
            for i in range(FT):
                u = u_up[i // 2]
                if i % 2 == 0:
                    weights(u)
                w = slot(u).rearrange("p (k s c) -> p k s c", k=KT, s=2)
                m = i % 2
                for s in range(2):
                    o = open_tile(f"f{2 * i + s}")
                    for k in range(KT):
                        if i == 0 and s == 0:
                            pe.wait_ge(ev("u_tiles"), KT + k + 1)
                        mm = pe.matmul(o[:, 0:T], w[:, k, s, m * P:m * P + P], uT[:, k, :], start=k == 0, stop=k == KT - 1)
                    done(mm)
                if m == 1:
                    used()
                if 13 <= i <= 16:
                    c = i - 13
                    if c == 0:
                        pe.wait_ge(ev("ctx_loaded"), 32)
                    if c >= 2:
                        pe.wait_ge(ev("ctx_copied"), c - 1)
                    for kk in range(2):
                        for w_ in range(2):
                            mm = pe.transpose(ps[:, 4 + c % 2, kk * L + w_ * P:kk * L + w_ * P + P],
                                              ctok[:, w_, (2 * c + kk) * P:(2 * c + kk) * P + P], ident)
                    mm.then_inc(ev("ctx_turned"), 1)
                if i == 18:
                    pe.wait_ge(ev("ctx_squared"), 1)
                    group([(ones[:], hx[:, k, 0:L]) for k in range(KT)], ps[:, 6, 0:L]).then_inc(ev("ctx_mean"), 1)
            for k in range(KT):
                cb, m = divmod(k, 4)
                o = open_tile(f"d{k}")
                for i, (k0, k1) in enumerate(DK):
                    u = u_dn[cb][i]
                    if m == 0:
                        weights(u)
                    w = slot(u)[:, 0:(k1 - k0) * 512].rearrange("p (k c) -> p k c", c=512)
                    for kk in range(k0, k1):
                        if k == 0:
                            pe.wait_ge(ev("ffn_act"), kk + 1)
                        mm = pe.matmul(o[:, 0:T], w[:, kk - k0, m * P:m * P + P], act_[:, kk, :], start=kk == 0, stop=kk == FT - 1)
                done(mm)
                if m == 3:
                    used(3)
            norm_sum("n3", T, lambda k: uT[:, k, :])
            if stop <= 6:
                return
            norm_sum("n4", L, lambda k: uT[:, k, 0:L])

            def in2(r):
                n, m = divmod(r, 4)
                u = u_in2[n]
                if m == 0:
                    weights(u)
                w = slot(u).rearrange("p (k c) -> p k c", k=KT)
                width = 2 * L if n in (1, 2) else L
                o = open_tile(f"q{r}")
                for k in range(KT):
                    if r == 0:
                        pe.wait_ge(ev("hx_tiles"), k + 1)
                    mm = pe.matmul(o[:, 0:width], w[:, k, m * P:m * P + P], hx[:, k, 0:width], start=k == 0, stop=k == KT - 1)
                done(mm)
                if m == 3:
                    used()

            def rotate(j):
                pe.wait_ge(ev("qk_copied"), j + 1)
                if j >= 2:
                    pe.wait_ge(ev("rot_read"), j - 1)
                src, n = (pq[:, j, :], L) if j < RH else (pk[:, j - RH, :], 2 * L)
                pe.matmul(ps[:, 4 + j % 2, 0:n], cs("rot"), src, start=True, stop=True).then_inc(ev("rot_done"), 1)

            def turn_v(h):
                pe.wait_ge(ev("v_copied"), h + 1)
                if h >= 2:
                    pe.wait_ge(ev("v_turn_copied"), h - 1)
                for t in range(4):
                    mm = pe.transpose(ps[:, 6 + h % 2, t * P:t * P + P], pv[:, h, t * P:t * P + P], ident)
                mm.then_inc(ev("v_turned"), 1)

            def ret_scores(h):
                pe.wait_ge(ev("rotated"), RH + h + 1)
                pe.wait_ge(ev("rot_read"), 2 * RH)
                if h:
                    pe.wait_ge(ev("ret_p"), h)
                for t in range(4):
                    mm = pe.matmul(ps[:, 4 + t // 2, (t % 2) * L:(t % 2) * L + L], pk[:, h, t * P:t * P + P], pq[:, h, :], start=True, stop=True)
                mm.then_inc(ev("ret_s"), 1)

            def ret_out(h):
                pe.wait_ge(ev("ret_p"), h + 1)
                pe.wait_ge(ev("v_turn_copied"), RH)
                if h >= 2:
                    pe.wait_ge(ev("ret_y"), h - 1)
                group([(vtok[:, h, t, :], rP_[:, h % 2][:, t, :]) for t in range(4)], ps[:, 6 + h % 2, 0:L]).then_inc(ev("ret_o"), 1)

            def ret_mean(h, which):
                pe.wait_ge(ev("ret_y" if which == 0 else "ret_sq"), h + 1)
                if h or which:
                    pe.wait_ge(ev("ret_mean_read"), 2 * h + which)
                src = ry[:, h, :] if which == 0 else rr[:, 1, 0:L]
                pe.matmul(ps[:, 3, 0:L], ones1[:], src, start=True, stop=True).then_inc(ev("ret_mean"), 1)

            for r in range(28):
                in2(r)
                if 6 <= r < 14:
                    rotate(r - 6)
                if r in (13, 14, 15, 16):
                    turn_v(r - 13)
                if r in (15, 18, 21, 24):
                    ret_scores((r - 15) // 3)
                if r in (16, 19, 22, 25):
                    ret_out((r - 16) // 3)
                if r in (17, 20, 23, 26):
                    ret_mean((r - 17) // 3, 0)
                if r in (18, 21, 24, 27):
                    ret_mean((r - 18) // 3, 1)
            if stop <= 7:
                return
            for k in range(KT):
                cb, m = divmod(k, 4)
                if k == 0:
                    pe.wait_ge(ev("mix2_ready"), 1)
                o = open_tile(f"w{k}")
                if m == 0:
                    weights(u_out2[cb])
                w = slot(u_out2[cb]).rearrange("p (k c) -> p k c", k=KT)
                done(group([(w[:, i, m * P:m * P + P], mixed[:, i, :]) for i in range(KT)], o[:, 0:L]))
                if m == 3:
                    used()
            norm_sum("n5", L, lambda k: uT[:, k, 0:L])
            norm_sum("n6", L, lambda k: uT[:, k, 0:L])
            pe.wait_ge(ev("ret_mean_read"), 2 * RH)
            for w in range(2):
                for k in range(KT):
                    if w == 0:
                        pe.wait_ge(ev("h2_tiles"), k + 1)
                    mm = pe.matmul(ps[:, 3, w * 16:w * 16 + 16], h2[:, k, w * P:w * P + P], wsm[:, 1, k, :], start=k == 0, stop=k == KT - 1)
            mm.then_inc(ev("logits"), 1)
            for w in range(2):
                for k in range(KT):
                    mm = pe.transpose(ps[:, 4 + 2 * w + k // 4, (k % 4) * P:(k % 4) * P + P], h2[:, k, w * P:w * P + P], ident)
            mm.then_inc(ev("h2_turned"), 1)
            pe.wait_ge(ev("aff_ready"), 1)
            for w in range(2):
                mm = pe.transpose(ps[0:16, 3, 128 + w * P:128 + w * P + P], aff[:, w, :], ident)
            mm.then_inc(ev("aff_turned"), 1)
            pe.wait_ge(ev("rank_ready"), 1)
            for w in range(2):
                mm = pe.transpose(ps[:, 3, w * 16:w * 16 + 16], rtk[0:16, 3, w * P:w * P + P], ident[0:16, 0:16])
            mm.then_inc(ev("rank_turned"), 1)
            if stop <= 8:
                return
            zeros = uT[:].rearrange("p a b -> p (a b)")[:, 0:512]
            pe.wait_ge(ev("sel_ready"), 1)
            for b in range(4):
                pe.matmul(ps[:, 4 + b, :], ident, zeros, start=True, stop=False, skip_group_check=True)
            with pe.Fori(0, NE) as e:
                pe.wait_ge(ev("sg4_ready"), e + 1)
                for k in range(KT):
                    group([(h2tok[:, w, k * P:k * P + P], sel[:, w, e, :]) for w in range(2)], ps[:, 3, k * CAP:k * CAP + CAP])
                for w in range(2):
                    mm = pe.transpose(ps[:, 3, 256 + w * P:256 + w * P + P], sg4[:, w].rearrange("p j s -> p (j s)"), ident)
                mm.then_inc(ev("gathered"), 1)
                pe.wait_ge(ev("xs_ready"), e + 1)
                for half in range(2):
                    for i in range(4):
                        s = (U0 + 4 * half + i) % RING
                        pe.wait_ge(ev(f"slot{s}_loaded"), e * 32 + (slot_count[s] + 16 * (1 + (4 * half + i) // RING)))
                        w = ring[:, s, :].rearrange("p (k c) -> p k c", k=2)
                        for k in range(2):
                            for j in range(4):
                                kt = 2 * i + k
                                mm = pe.matmul(ps[32 * j:32 * j + 32, half, :], xs[:, kt, :], w[:, k, 512 * j:512 * j + 512],
                                               start=kt == 0, stop=kt == KT - 1)
                        mm.then_inc(ev("units_used"), 1)
                pe.wait_ge(ev("hidden"), e + 1)
                for b in range(4):
                    mm = pe.transpose(ps[:, 2, b * P:b * P + P], he[:, b * P:b * P + P], ident)
                mm.then_inc(ev("hidden_turned"), 1)
                pe.wait_ge(ev("heT_ready"), e + 1)
                for i in range(4):
                    s = (U0 + 8 + i) % RING
                    pe.wait_ge(ev(f"slot{s}_loaded"), e * 32 + (slot_count[s] + 16 * (1 + (8 + i) // RING)))
                    w = ring[:, s, :].rearrange("p (j c) -> p j c", j=4)
                    for half in range(2):
                        for j in range(4):
                            mm = pe.matmul(ps[32 * j:32 * j + 32, half, :], heT[:, i, 32 * j:32 * j + 32], w[:, j, 512 * half:512 * half + 512],
                                           start=i == 0, stop=i == 3)
                    mm.then_inc(ev("units_used"), 1)
                pe.wait_ge(ev("y_ready"), e + 1)
                for k in range(KT):
                    mm = pe.matmul(ps[:, 4 + k // 2, (k % 2) * L:(k % 2) * L + L], ye[:, k * P:k * P + P], Gt, start=False, stop=False, skip_group_check=True)
                mm.then_inc(ev("scattered"), 1)
            for b in range(4):
                mm = pe.matmul(ps[:, 4 + b, :], ident, zeros, start=False, stop=True, skip_group_check=True)
                mm.then_inc(ev("experts_done"), 1)
            pe.wait_ge(ev("sq7"), 2)
            group([(ones[:], mixed[:, k, :]) for k in range(KT)], ps[:, 0, 0:L]).then_inc(ev("mean7"), 1)
            for w in range(2):
                for k in range(KT):
                    if w == 0:
                        pe.wait_ge(ev("y_final"), k + 1)
                    mm = pe.transpose(ps[:, 4 + 2 * w + k // 4, (k % 4) * P:(k % 4) * P + P], hT[:, k, w * P:w * P + P], ident)
                mm.then_inc(ev("y_turned"), 1)

        @block.scalar
        def _(act):
            st = Steps(act, ev("act_steps"))

            def evict(name, dst, n, fn, rows=P, **kw):
                act.wait_ge(ev("tiles_done"), TN[name] + 1)
                act.activation(dst, bank_of(name)[0:rows, 0:n], fn, **kw).then_inc(ev("tiles_freed"), 1)

            def root(name, n):
                act.wait_ge(ev("tiles_done"), TN[name] + 1)
                act.activation(bc[:, 0, 0:n], bank_of(name)[:, 0:n], ACT.Sqrt, bias=eps[:]).then_inc(ev("tiles_freed"), 1)
                act.wait_ge(ev("tiles_freed"), TN[name] + 1)
                act.nop().then_inc(ev("root"), 1)

            def load(dst, src, sem, **kw):
                act.dma_start(dst, src, **kw).then_inc(ev(sem), 16)

            act.wait_ge(ev("rows_cleared"), 1)

            def rows(name, src):
                b, r, n = PAR[name]
                n = src.shape[0]
                load(prow[r:r + n, b, :], src, "par_loaded")

            def r1(w):
                return w.rearrange("o (k p) -> (o k) p", p=P)

            rows("norm1", r1(a["norm1_w"]))
            rows("lb0", r1(a["hg_lb_logits"][0:1]))
            rows("lb1", r1(a["hg_lb_logits"][1:2]))
            rows("hgn", r1(a["hg_norm_w"]))
            rows("m2cw", r1(a["m2_conv_w"][0]))
            rows("m2cb", r1(a["m2_conv_b"]))
            rows("m2n", r1(a["m2_norm_w"]))
            rows("norm2", r1(a["norm2_w"]))
            rows("fin", a["final_norm_w"].rearrange("(k p) -> k p", p=P))
            rows("ffw01", r1(a["ffn_conv_w"][0, 0:2]))
            rows("prem", r1(a["pre_mix_g_2"]))
            rows("postm", r1(a["post_mix_g_2"]))
            rows("pref", r1(a["pre_ffn_g_2"]))
            rows("postf", r1(a["post_ffn_g_2"]))
            rows("ffw2", r1(a["ffn_conv_w"][0, 2:3]))
            rows("ffb", r1(a["ffn_conv_b"]))
            rows("cw2", r1(a["conv_w_2"][0]))
            rows("cb2", r1(a["conv_b_2"]))
            rows("retn", r1(a["ret_norm_g_2"]))
            rows("c", r1(a["c_2"]))
            rows("cctx", a["c_ctx_2"].rearrange("(k p) -> k p", p=P))
            rows("bada", r1(a["b_ada_2"]))
            load(chan[:, 0, 0:1], a["m2_dt_bias"].rearrange("o h -> h o"), "small_loaded")
            load(chan[:, 0, 1:2], a["m2_a_log"].rearrange("o h -> h o"), "small_loaded")
            for half in range(2):
                load(bcast8[64 * half:64 * half + 64, 0:8],
                     a["m2_d"].rearrange("o (k two) -> o two k", two=2)[:, half, :].to_broadcast([64, 8]), "small_loaded",
                     allow_slow_non_contiguous=True)
            load(bcast8[:, 8:24], a["b_router_2"].to_broadcast([P, 16]), "small_loaded")
            load(bcast8[:, 24:32], a["ret_decay_logit_2"].rearrange("o d h -> o (d h)").to_broadcast([P, 8]), "small_loaded")
            load(wsm[:, 0], kview(w_in)[:, :, 6656:6672], "small_loaded")
            load(wsm[:, 1], kview(a["w_router_2"][0]), "small_loaded")

            for k in range(KT):
                act.wait_ge(ev("stream_tiles"), k + 1)
                act.activation(uT[:, k, :], hT[:, k, :], ACT.Square).then_inc(ev("squares"), 1)
            act.wait_ge(ev("par_ready"), 1)
            act.wait_ge(ev("cond_cleared"), 1)
            st(act.activation(cond[:, :, 0], pc("c", 0, 8), ACT.Silu))
            st.link(act.activation(cond[:, :, 1], pc("cctx", 0, 8), ACT.Silu))
            act.nop().then_inc(ev("cond_ready"), 1)
            act.wait_ge(ev("lb_shift"), 1)
            act.activation(small[:, 0:16], small[:, 0:16], ACT.Exp).then_inc(ev("lb_exp"), 1)
            root("n1", T)
            if stop <= 1:
                return

            def conv_silu(t):
                act.wait_ge(ev("m2_conv_sum"), t + 1)
                act.activation(proj[:, TX + t, :], m2_t[:, t % 2, :], ACT.Silu).then_inc(ev("m2_conv"), 1)

            def dt_first():
                act.wait_ge(ev("small_loaded"), 16 * 8)
                evict("dt", ch(1), T, ACT.Identity, rows=16, bias=chan[:, 0, 0:1])
                st.link(act.activation(chan[:, 0, 2:3], chan[:, 0, 1:2], ACT.Exp))
                act.wait_ge(ev("tiles_freed"), TN["dt"] + 1)
                act.nop().then_inc(ev("dt_in"), 1)
                act.wait_ge(ev("dt_abs"), 1)
                act.activation(ch(6), ch(5), ACT.Exp, scale=-1.0).then_inc(ev("dt_exp"), 1)
                act.wait_ge(ev("dt_one"), 1)
                act.activation(ch(8), ch(7), ACT.Ln).then_inc(ev("dt_log"), 1)

            def dt_end():
                act.wait_ge(ev("m2_end"), 1)
                act.activation(ch(3)[:, 0:256], ch(4)[:, 0:256], ACT.Exp).then_inc(ev("m2_end_exp"), 1)

            def m2_exp(q):
                act.wait_ge(ev("m2_a"), q + 1)
                if q:
                    act.wait_ge(ev("m2_y"), 2 * q)
                act.activation(m2C[:, :, 0:128], ps[:, 5, :].rearrange("p (h t) -> p h t", h=4), ACT.Exp).then_inc(ev("m2_ea"), 1)
                act.activation(m2C[:, :, 128:144], ps[:, 7, 0:64].rearrange("p (h t) -> p h t", h=4), ACT.Exp).then_inc(ev("m2_ea"), 1)
                for w, buf in enumerate((m2P0, m2P1, m2P2)):
                    act.wait_ge(ev("m2_seg"), 3 * q + w + 1)
                    act.activation(buf, buf, ACT.Exp).then_inc(ev("m2_seg_exp"), 1)

            def hg_log(h):
                act.wait_ge(ev("hg_f"), h + 1)
                act.activation(hg_lf, hg_f, ACT.Ln).then_inc(ev("hg_log"), 1)

            def hg_exps(h):
                b = h % 2
                act.wait_ge(ev("hg_b"), h + 1)
                st(act.activation(hg_K0[:, b], hg_B[:, b, 0, :], ACT.Exp, scale=-1.0))
                st.link(act.activation(hg_D[:, b], hg_D[:, b], ACT.Exp))
                act.activation(hg_B[:, b], hg_B[:, b], ACT.Exp).then_inc(ev("hg_exp"), 1)

            def hg_keys(h):
                act.wait_ge(ev("hg_turned"), h + 1)
                act.activation(hg_ke, ps[:, 7, 0:256].rearrange("p (w c) -> p w c", w=2), ACT.Copy).then_inc(ev("hg_ke"), 1)

            def hgrn(j):
                h = (j - 32) // 3
                if j < 32 or h >= HEADS:
                    return
                if (j - 32) % 3 == 0:
                    if h + 1 < HEADS:
                        hg_log(h + 1)
                    hg_keys(h)
                    if h + 1 < HEADS:
                        hg_exps(h + 1)
                if (j - 32) % 3 == 1:
                    act.wait_ge(ev("hg_out"), h + 1)
                    act.activation(hg_sq, ps[:, 6, 0:T], ACT.Square).then_inc(ev("hg_squared"), 1)
                if (j - 32) % 3 == 2:
                    act.wait_ge(ev("hg_mean"), h + 1)
                    act.activation(hg_lf, ps[:, 7, 0:T], ACT.Sqrt, bias=eps[:]).then_inc(ev("hg_root"), 1)

            def gate_squares(g):
                act.wait_ge(ev("m2_gated"), g + 1)
                for k in range(4):
                    act.activation(proj[:, TX + 4 * g + k, :], proj[:, TZ + 4 * g + k, :], ACT.Square).then_inc(ev("squares"), 1)

            for j in range(NPROJ):
                n, m = divmod(j, 4)
                if 2 <= j <= 13:
                    conv_silu(j - 2)
                if j == 12:
                    dt_first()
                if j == 14:
                    dt_end()
                if j in (19, 21, 26, 28):
                    m2_exp((19, 21, 26, 28).index(j))
                if j == 30:
                    hg_log(0)
                    hg_exps(0)
                hgrn(j)
                if j == 49:
                    gate_squares(0)
                if j == 50:
                    root("mz0", T)
                unit_ = ORDER[n]
                fn = {0: ACT.Silu, 1: ACT.Sigmoid, 2: ACT.Copy, 3: ACT.Silu, 4: ACT.Silu}.get(unit_ // 2, ACT.Copy)
                evict(f"p{j}", proj[:, 4 * unit_ + m, :], T, fn)
                act.wait_ge(ev("tiles_freed"), TN[f"p{j}"] + 1)
                act.nop().then_inc(ev("proj_tiles"), 1)
            if stop <= 2:
                return
            hgrn(52)
            gate_squares(1)
            root("mz1", T)
            for j in range(53, 56):
                hgrn(j)
            for k in range(KT):
                act.wait_ge(ev("stream_tiles"), 2 * KT + k + 1)
                act.activation(uT[:, k, :], hT[:, k, :], ACT.Square).then_inc(ev("squares"), 1)
            root("n2", T)
            if stop <= 5:
                return
            for i in range(FT):
                for s in range(2):
                    m = s * FT + i
                    act.wait_ge(ev("tiles_done"), TN[f"f{2 * i + s}"] + 1)
                    if i >= 2:
                        act.wait_ge(ev("ffn_act"), i - 1)
                    act.activation(fc[:, i % 2, s, :], bank_of(f"f{2 * i + s}")[:, 0:T], ACT.Identity, scale=pc("ffw2", m),
                                   bias=pc("ffb", m)).then_inc(ev("ffn_tap"), 1)
                act.wait_ge(ev("ffn_conv"), 2 * i + 1)
                act.activation(fc[:, i % 2, 0, :], fc[:, i % 2, 0, :], ACT.Silu).then_inc(ev("ffn_silu"), 1)
                if i == 17:
                    act.wait_ge(ev("ctx_copied"), 4)
                    act.activation(hx[:, :, 0:L], hx[:, :, L:2 * L], ACT.Square).then_inc(ev("ctx_squared"), 1)
                if i == 18:
                    act.wait_ge(ev("ctx_mean"), 1)
                    act.activation(bc[:, 0, L:2 * L], ps[:, 6, 0:L], ACT.Sqrt, bias=eps[:]).then_inc(ev("ctx_root"), 1)
                if i == 19:
                    act.wait_ge(ev("lg_abs"), 1)
                    act.activation(small[:, 40:48], small[:, 32:40], ACT.Exp, scale=-1.0).then_inc(ev("lg_exp"), 1)
                    act.wait_ge(ev("lg_one"), 1)
                    act.activation(small[:, 56:64], small[:, 48:56], ACT.Ln).then_inc(ev("lg_log"), 1)
            for k in range(KT):
                act.wait_ge(ev("stream_tiles"), 3 * KT + k + 1)
                act.activation(uT[:, k, :], hT[:, k, :], ACT.Square).then_inc(ev("squares"), 1)
            root("n3", T)
            if stop <= 6:
                return
            for k in range(KT):
                act.wait_ge(ev("x2_tiles"), k + 1)
                act.activation(uT[:, k, 0:L], hT[:, k, 0:L], ACT.Square).then_inc(ev("squares"), 1)
            root("n4", L)

            def ret_powers(h):
                act.wait_ge(ev("ret_arg"), h + 1)
                st(act.activation(rD[:, h % 2, 0:2, :], rD[:, h % 2, 0:2, :], ACT.Exp))
                st(act.activation(rD[:, h % 2, 2:4, :], dist[:, 4:6, :], ACT.Exp, scale=small[:, 80 + h:81 + h]))
                st.link(act.activation(rr[:, 0, :], dist[:, 6:8, :].rearrange("p a b -> p (a b)"), ACT.Exp, scale=small[:, 84 + h:85 + h]))
                act.nop().then_inc(ev("ret_pow"), 1)

            def ret_square(h):
                act.wait_ge(ev("ret_centred"), h + 1)
                act.activation(rr[:, 1, 0:L], ry[:, h, :], ACT.Square).then_inc(ev("ret_sq"), 1)

            def ret_root(h):
                act.wait_ge(ev("ret_mean"), 2 * h + 2)
                if h:
                    act.wait_ge(ev("ret_normed"), h)
                act.activation(bc[:, 0, 0:L], ps[:, 3, 0:L], ACT.Sqrt, bias=eps[:]).then_inc(ev("ret_mean_read"), 1)
                act.wait_ge(ev("ret_mean_read"), 2 * h + 2)
                act.nop().then_inc(ev("ret_root"), 1)

            for r in range(28):
                n, m = divmod(r, 4)
                width = 2 * L if n in (1, 2) else L
                dst = (pq, pk, pv, pg, pcg, pu, pb)[n][:, m, :]
                evict(f"q{r}", dst, width, ACT.Silu if n == 3 else ACT.Copy)
                act.wait_ge(ev("tiles_freed"), TN[f"q{r}"] + 1)
                act.nop().then_inc(ev("qk_copied" if n < 2 else "v_copied" if n == 2 else "cgx_copied"), 1)
                if r == 13:
                    ret_powers(0)
                if r in (16, 19, 22):
                    ret_powers((r - 16) // 3 + 1)
                if r in (17, 20, 23, 26):
                    ret_square((r - 17) // 3)
                if r in (18, 21, 24, 27):
                    ret_root((r - 18) // 3)
            if stop <= 7:
                return
            for k in range(KT):
                act.wait_ge(ev("mx_tiles"), k + 1)
                act.activation(uT[:, k, 0:L], mx[:, k, :], ACT.Square).then_inc(ev("squares"), 1)
            root("n5", L)
            for k in range(KT):
                act.wait_ge(ev("x3_tiles"), k + 1)
                act.activation(uT[:, k, 0:L], hT[:, k, 0:L], ACT.Square).then_inc(ev("squares"), 1)
            root("n6", L)
            act.wait_ge(ev("soft_shift"), 1)
            act.activation(aff[:], aff[:], ACT.Exp).then_inc(ev("soft_exp"), 1)
            act.wait_ge(ev("h2_turned"), 1)
            for i in range(4):
                act.activation(h2tok[:, i // 2, (i % 2) * 512:(i % 2) * 512 + 512], ps[:, 4 + i, :], ACT.Copy).then_inc(ev("h2tok_copied"), 1)
            if stop <= 8:
                return
            with act.Fori(0, NE) as e:
                act.wait_ge(ev("units_used"), e * 12 + (U0 + 4))
                act.activation(sa, ps[:, 0, :], ACT.Silu).then_inc(ev("gate_silu"), 1)
                act.wait_ge(ev("hidden_turned"), e + 1)
                act.activation(heT[:], ps[:, 2, :].rearrange("p (b c) -> p b c", b=4), ACT.Copy).then_inc(ev("heT_ready"), 1)
                act.wait_ge(ev("units_used"), e * 12 + (U0 + 12))
                act.activation(ye[:, 0:512], ps[:, 0, :], ACT.Copy).then_inc(ev("y_half"), 1)
            for b in range(2):
                act.wait_ge(ev("mx7"), 2 * b + 2)
                act.activation(mixed[:, 4 * b:4 * b + 4, :], mx[:, 4 * b:4 * b + 4, :], ACT.Square).then_inc(ev("sq7"), 1)
            act.wait_ge(ev("mean7"), 1)
            act.activation(bc[:, 0, 0:L], ps[:, 0, 0:L], ACT.Sqrt, bias=eps[:]).then_inc(ev("root7"), 1)
            act.wait_ge(ev("y_turned"), 1)
            act.activation(otok[:, 0, 512:1024], ps[:, 5, :], ACT.Copy).then_inc(ev("out_half"), 1)
            act.wait_ge(ev("y_turned"), 2)
            act.activation(otok[:, 1, 512:1024], ps[:, 7, :], ACT.Copy).then_inc(ev("out_half"), 1)

        @block.vector
        def _(dve):
            st = Steps(dve, ev("dve_steps"))
            tt, ts, stt = dve.tensor_tensor, dve.tensor_scalar, dve.scalar_tensor_tensor
            roots = [0]

            def inverse_root(n):
                roots[0] += 1
                dve.wait_ge(ev("root"), roots[0])
                st.link(dve.reciprocal(bc[:, 1, 0:n], bc[:, 0, 0:n]))

            dve.memset(prow, 0.0).then_inc(ev("rows_cleared"), 1)
            st(dve.memset(ones[:], 1.0 / D))
            st(dve.memset(ones4[:], 1.0 / 512))
            st(dve.memset(ones1[:], 1.0 / P))
            st(dve.memset(eps[:], 1e-6))
            st.wait()
            dve.memset(cond[:], 0.0).then_inc(ev("cond_cleared"), 1)
            for k in range(KT):
                dve.wait_ge(ev("tiles_done"), k + 1)
                dve.tensor_copy(hT[:, k, :], bank_of(f"x{k}")[:, 0:T]).then_inc(ev("tiles_freed"), 1)
                dve.wait_ge(ev("tiles_freed"), k + 1)
                dve.nop().then_inc(ev("stream_tiles"), 1)
            dve.wait_ge(ev("par_turned"), 1)
            dve.tensor_copy(par[:], ps[:, 3, :]).then_inc(ev("par_ready"), 1)
            dve.wait_ge(ev("par_ready"), 1)
            st.link(tt(small[:, 16:24], pc("lb0", 0, 8), pc("lb1", 0, 8), ALU.max))
            st(tt(small[:, 0:8], pc("lb0", 0, 8), small[:, 16:24], ALU.subtract))
            st.link(tt(small[:, 8:16], pc("lb1", 0, 8), small[:, 16:24], ALU.subtract))
            dve.nop().then_inc(ev("lb_shift"), 1)
            dve.wait_ge(ev("lb_exp"), 1)
            st.link(tt(small[:, 16:24], small[:, 0:8], small[:, 8:16], ALU.add))
            st.link(dve.reciprocal(small[:, 24:32], small[:, 16:24]))
            lb, oml = small[:, 96:104], small[:, 104:112]
            st.link(tt(lb, small[:, 0:8], small[:, 24:32], ALU.mult))
            st.link(ts(oml, lb, -1.0, 1.0, ALU.mult, ALU.add))

            def normed(name):
                inverse_root(T)
                for k in range(KT):
                    stt(uT[:, k, :], hT[:, k, :], pc(name, k), bc[:, 1, 0:T], ALU.mult, ALU.mult).then_inc(ev("u_tiles"), 1)

            normed("norm1")
            if stop <= 1:
                dve.wait_ge(ev("u_tiles"), 8)
                return

            def mod_row(n):
                dve.wait_ge(ev("units_used"), 2 * n + 2)
                dve.tensor_copy(mrow, ps[:, 3, :]).then_inc(ev("mod_row"), 1)

            def mod_add(n):
                dve.wait_ge(ev("mod_turned"), n + 1)
                tt(mod[:, 4 * n:4 * n + 4, :], ps[:, 3, 0:8].rearrange("p (b c) -> p b c", c=2),
                   pc("bada", 4 * n, 4).unsqueeze(2).to_broadcast([P, 4, 2]), ALU.add).then_inc(ev("mod_done"), 1)

            def conv(t):
                dve.wait_ge(ev("proj_tiles"), t + 1)
                x, o = proj[:, TX + t, :], m2_t[:, t % 2, :]
                if t == 0:
                    dve.wait_ge(ev("tiles_done"), TN["n1"] + 1)
                if t >= 2:
                    dve.wait_ge(ev("m2_conv"), t - 1)
                st.link(ts(o, x, pc("m2cw", 36 + t), pc("m2cb", t), ALU.mult, ALU.add))
                for s in (1, 2, 3):
                    ins = stt(o[:, s:T], x[:, 0:T - s], pc("m2cw", 12 * (3 - s) + t), o[:, s:T], ALU.mult, ALU.add)
                    if s < 3:
                        st.link(ins)
                ins.then_inc(ev("m2_conv_sum"), 1)

            def log1p_of_exp(u, e, one, lg, tmp, ev_abs, ev_exp, ev_one, ev_log):
                st.link(stt(tmp, u, -1.0, u, ALU.mult, ALU.max))
                dve.nop().then_inc(ev(ev_abs), 1)
                dve.wait_ge(ev(ev_exp), 1)
                st.link(ts(one, e, 1.0, None, ALU.add))
                dve.nop().then_inc(ev(ev_one), 1)
                dve.wait_ge(ev(ev_log), 1)
                st.link(tt(lg, lg, e, ALU.mult))
                st.link(ts(tmp, one, -1.0, 1e-30, ALU.add, ALU.max))
                st.link(dve.reciprocal(tmp, tmp))
                st.link(tt(lg, lg, tmp, ALU.mult))
                st.link(ts(tmp, one, 1.0, None, ALU.is_equal))
                st.link(tt(tmp, tmp, e, ALU.mult))
                st.link(tt(lg, lg, tmp, ALU.add))

            def dt_rows():
                dve.wait_ge(ev("dt_in"), 1)
                log1p_of_exp(ch(1), ch(6), ch(7), ch(8), ch(5), "dt_abs", "dt_exp", "dt_one", "dt_log")
                st.link(stt(ch(1), ch(1), 0.0, ch(8), ALU.max, ALU.add))
                st.link(ts(ch(4), ch(1), chan[:, 0, 2:3], -1.0, ALU.mult, ALU.mult))
                st.link(dve.tensor_tensor_scan(ch(0), cs("reset", 16)[:, 3 * T:4 * T], ch(4), 0.0, ALU.mult, ALU.add))
                for w in range(2):
                    s = slice(w * P, w * P + P)
                    st(tt(ch(4)[:, s], ch(0)[:, w * P + 127:w * P + 128].to_broadcast([16, P]), ch(0)[:, s], ALU.subtract))
                st(dve.memset(ch(3)[:, 256:T], 1.0))
                st.wait()
                dve.nop().then_inc(ev("m2_end"), 1)
                dve.wait_ge(ev("m2_end_exp"), 1)
                dve.nop().then_inc(ev("m2_rows"), 1)

            def m2_tokens():
                dve.wait_ge(ev("m2_rows_turned"), 1)
                pr = ps[:, 4, 0:144].rearrange("p (w i h) -> p w i h", w=3, i=3)
                st(dve.tensor_copy(tkq[:, 0:2], pr[:, 0:2]))
                st(dve.tensor_copy(tkq[0:16, 2], pr[0:16, 2]))
                st.wait()
                dve.nop().then_inc(ev("m2_tk"), 1)

            def m2_stage(g):
                dve.wait_ge(ev("m2_turned"), g + 1)
                hs = slice(8 * g, 8 * g + 8)
                for w, (t0, n) in enumerate(WINDOWS):
                    st(tt(m2_x[0:n, w, :].rearrange("p (h c) -> p h c", h=8), ps[0:n, 4 + w, :].rearrange("p (h c) -> p h c", h=8),
                          tkq[0:n, w, 0, hs].unsqueeze(2).to_broadcast([n, 8, 64]), ALU.mult))
                st(dve.tensor_copy(m2_b, ps[:, 7, 0:256].rearrange("p (w c) -> p w c", w=2)))
                st.wait()
                for w in range(2):
                    st(tt(m2_xe[:, w, :].rearrange("p (h c) -> p h c", h=8), m2_x[:, w, :].rearrange("p (h c) -> p h c", h=8),
                          tkq[:, w, 2, hs].unsqueeze(2).to_broadcast([P, 8, 64]), ALU.mult))
                st.wait()
                dve.nop().then_inc(ev("m2_staged"), 1)

            def m2_masks(g):
                dve.wait_ge(ev("m2_update"), g + 1)
                st(tt(m2_cb, ps[:, 4, 0:256].rearrange("p (w c) -> p w c", w=2),
                      cs("causal").unsqueeze(1).to_broadcast([P, 2, P]), ALU.mult))
                st(tt(m2_cb2[0:16], ps[0:16, 5, 0:16], cs("causal", 16)[:, 0:16], ALU.mult))
                for w in range(2):
                    st(dve.tensor_copy(m2_S[:, w, :], ps[:, 6 + w, :]))
                st.wait()
                dve.nop().then_inc(ev("m2_group"), 1)

            def m2_scores(q):
                g = q // 2
                dve.wait_ge(ev("m2_a"), q + 1)
                if q:
                    dve.wait_ge(ev("m2_y"), 2 * q)
                bufs = ((m2P0, P), (m2P1, P), (m2P2, 16))
                for w, (buf, n) in enumerate(bufs):
                    if w:
                        dve.wait_ge(ev("m2_ea"), 2 * q + w)
                    st.link(tt(buf, ps[0:n, (4, 5, 7)[w], 0:4 * n].rearrange("p (h t) -> p h t", h=4),
                               tkq[0:n, w, 1, 4 * q:4 * q + 4].unsqueeze(2).to_broadcast([n, 4, n]), ALU.subtract))
                    ts(buf, buf, 0.0, None, ALU.min).then_inc(ev("m2_seg"), 1)
                hs = slice(256 * (q % 2), 256 * (q % 2) + 256)
                s0 = m2_S[:, 0, hs].rearrange("p (h c) -> p h c", h=4)
                s1 = m2_S[:, 1, hs].rearrange("p (h c) -> p h c", h=4)
                tmp = m2_seg.rearrange("p (h c) -> p h c", h=4)
                st.link(tt(tmp, s0, m2C[:, :, 127:128].to_broadcast([P, 4, 64]), ALU.mult))
                st.link(tt(s1, s1, tmp, ALU.add))
                st(tt(m2C, m2C, proj[:, TCM + g, 128:T].unsqueeze(1).to_broadcast([P, 4, 144]), ALU.mult))
                for w, (buf, n) in enumerate(bufs):
                    dve.wait_ge(ev("m2_seg_exp"), 3 * q + w + 1)
                    cb = m2_cb[:, w, :] if w < 2 else m2_cb2[0:16]
                    st(tt(buf, buf, cb.unsqueeze(1).to_broadcast([n, 4, n]), ALU.mult))
                st.wait()
                dve.nop().then_inc(ev("m2_pc"), 1)

            def m2_outputs(q):
                for pair in range(2):
                    c = 2 * q + pair
                    dve.wait_ge(ev("m2_y"), c + 1)
                    stt(proj[:, TX + c, :], proj[:, TX + c, :], bcast8[:, c:c + 1], ps[:, 6 + pair, 0:T], ALU.mult, ALU.add).then_inc(ev("m2_out"), 1)

            def m2_gate(g):
                dve.wait_ge(ev("m2_out"), 8)
                dve.wait_ge(ev("proj_tiles"), 48 + 4 * g)
                z = proj[:, TZ + 4 * g:TZ + 4 * g + 4, :]
                tt(z, z, proj[:, TX + 4 * g:TX + 4 * g + 4, :], ALU.mult).then_inc(ev("m2_gated"), 1)

            def m2_norm(g):
                inverse_root(T)
                dve.wait_ge(ev("m2_gated"), g + 1)
                for k in range(4):
                    m = TZ + 4 * g + k
                    st(stt(proj[:, m, :], proj[:, m, :], pc("m2n", 4 * g + k), bc[:, 1, 0:T], ALU.mult, ALU.mult))
                st.wait()
                dve.nop().then_inc(ev("m2_normed"), 1)

            reset = cs("reset").rearrange("p (l t) -> p l t", l=4)
            mask = cs("mask").bitcast(U32).rearrange("p (l r) -> p l r", l=4)

            def hg_cumulate(h):
                b = h % 2
                dve.wait_ge(ev("proj_tiles"), 16 if h < 4 else 32)
                st.link(ts(hg_f, proj[:, h + TF_, :], oml[:, h:h + 1], lb[:, h:h + 1], ALU.mult, ALU.add))
                dve.nop().then_inc(ev("hg_f"), 1)
                st(ts(hg_k, hg_f, -1.0, 1.0, ALU.mult, ALU.add))
                dve.wait_ge(ev("hg_log"), h + 1)
                for l in range(4):
                    st(dve.tensor_tensor_scan(hg_B[:, b, l, :], reset[:, l, :], hg_lf, 0.0, ALU.mult, ALU.add))
                st.wait()
                for l, w in enumerate(LEVELS):
                    B = hg_B[:, b, l, 0:256].rearrange("p (c w) -> p c w", w=w)
                    st(tt(hg_D[:, b, l, :].rearrange("p (c w) -> p c w", w=w),
                          B[:, :, w - 1:w].to_broadcast([P, 256 // w, w]), B, ALU.subtract))
                st.wait()
                dve.nop().then_inc(ev("hg_b"), 1)

            def hg_decay(h):
                b = h % 2
                dve.wait_ge(ev("hg_exp"), h + 1)
                st(dve.tensor_copy(small[:, 120 + b:121 + b], hg_B[:, b, 3, 255:256]))
                st(tt(hg_K0[:, b], hg_K0[:, b], hg_k, ALU.mult))
                st(tt(hg_D[:, b], hg_D[:, b], hg_k[:, 0:256].unsqueeze(1).to_broadcast([P, 4, 256]), ALU.mult))
                st.wait()
                dve.wait_ge(ev("proj_tiles"), 24 if h < 4 else 40)
                st.link(tt(hg_B[:, b], hg_B[:, b], proj[:, h + TQ, :].unsqueeze(1).to_broadcast([P, 4, T]), ALU.mult))
                dve.nop().then_inc(ev("hg_staged"), 1)

            def hg_values(h):
                dve.wait_ge(ev("hg_turned"), h + 1)
                st(dve.tensor_copy(hg_v[:, 0:2, :], ps[:, 6, 0:256].rearrange("p (w c) -> p w c", w=2)))
                st(dve.tensor_copy(hg_v[0:16, 2, :], ps[0:16, 6, 256:384]))
                st.wait()
                dve.nop().then_inc(ev("hg_v"), 1)

            def hg_mask(h):
                dve.wait_ge(ev("hg_scores"), h + 1)
                for l in range(4):
                    st.link(dve.copy_predicated(hg_P, mask[:, l, :].unsqueeze(1).to_broadcast([P, 2, P]),
                                                ps[:, 4 + l // 2, (l % 2) * 256:(l % 2) * 256 + 256].rearrange("p (w r) -> p w r", w=2)))
                st(dve.copy_predicated(hg_P2[0:16, :], mask[0:16, 0, 0:16], ps[0:16, 6, 384:400]))
                dve.wait_ge(ev("hg_update"), h + 1)
                st.link(dve.tensor_copy(hg_S[:, 0, :], ps[:, 7, 0:128]))
                st.link(stt(hg_S[:, 1, :], hg_S[:, 0, :], small[:, 120 + h % 2:121 + h % 2], ps[:, 7, 128:256], ALU.mult, ALU.add))
                dve.nop().then_inc(ev("hg_masked"), 1)

            def hg_finish(h):
                dve.wait_ge(ev("hg_root"), h + 1)
                dve.wait_ge(ev("proj_tiles"), 28 if h < 4 else 44)
                st.link(dve.reciprocal(hg_f, hg_lf))
                st.link(stt(hg_o, ps[:, 6, 0:T], pc("hgn", h), hg_f, ALU.mult, ALU.mult))
                tt(proj[:, h + TQ, :], hg_o, proj[:, h + TG, :], ALU.mult).then_inc(ev("hg_head"), 1)
                dve.wait_ge(ev("hg_head"), h + 1)

            def hgrn(j):
                h = (j - 32) // 3
                if j < 32 or h >= HEADS:
                    return
                if (j - 32) % 3 == 0:
                    hg_values(h)
                    if h + 1 < HEADS:
                        hg_cumulate(h + 1)
                if (j - 32) % 3 == 1:
                    hg_mask(h)
                    if h + 1 < HEADS:
                        hg_decay(h + 1)
                if (j - 32) % 3 == 2:
                    hg_finish(h)

            for j in range(NPROJ):
                n, m = divmod(j, 4)
                if 1 <= j <= 12:
                    conv(j - 1)
                if m == 0 and n:
                    mod_row(n - 1)
                if m == 3 and n:
                    mod_add(n - 1)
                if j == 12:
                    dt_rows()
                if j == 16:
                    m2_tokens()
                if j in (17, 24):
                    m2_stage((17, 24).index(j))
                if j in (18, 25):
                    m2_masks((18, 25).index(j))
                if j in (21, 23, 28, 30):
                    m2_outputs((21, 23, 28, 30).index(j))
                if j in (19, 21, 26, 28):
                    m2_scores((19, 21, 26, 28).index(j))
                if j == 30:
                    dve.wait_ge(ev("m2_out"), 8)
                    st(dve.memset(hg_P, 0.0))
                    st.link(dve.memset(hg_P2, 0.0))
                    hg_cumulate(0)
                    hg_decay(0)
                hgrn(j)
                if j == 48:
                    m2_gate(0)
                if j == 51:
                    m2_norm(0)
            if stop <= 2:
                return
            hgrn(52)
            m2_gate(1)
            m2_norm(1)

            def add_tile(name, k, n=T):
                dve.wait_ge(ev("tiles_done"), TN[name] + 1)
                if name == "ob0":
                    dve.wait_ge(ev("tiles_freed"), TN[name])
                tt(hT[:, k, 0:n], hT[:, k, 0:n], bank_of(name)[:, 0:n], ALU.add).then_inc(ev("tiles_freed"), 1)
                dve.wait_ge(ev("tiles_freed"), TN[name] + 1)
                dve.nop().then_inc(ev("stream_tiles"), 1)

            for k in range(KT):
                if k:
                    hgrn(52 + k)
                add_tile(f"ob{k}", k)
            for k in range(KT):
                add_tile(f"oa{k}", k)
            normed("norm2")
            if stop <= 5:
                return
            gain = small[:, 128:144].rearrange("p (k c) -> p k c", c=2)
            for i in range(FT):
                for s in range(2):
                    m = s * FT + i
                    dve.wait_ge(ev("ffn_tap"), 2 * i + s + 1)
                    o, x = fc[:, i % 2, s, :], bank_of(f"f{2 * i + s}")
                    st.link(stt(o[:, 1:T], x[:, 0:T - 1], pc("ffw01", 44 + m), o[:, 1:T], ALU.mult, ALU.add))
                    st.link(stt(o[:, 2:T], x[:, 0:T - 2], pc("ffw01", m), o[:, 2:T], ALU.mult, ALU.add))
                    dve.nop().then_inc(ev("tiles_freed"), 1)
                    dve.nop().then_inc(ev("ffn_conv"), 1)
                dve.wait_ge(ev("ffn_silu"), i + 1)
                tt(act_[:, i, :], fc[:, i % 2, 0, :], fc[:, i % 2, 1, :], ALU.mult).then_inc(ev("ffn_act"), 1)
                if 14 <= i <= 17:
                    c = i - 14
                    dve.wait_ge(ev("ctx_turned"), c + 1)
                    dve.tensor_copy(hx[:, 2 * c:2 * c + 2, L:2 * L], ps[:, 4 + c % 2, :].rearrange("p (k c) -> p k c", k=2)).then_inc(ev("ctx_copied"), 1)
                if i == 18:
                    for c in range(2):
                        st(stt(gain[:, :, c], mod[:, 8:16, c], 1.0, pc("prem", 0, 8), ALU.add, ALU.mult))
                if i == 19:
                    lgt = bcast8[:, 24:32]
                    log1p_of_exp(lgt, small[:, 40:48], small[:, 48:56], small[:, 56:64], small[:, 32:40], "lg_abs", "lg_exp", "lg_one", "lg_log")
                    st.link(stt(small[:, 80:88], lgt, 0.0, small[:, 56:64], ALU.min, ALU.subtract))
                if i == 20:
                    dve.wait_ge(ev("ctx_root"), 1)
                    st.link(dve.reciprocal(bc[:, 1, L:2 * L], bc[:, 0, L:2 * L]))
                    for k in range(KT):
                        st(stt(hx[:, k, L:2 * L], hx[:, k, L:2 * L], gain[:, k, 1:2], bc[:, 1, L:2 * L], ALU.mult, ALU.mult))
                    st.wait()
                    st.link(tt(hx[:, :, L:2 * L], hx[:, :, L:2 * L], mod[:, 0:8, 1:2].to_broadcast([P, KT, L]), ALU.add))

            def ret_args(h):
                if h >= 2:
                    dve.wait_ge(ev("ret_p"), h - 1)
                st.link(ts(rD[:, h % 2, 0:2, :], dist[:, 0:2, :], small[:, 80 + h:81 + h], None, ALU.mult))
                st.link(stt(rD[:, h % 2, 0:2, :], dist[:, 2:4, :], small[:, 84 + h:85 + h], rD[:, h % 2, 0:2, :], ALU.mult, ALU.add))
                dve.nop().then_inc(ev("ret_arg"), 1)

            for k in range(KT):
                add_tile(f"d{k}", k)
            inverse_root(T)
            for k in range(KT):
                st.link(stt(hT[:, k, :], hT[:, k, :], pc("fin", k), bc[:, 1, 0:T], ALU.mult, ALU.mult))
                st.link(dve.tensor_copy(uT[:, k, 0:L], hT[:, k, META:T]))
                dve.tensor_copy(hT[:, k, 0:L], uT[:, k, 0:L]).then_inc(ev("x2_tiles"), 1)
            if stop <= 6:
                dve.wait_ge(ev("x2_tiles"), 8)
                return
            inverse_root(L)
            dve.wait_ge(ev("ctx_mean"), 1)
            for k in range(KT):
                st.link(stt(hx[:, k, 0:L], hT[:, k, 0:L], gain[:, k, 0:1], bc[:, 1, 0:L], ALU.mult, ALU.mult))
                ts(hx[:, k, 0:L], hx[:, k, 0:L], mod[:, k, 0:1], None, ALU.add).then_inc(ev("hx_tiles"), 1)

            cos = dist[:, 8:10, :].rearrange("p a b -> p (a b)")
            sin = dist[:, 10:12, :].rearrange("p a b -> p (a b)")

            def rotate(j):
                src, n = (pq[:, j, :], L) if j < RH else (pk[:, j - RH, :], 2 * L)
                dve.wait_ge(ev("rot_done"), j + 1)
                tt(rr[:, 1, 0:n], ps[:, 4 + j % 2, 0:n], sin[:, 0:n], ALU.mult).then_inc(ev("rot_read"), 1)
                st(tt(src, src, cos[:, 0:n], ALU.mult))
                st.wait()
                dve.wait_ge(ev("rot_read"), j + 1)
                tt(src, src, rr[:, 1, 0:n], ALU.add).then_inc(ev("rotated"), 1)
                dve.wait_ge(ev("rotated"), j + 1)

            def turn_v(h):
                dve.wait_ge(ev("v_turned"), h + 1)
                dve.tensor_copy(vtok[:, h], ps[:, 6 + h % 2, :].rearrange("p (t c) -> p t c", t=4)).then_inc(ev("v_turn_copied"), 1)

            def ret_decayed(h):
                b = h % 2
                dve.wait_ge(ev("ret_pow"), h + 1)
                st.link(tt(rD[:, b, 2:4, :], rD[:, b, 2:4, :], rr[:, 0, :].rearrange("p (a b) -> p a b", a=2), ALU.add))
                dve.wait_ge(ev("ret_s"), h + 1)
                if h >= 2:
                    dve.wait_ge(ev("ret_o"), h - 1)
                for i in range(2):
                    st(stt(rP_[:, h % 2][:, 2 * i:2 * i + 2, :], ps[:, 4 + i, :].rearrange("p (a b) -> p a b", a=2), float(P) ** -0.5,
                           rD[:, b, 2 * i:2 * i + 2, :], ALU.mult, ALU.mult))
                st.wait()
                dve.nop().then_inc(ev("ret_p"), 1)

            def ret_output(h):
                dve.wait_ge(ev("ret_o"), h + 1)
                dve.tensor_copy(ry[:, h, :], ps[:, 6 + h % 2, 0:L]).then_inc(ev("ret_y"), 1)

            def ret_centre(h):
                dve.wait_ge(ev("ret_mean"), 2 * h + 1)
                dve.wait_ge(ev("ret_y"), h + 1)
                tt(ry[:, h, :], ry[:, h, :], ps[:, 3, 0:L], ALU.subtract).then_inc(ev("ret_mean_read"), 1)
                dve.wait_ge(ev("ret_mean_read"), 2 * h + 1)
                dve.nop().then_inc(ev("ret_centred"), 1)

            def ret_norm(h):
                dve.wait_ge(ev("ret_root"), h + 1)
                st.link(dve.reciprocal(bc[:, 1, 0:L], bc[:, 0, 0:L]))
                dve.nop().then_inc(ev("ret_normed"), 1)
                st.link(stt(ry[:, h, :], ry[:, h, :], pc("retn", h), bc[:, 1, 0:L], ALU.mult, ALU.mult))

            for r in range(28):
                if 6 <= r < 14:
                    rotate(r - 6)
                if r == 13:
                    ret_args(0)
                if r in (13, 14, 15, 16):
                    turn_v(r - 13)
                if r in (15, 18, 21, 24):
                    ret_decayed((r - 15) // 3)
                if r in (16, 19, 22, 25):
                    ret_output((r - 16) // 3)
                    if r < 25:
                        ret_args((r - 16) // 3 + 1)
                if r in (17, 20, 23, 26):
                    ret_centre((r - 17) // 3)
                if r in (18, 21, 24, 27):
                    ret_norm((r - 18) // 3)
                if r == 27:
                    dve.wait_ge(ev("cgx_copied"), 12)
                    st.link(tt(pu, pu, pcg, ALU.mult))
            dve.wait_ge(ev("cgx_copied"), 16)
            st(tt(mixed[:, 4:8, :], ry, pg, ALU.mult))
            for k in range(4):
                st(ts(mixed[:, k, :], pu[:, k, :], pc("cw2", 4 + k), pc("cb2", k), ALU.mult, ALU.add))
            st.wait()
            for side in range(2):
                for k in range(4):
                    o = mixed[:, k, :].rearrange("p (r c) -> p r c", c=64)
                    x = pu[:, k, :].rearrange("p (r c) -> p r c", c=64)
                    if side == 0:
                        st(stt(o[:, :, 1:64], x[:, :, 0:63], pc("cw2", k), o[:, :, 1:64], ALU.mult, ALU.add))
                    else:
                        st(stt(o[:, :, 0:63], x[:, :, 1:64], pc("cw2", 8 + k), o[:, :, 0:63], ALU.mult, ALU.add))
                st.wait()
            st.link(tt(mixed[:, 0:4, :], mixed[:, 0:4, :], pb, ALU.mult))
            dve.nop().then_inc(ev("mix2_ready"), 1)
            if stop <= 7:
                return
            for k in range(KT):
                dve.wait_ge(ev("tiles_done"), TN[f"w{k}"] + 1)
                if k == 0:
                    dve.wait_ge(ev("tiles_freed"), TN["w0"])
                dve.tensor_copy(mx[:, k, :], bank_of(f"w{k}")[:, 0:L]).then_inc(ev("tiles_freed"), 1)
                dve.wait_ge(ev("tiles_freed"), TN[f"w{k}"] + 1)
                dve.nop().then_inc(ev("mx_tiles"), 1)

            def post(name, gate):
                st(tt(small[:, 128:136], mod[:, gate:gate + 8, 0], pc(name, 0, 8), ALU.mult))

            def onto_stream(event):
                for k in range(KT):
                    st.link(stt(mx[:, k, :], mx[:, k, :], small[:, 128 + k:129 + k], bc[:, 1, 0:L], ALU.mult, ALU.mult))
                    tt(hT[:, k, 0:L], hT[:, k, 0:L], mx[:, k, :], ALU.add).then_inc(ev(event), 1)

            post("postm", 16)
            st(stt(small[:, 144:152], mod[:, 32:40, 0], 1.0, pc("pref", 0, 8), ALU.add, ALU.mult))
            inverse_root(L)
            onto_stream("x3_tiles")
            inverse_root(L)
            dve.wait_ge(ev("x3_tiles"), KT)
            for k in range(KT):
                st.link(stt(h2[:, k, :], hT[:, k, 0:L], small[:, 144 + k:145 + k], bc[:, 1, 0:L], ALU.mult, ALU.mult))
                ts(h2[:, k, :], h2[:, k, :], mod[:, 24 + k, 0:1], None, ALU.add).then_inc(ev("h2_tiles"), 1)
            dve.wait_ge(ev("logits"), 1)
            st.link(tt(aff, ps[:, 3, 0:32].rearrange("p (w e) -> p w e", w=2), bcast8[:, 8:24].unsqueeze(1).to_broadcast([P, 2, NE]), ALU.add))
            st.link(dve.tensor_reduce(small[:, 160:162], aff, AX, ALU.max))
            st.link(tt(aff, aff, small[:, 160:162].unsqueeze(2).to_broadcast([P, 2, NE]), ALU.subtract))
            dve.nop().then_inc(ev("soft_shift"), 1)
            dve.wait_ge(ev("soft_exp"), 1)
            st.link(dve.tensor_reduce(small[:, 162:164], aff, AX, ALU.add))
            st.link(dve.reciprocal(small[:, 164:166], small[:, 162:164]))
            st.link(tt(aff, aff, small[:, 164:166].unsqueeze(2).to_broadcast([P, 2, NE]), ALU.mult))
            dve.nop().then_inc(ev("aff_ready"), 1)
            dve.wait_ge(ev("aff_turned"), 1)
            st.link(dve.tensor_copy(rtk[0:16, 0, :], ps[0:16, 3, 128:384]))
            for i in range(4):
                st.link(dve.max(rtk[0:16, 4, 8 * i:8 * i + 8], rtk[0:16, i % 2, :]))
                st.link(dve.match_replace(rtk[0:16, (i + 1) % 2, :], rtk[0:16, 4, 8 * i:8 * i + 8], rtk[0:16, i % 2, :], -1.0))
            st(ts(rtk[0:16, 1, :], rtk[0:16, 0, :], 0.0, None, ALU.is_lt))
            st.link(dve.memset(rtk[0:16, 5, :], 1.0))
            st.link(dve.tensor_tensor_scan(rtk[0:16, 2, :], rtk[0:16, 5, :], rtk[0:16, 1, :], 0.0, ALU.mult, ALU.add))
            st.link(tt(rtk[0:16, 3, :], rtk[0:16, 2, :], rtk[0:16, 1, :], ALU.mult))
            dve.nop().then_inc(ev("rank_ready"), 1)
            st(dve.memset(uT[:], 0.0))
            dve.wait_ge(ev("rank_turned"), 1)
            st.link(dve.tensor_copy(small[:, 168:200], ps[:, 3, 0:32]))
            for w in range(2):
                st(tt(sel[:, w], small[:, 168 + 16 * w:184 + 16 * w].unsqueeze(2).to_broadcast([P, NE, CAP]),
                      cs("slot").unsqueeze(1).to_broadcast([P, NE, CAP]), ALU.is_equal))
            st.wait()
            for w in range(2):
                st(tt(selg[:, w], sel[:, w], aff[:, w, :].unsqueeze(2).to_broadcast([P, NE, CAP]), ALU.mult))
            st.wait()
            dve.wait_ge(ev("h2tok_copied"), 4)
            dve.nop().then_inc(ev("sel_ready"), 1)
            if stop <= 8:
                return
            SX = 4
            with dve.Fori(0, NE) as e:
                st.loop(e, SX)
                for w in range(2):
                    st(dve.tensor_copy(sg4[:, w], selg[:, w, e, :].unsqueeze(1).to_broadcast([P, 4, CAP])))
                st.wait()
                dve.nop().then_inc(ev("sg4_ready"), 1)
                dve.wait_ge(ev("gathered"), e + 1)
                st(dve.tensor_copy(xs, ps[:, 3, 0:256].rearrange("p (k s) -> p k s", k=KT)))
                st(dve.tensor_copy(Gt, ps[:, 3, 256:512]))
                st.wait()
                dve.nop().then_inc(ev("xs_ready"), 1)
                dve.wait_ge(ev("gate_silu"), e + 1)
                dve.wait_ge(ev("units_used"), e * 12 + (U0 + 8))
                tt(he, sa, ps[:, 1, :], ALU.mult).then_inc(ev("hidden"), 1)
                dve.wait_ge(ev("units_used"), e * 12 + (U0 + 12))
                dve.tensor_copy(ye[:, 512:1024], ps[:, 1, :]).then_inc(ev("y_other"), 1)
                dve.wait_ge(ev("y_other"), e + 1)
                dve.wait_ge(ev("y_half"), e + 1)
                dve.nop().then_inc(ev("y_ready"), 1)
                dve.wait_ge(ev("scattered"), e + 1)
            st.close(NE, SX)
            post("postf", 40)
            for b in range(4):
                dve.wait_ge(ev("experts_done"), b + 1)
                dve.tensor_copy(mx[:, 2 * b:2 * b + 2, :], ps[:, 4 + b, :].rearrange("p (a c) -> p a c", a=2)).then_inc(ev("mx7"), 1)
            dve.wait_ge(ev("mx7"), 4)
            dve.wait_ge(ev("root7"), 1)
            st.link(dve.reciprocal(bc[:, 1, 0:L], bc[:, 0, 0:L]))
            onto_stream("y_final")
            for w in range(2):
                dve.wait_ge(ev("y_turned"), w + 1)
                st.link(dve.tensor_copy(otok[:, w, 0:512], ps[:, 4 + 2 * w, :]))
                dve.wait_ge(ev("out_half"), w + 1)
                dve.nop().then_inc(ev("out_ready"), 1)


NAMES = ["x", "meta_tokens", "norm1_w", "w_in", "hg_lb_logits", "hg_norm_w", "m2_conv_w", "m2_conv_b", "m2_dt_bias",
         "m2_a_log", "m2_d", "m2_norm_w", "w_out", "norm2_w", "ffn_w_up", "ffn_conv_w", "ffn_conv_b", "ffn_w_down",
         "final_norm_w", "c_2", "ctx_2", "c_ctx_2", "w_ada_2", "b_ada_2", "pre_mix_g_2", "post_mix_g_2", "pre_ffn_g_2",
         "post_ffn_g_2", "w_in_2", "conv_w_2", "conv_b_2", "ret_decay_logit_2", "ret_norm_g_2", "w_out_2",
         "w_router_2", "b_router_2", "w_gate_2", "w_up_2", "w_down_2"]


def kernel(**inputs):
    import concourse.bacc as bacc
    from concourse.bass_utils import run_bass_kernel_spmd

    nc = bacc.Bacc("TRN2", target_bir_lowering=False, num_devices=1, dynamic_dma_scratch_size=1024)
    arrays = {n: np.ascontiguousarray(inputs[n]) for n in NAMES}
    arrays["cst"], arrays["dist"] = constants()
    aps = {n: nc.dram_tensor("in_" + n, v.shape, mybir.dt.from_np(v.dtype), kind="ExternalInput").ap() for n, v in arrays.items()}
    out = nc.dram_tensor("out_y", (1, SEQ, D), F32, kind="ExternalOutput").ap()
    build(nc, aps, out)
    r = run_bass_kernel_spmd(nc, [{"in_" + n: v for n, v in arrays.items()}], core_ids=[0])
    return r.results[0]["out_y"]
```

```python
from contextlib import ExitStack

import numpy as np
import concourse.bass as bass
from concourse import mybir

F32 = mybir.dt.float32
F32R = mybir.dt.float32r
U32 = mybir.dt.uint32
ACT = mybir.ActivationFunctionType
ALU = mybir.AluOpType
AX = mybir.AxisListType.X

P = 128
D = 1024
KT = D // P
META, SEQ = 16, 256
T = META + SEQ
WINDOWS = [(0, 128), (128, 128), (256, 16)]
LEVELS = [16, 32, 64, 128]
HEADS = 8
M2H, M2P, M2G = 16, 64, 2
FF = 2816
FT = FF // P
L = 256
RH = 4
NE, CAP, DE = 16, 32, 2048
RING = 6
RING1 = 5
HB = 4
UNIT = 4096
TB = 3
WORDS = 22800

TQ, TF_, TI, TG, TZ, TX, TBM, TCM = 0, 8, 16, 24, 32, 40, 48, 50
NPROJ = 52


def par_rows():
    plan = [
        [("norm1", 8), ("lb0", 8), ("lb1", 8), ("hgn", 8), ("m2cw", 48), ("m2cb", 12), ("m2n", 8),
         ("norm2", 8), ("c", 8), ("cctx", 8)],
        [("ffw01", 88), ("prem", 8), ("postm", 8), ("pref", 8), ("postf", 8), ("fin", 8)],
        [("ffw2", 44), ("ffb", 44), ("cw2", 12), ("cb2", 4), ("retn", 4)],
        [("bada", 48)],
    ]
    where, rows = {}, []
    for b, names in enumerate(plan):
        at = 0
        for name, n in names:
            where[name] = (b, at, n)
            at += n
        rows.append(at)
    return where, rows


PAR, PAR_ROWS = par_rows()

CST = {}
_at = 0
for _name, _n in [("ident", P), ("rot", P), ("causal", P), ("mask", 4 * P), ("reset", 4 * T), ("sel2", 2),
                  ("slot", CAP)]:
    CST[_name] = (_at, _n)
    _at += _n
NCST = _at
NDIST = 8 * L


def constants():
    c = np.zeros((P, NCST), np.float32)

    def put(name, a):
        at, n = CST[name]
        c[:, at:at + n] = a

    i = np.arange(P)
    put("ident", np.eye(P))
    rot = np.zeros((P, P), np.float32)
    rot[i[64:], i[:64]] = -1.0
    rot[i[:64], i[64:]] = 1.0
    put("rot", rot)
    s, r = i[:, None], i[None, :]
    put("causal", s <= r)
    masks = [(s // 16 == r // 16) & (s <= r)]
    for w in LEVELS[1:]:
        masks.append((s // w == r // w) & (s % w < w // 2) & (r % w >= w // 2))
    put("mask", np.concatenate(masks, 1))
    t = np.arange(T)
    put("reset", np.tile(np.concatenate([t % w != 0 for w in LEVELS])[None], (P, 1)))
    put("sel2", (i[:, None] % 32) == np.arange(2)[None])
    put("slot", np.tile(np.arange(1, CAP + 1, dtype=np.float32)[None], (P, 1)))
    inv = (1.0 / (np.float32(10000.0) ** (np.arange(64, dtype=np.float32) / np.float32(64)))).astype(np.float32)
    pos = np.concatenate([L + np.arange(L), np.arange(L)]).astype(np.float32)
    ang = (pos[None, :] * inv[:, None]).astype(np.float32)
    n = np.arange(L)[None, :]
    lat = [np.maximum(n - (128 * k + s), 0) for k in range(2)] + [np.maximum((128 * k + s) - n, 0) for k in range(2)]
    ctx = [L + n - (128 * k + s) for k in range(2)] + [L - n + (128 * k + s) for k in range(2)]
    dist = np.concatenate(lat + ctx + [np.tile(f(ang), (2, 1)) for f in (np.cos, np.sin)], 1).astype(np.float32)
    return c, dist


class Steps:

    def __init__(self, engine, sem):
        self.engine, self.sem, self.n, self.turn = engine, sem, 0, 0

    def __call__(self, ins):
        self.n += 1
        ins.then_inc(self.sem, 1)

    def wait(self):
        self.engine.wait_ge(self.sem, self.turn + self.n)

    def link(self, ins):
        self(ins)
        self.wait()

    def loop(self, i, steps):
        self.turn = self.turn + i * steps
        self.start = self.n

    def close(self, turns, steps):
        assert self.n - self.start == steps, (self.n - self.start, steps)
        self.turn = 0
        self.n += (turns - 1) * steps


def build(nc, a, out):
    with ExitStack() as ctx:
        def sb(name, shape, dt=F32):
            return ctx.enter_context(nc.sbuf_tensor(name, shape, dt))

        sems = {}

        def ev(name):
            if name not in sems:
                sems[name] = ctx.enter_context(nc.semaphore("s_" + name))
            return sems[name]

        with ExitStack() as first:
            twins = [first.enter_context(nc.sbuf_tensor(name, shape, F32R)) for name, shape in
                     [("ring_r", [P, RING, UNIT]), ("arena_r", [P, WORDS]), ("uT_r", [P, KT, T])]]
        ring = sb("ring", [P, RING, UNIT])
        arena = sb("arena", [P, WORDS])
        uT = sb("uT", [P, KT, T])
        twin_of = dict(zip(("ring", "arena", "uT"), twins))

        def r_(ap):
            return bass.AP(tensor=twin_of[ap.tensor.name], offset=ap.offset, ap=[list(x) for x in ap.ap])

        def f_(ap):
            return r_(ap).bitcast(F32)

        cst = sb("cst", [P, NCST])
        hT = sb("hT", [P, KT, T])
        par = sb("par", [P, 4 * P])
        mod = sb("mod", [P, 48, 2])
        cond = sb("cond", [P, KT, 32])
        ones = sb("ones", [P, P])
        ones4 = sb("ones4", [P, P])
        ones1 = sb("ones1", [P, P])
        eps = sb("eps", [P, 1])
        bc = sb("bc", [P, 2, 2 * L])
        small = sb("small", [P, 256])
        wsm = sb("wsm", [P, 2, KT, 16])
        tkq = sb("tkq", [P, 3, 3, 16])
        bcast8 = sb("bcast8", [P, 40])
        ps = ctx.enter_context(nc.psum_tensor("ps", [P, 8, 512], F32))

        class Arena:

            def __init__(self, at):
                self.at = at

            def take(self, *shape):
                n = int(np.prod(shape))
                v = arena[:, self.at:self.at + n]
                self.at += n
                assert self.at <= WORDS, self.at
                if len(shape) == 2:
                    v = v.rearrange("p (a b) -> p a b", a=shape[0])
                if len(shape) == 3:
                    v = v.rearrange("p (a b c) -> p a b c", a=shape[0], b=shape[1])
                return v

        def cs(name, rows=P):
            at, n = CST[name]
            return cst[0:rows, at:at + n]

        ident = cs("ident")

        def pc(name, i=0, n=1):
            b, at, rows = PAR[name]
            return par[:, b * P + at + i:b * P + at + i + n]

        A = Arena(0)
        proj = A.take(NPROJ, T)
        mrow = A.take(512)
        x_at = A.at
        tok = A.take(3, D)
        prow = A.take(4, P)
        chan = A.take(2, T)[0:16]
        A = Arena(x_at)
        hg_B = A.take(2, 4, T)
        hg_D = A.take(2, 4, 256)
        hg_K0 = A.take(2, T)
        hg_v = A.take(3, P)
        hg_ke = A.take(2, P)
        hg_P = A.take(2, P)
        hg_P2 = A.take(16)
        hg_S = A.take(2, P)
        uhi = A.take(KT, T)
        hg_f, hg_k, hg_lf, hg_sq = (proj[:, TBM + i, :] for i in range(4))
        hg_o = hg_sq
        A = Arena(x_at)
        m2_t = A.take(2, T)
        rows_at = A.at
        m2_x = A.take(3, 512)
        m2_b = A.take(2, P)
        m2_cb = A.take(2, P)
        m2_cb2 = A.take(16)
        m2_seg = A.take(256)
        m2P2 = A.take(4, 16)[0:16]
        m2C = A.take(4, 144)
        assert A.at <= x_at + 3 * D + 4 * P
        A = Arena((TG + 4) * T)
        m2_xe = A.take(2, 512)
        m2_S = A.take(2, 512)
        m2P0 = A.take(4, P)
        m2P1 = A.take(4, P)
        assert A.at <= TX * T

        def ch(row):
            return chan[:, row, :] if row < 2 else arena[0:16, rows_at + (row - 2) * T:rows_at + (row - 1) * T]

        A = Arena(0)
        act_ = A.take(FT, T)
        fc = A.take(2, 2, T)
        dist_at = A.at
        dist = A.take(12, L)
        ctok = A.take(2, D)
        vtok = ctok.rearrange("p w (a b) -> p (w a) b", b=512).rearrange("p h (t c) -> p h t c", t=4)
        hx_at = A.at
        hx = A.take(KT, 2 * L)
        act_hi = Arena(A.at).take(FT, T)
        uhi2 = Arena(dist_at).take(KT, T)
        hxhi = A.take(KT, 2 * L)
        pcg, pu = hx[:, 0:4, L:2 * L], hx[:, 4:8, L:2 * L]
        pg = hxhi[:, 0:4, L:2 * L]
        rD = A.take(2, 4, L)
        A = Arena(0)
        pq = A.take(4, L)
        pk = A.take(4, 2 * L)
        pv = A.take(4, 2 * L)
        pb = A.take(4, L)
        A = Arena(hx_at)
        mixed = A.take(KT, L)
        mx = A.take(KT, L)
        rr = cst[:, CST["mask"][0]:CST["mask"][0] + 4 * L].rearrange("p (a b) -> p a b", a=2)
        rP_ = uT[:].rearrange("p a b -> p (a b)")[:, 0:8 * L].rearrange("p (a b c) -> p a b c", a=2, b=4)
        ry = pq
        A = Arena(0)
        h2 = A.take(KT, L)
        h2tok = A.take(2, D)
        sel = A.take(2, NE, CAP)
        selg = A.take(2, NE, CAP)
        aff = A.take(2, NE)
        rtk = A.take(8, L)
        sg4 = A.take(2, 4, CAP)
        Gt = A.take(L)
        xs = A.take(KT, CAP)
        sa = A.take(512)
        he = A.take(512)
        heT = A.take(4, P)
        ye = A.take(D)
        assert A.at <= hx_at
        gtok = mixed.rearrange("p k l -> p (k l)")[:, 0:D]
        ysq = mixed.rearrange("p k l -> p (k l)")[:, D:2 * D]
        A = Arena(hx_at + 2 * KT * L)
        otok = A.take(2, D)

        def slot(u):
            return ring[:, u % RING1, :]

        units = []

        def unit(pieces):
            units.append(pieces)
            return len(units) - 1

        def kview(w):
            return w.rearrange("(k p) c -> p k c", p=P)

        def cols(w, c0, k0=0, k1=KT, n=512):
            u = len(units)
            return unit([(slot(u)[:, 0:(k1 - k0) * n].rearrange("p (k c) -> p k c", c=n),
                          kview(w)[:, k0:k1, c0:c0 + n])])

        w_in, w_ada = a["w_in"][0], a["w_ada_2"][0]
        ORDER = [10, 11, 12, 2, 0, 4, 6, 3, 1, 5, 7, 8, 9]
        u_in, u_ada = [], []
        for n, blk in enumerate(ORDER):
            u_in.append(cols(w_in, 512 * blk))
            if n < 12:
                u_ada.append(cols(w_ada, 512 * n))
        u_out = [[cols(a["w_out"][0], 512 * cb, 8 * kh, 8 * kh + 8) for cb in range(2)] for kh in (1, 0)]
        u_up = []
        for i in range(11):
            v = slot(len(units)).rearrange("p (k s c) -> p k s c", k=KT, s=2)
            w = kview(a["ffn_w_up"][0])
            u_up.append(unit([(v[:, :, s, :], w[:, :, FF * s + 256 * i:FF * s + 256 * i + 256]) for s in range(2)]))
        DK = [(0, 8), (8, 16), (16, 22)]
        u_dn = [[cols(a["ffn_w_down"][0], 512 * cb, k0, k1) for k0, k1 in DK] for cb in range(2)]
        ORDER2 = [3, 4, 5, 1, 2, 6, 0]
        u_in2 = [cols(a["w_in_2"][0], 512 * n) for n in ORDER2]
        u_out2 = [cols(a["w_out_2"][0], 512 * n) for n in range(2)]
        U0 = len(units)
        slot_count = [0] * RING
        ready_at = []
        for u, pieces in enumerate(units):
            slot_count[u % RING1] += 16 * len(pieces)
            ready_at.append(slot_count[u % RING1])

        def slot_ready(u):
            return ev(f"slot{u % RING1}_loaded")

        chunks, CH = [], {}

        def chunk(name, u, view):
            CH[name] = len(chunks)
            chunks.append((u, view))

        def kcols(u, m, n=KT):
            return slot(u)[:, 0:n * 512].rearrange("p (k c) -> p k c", c=512)[:, :, m * P:m * P + P]

        for j in range(NPROJ):
            chunk(f"p{j}", u_in[j // 4], kcols(u_in[j // 4], j % 4))
        for half in range(2):
            for k in range(KT):
                u = u_out[half][k // 4]
                chunk(f"o{'ba'[half]}{k}", u, kcols(u, k % 4))
        for i in range(2 * FT):
            u = u_up[i // 4]
            chunk(f"f{i}", u, slot(u).rearrange("p (k s c) -> p k s c", k=KT, s=2)[:, :, i % 2, (i // 2 % 2) * P:(i // 2 % 2) * P + P])
        for k in range(KT):
            for i, (k0, k1) in enumerate(DK):
                u = u_dn[k // 4][i]
                chunk(f"d{k}.{i}", u, kcols(u, k % 4, k1 - k0))
        for r in range(28):
            chunk(f"q{r}", u_in2[r // 4], kcols(u_in2[r // 4], r % 4))

        def rounded(c):
            nk = chunks[c][1].shape[1]
            at = (c % HB) * KT * P
            return ring[:, RING - 1, at:at + nk * P].rearrange("p (k c) -> p k c", k=nk)


        seq = [f"x{k}" for k in range(KT)] + ["n1"]
        for j in range(NPROJ):
            seq += ["dt"] * (j == 12) + ["mz0"] * (j == 50) + [f"p{j}"]
        seq += [f"ob{k}" for k in range(KT)] + [f"oa{k}" for k in range(KT)] + ["n2"]
        seq += [f"f{i}" for i in range(2 * FT)] + [f"d{k}" for k in range(KT)] + ["n3", "n4"]
        seq += [f"q{j}" for j in range(28)] + [f"w{k}" for k in range(KT)] + ["n5", "n6"]
        TN = {name: i for i, name in enumerate(seq)}

        def bank_of(name):
            return ps[:, TN[name] % TB, :]

        block = ctx.enter_context(nc.Block())
        PAR_LOADS = [10, 6, 5, 1]

        @block.sync
        def _(sp):
            def load(dst, src, sem, **kw):
                sp.dma_start(dst, src, **kw).then_inc(ev(sem), 16)

            load(cst[:], a["cst"], "cst_loaded")
            load(tok[0:16, 0, :], a["meta_tokens"], "tok_loaded")
            load(tok[16:128, 0, :], a["x"][0, 0:112], "tok_loaded")
            load(tok[:, 1, :], a["x"][0, 112:240], "tok_loaded")
            load(tok[0:16, 2, :], a["x"][0, 240:256], "tok_loaded")

            def stream(u):
                if u == 0:
                    sp.wait_ge(ev("par_loaded"), 16 * PAR_LOADS[0])
                if u >= RING1:
                    sp.wait_ge(ev("units_used"), u - RING1 + 1)
                for dst, src in units[u]:
                    sp.dma_start(dst, src).then_inc(slot_ready(u), 16)

            def rows(name, src):
                b, r, n = PAR[name]
                n = src.shape[0]
                load(prow[r:r + n, b, :], src, "par2_loaded" if b else "par_loaded")

            def r1(w):
                return w.rearrange("o (k p) -> (o k) p", p=P)

            def more_parameters():
                rows("fin", a["final_norm_w"].rearrange("(k p) -> k p", p=P))
                rows("ffw01", r1(a["ffn_conv_w"][0, 0:2]))
                rows("prem", r1(a["pre_mix_g_2"]))
                rows("postm", r1(a["post_mix_g_2"]))
                rows("pref", r1(a["pre_ffn_g_2"]))
                rows("postf", r1(a["post_ffn_g_2"]))
                rows("ffw2", r1(a["ffn_conv_w"][0, 2:3]))
                rows("ffb", r1(a["ffn_conv_b"]))
                rows("cw2", r1(a["conv_w_2"][0]))
                rows("cb2", r1(a["conv_b_2"]))
                rows("retn", r1(a["ret_norm_g_2"]))
                rows("bada", r1(a["b_ada_2"]))
                load(chan[:, 0, 0:1], a["m2_dt_bias"].rearrange("o h -> h o"), "small_loaded")
                load(chan[:, 0, 1:2], a["m2_a_log"].rearrange("o h -> h o"), "small_loaded")
                for half in range(2):
                    load(bcast8[64 * half:64 * half + 64, 0:8],
                         a["m2_d"].rearrange("o (k two) -> o two k", two=2)[:, half, :].to_broadcast([64, 8]), "small_loaded",
                         allow_slow_non_contiguous=True)
                load(bcast8[:, 8:24], a["b_router_2"].to_broadcast([P, 16]), "small_loaded")
                load(bcast8[:, 24:32], a["ret_decay_logit_2"].rearrange("o d h -> o (d h)").to_broadcast([P, 8]), "small_loaded")
                load(wsm[:, 0], kview(w_in)[:, :, 6656:6672], "small_loaded")
                load(wsm[:, 1], kview(a["w_router_2"][0]), "small_loaded")

            for u in range(U0):
                stream(u)
                if u == 1:
                    more_parameters()
                if u == u_up[6]:
                    sp.wait_ge(ev("out_done"), 1)
                    load(ctok[:], a["ctx_2"][0].rearrange("(w p) c -> p w c", p=P), "ctx_loaded")
                if u == u_dn[1][1]:
                    sp.wait_ge(ev("units_used"), u_up[-1] + 1)
                    load(dist[:].rearrange("p a b -> p (a b)"), a["dist"], "dist_loaded")

            def expert_unit(used, e, i, after=0):
                s = i % RING
                if i < 8:
                    w = a["w_gate_2" if i < 4 else "w_up_2"][0, after:][e]
                    src = kview(w)[:, 2 * (i % 4):2 * (i % 4) + 2, :]
                    dst = ring[:, s, :].rearrange("p (k c) -> p k c", k=2)
                else:
                    w = a["w_down_2"][0].rearrange("e f c -> (e f) c")[bass.ds(e * DE, DE), :]
                    src = w.rearrange("(j b p) c -> b p j c", b=4, p=P)[i - 8]
                    dst = ring[:, s, :].rearrange("p (j c) -> p j c", j=4)
                sp.wait_ge(ev("units_used"), used)
                sp.dma_start(dst, src).then_inc(ev(f"slot{s}_loaded"), 16)

            for i in range(RING):
                before = [u for u in range(U0) if u % RING1 == i]
                expert_unit(before[-1] + 1 if before else u_in2[-1] + 1, 0, i)
            with sp.Fori(0, NE - 1) as e:
                for i in range(RING, 12 + RING):
                    expert_unit(e * 12 + (U0 + i - RING + 1), e, i % 12, i // 12)
            for i in range(RING, 12):
                expert_unit((NE - 1) * 12 + (U0 + i - RING + 1), NE - 1, i)
            for w in range(2):
                sp.wait_ge(ev("out_ready"), w + 1)
                sp.dma_start(out[0, w * P:w * P + P, :], otok[:, w, :]).then_inc(ev("stored"), 16)
            sp.wait_ge(ev("stored"), 32)

        @block.tensor
        def _(pe):
            opened = [0]

            def open_tile(name):
                assert TN[name] == opened[0], (name, opened[0])
                if opened[0] >= TB:
                    pe.wait_ge(ev("tiles_freed"), opened[0] - TB + 1)
                opened[0] += 1
                return bank_of(name)

            def done(mm):
                mm.then_inc(ev("tiles_done"), 1)

            def weights(u):
                pe.wait_ge(slot_ready(u), ready_at[u])

            def used(u_count=1):
                pe.wait_ge(ev("tiles_done"), opened[0])
                pe.nop().then_inc(ev("units_used"), u_count)

            def group(pairs, o):
                for i, (l, r) in enumerate(pairs):
                    mm = pe.matmul(o, l, r, start=i == 0, stop=i == len(pairs) - 1)
                return mm

            def split_products(name, o, xhi, xlo, k0=0, first=True, last=True, x_ready=None, ks=None, ready="u_tiles"):
                c = CH[name]
                pe.wait_ge(ev("w_lo"), c + 1)
                hi, lo = r_(rounded(c)), r_(chunks[c][1])
                nk = hi.shape[1]
                for k in ks or range(nk):
                    if x_ready is not None:
                        pe.wait_ge(ev(ready), x_ready + k + 1)
                    pe.matmul(o, hi[:, k, :], r_(xhi(k0 + k)), start=first and k == 0, stop=False)
                    mm = pe.matmul(o, hi[:, k, :], r_(xlo(k0 + k)), start=False, stop=False)
                    if k == nk - 1:
                        mm.then_inc(ev("hi_used"), 1)
                    mm = pe.matmul(o, lo[:, k, :], r_(xhi(k0 + k)), start=False, stop=last and k == nk - 1)
                return mm

            squares = [0]

            def norm_sum(name, n, src, w=ones, nk=KT):
                o = open_tile(name)
                for k in range(nk):
                    squares[0] += 1
                    pe.wait_ge(ev("squares"), squares[0])
                    mm = pe.matmul(o[:, 0:n], w[:], src(k), start=k == 0, stop=k == nk - 1)
                done(mm)

            pe.wait_ge(ev("cst_loaded"), 16)
            pe.wait_ge(ev("tok_loaded"), 64)
            for k in range(KT):
                o = open_tile(f"x{k}")
                for w, (t0, n) in enumerate(WINDOWS):
                    mm = pe.transpose(o[:, t0:t0 + n], tok[0:n, w, k * P:k * P + P], ident[0:n, 0:n])
                done(mm)
            def turn_parameters(blocks):
                for b in blocks:
                    n = PAR_ROWS[b]
                    mm = pe.transpose(ps[:, 3 if b == 0 else 4, b * P:b * P + n], prow[0:n, b, :], ident[0:n, 0:n])
                mm.then_inc(ev("par_turned"), 1)

            pe.wait_ge(ev("par_loaded"), 16 * PAR_LOADS[0])
            turn_parameters([0])
            norm_sum("n1", T, lambda k: uT[:, k, :])

            def ada(n):
                weights(u_ada[n])
                if n:
                    pe.wait_ge(ev("mod_done"), n)
                else:
                    pe.wait_ge(ev("cond_ready"), 1)
                w = slot(u_ada[n]).rearrange("p (k c) -> p k c", k=KT)
                for k in range(KT):
                    j = k % 4
                    mm = pe.matmul(ps[32 * j:32 * j + 32, 3, :], cond[:, k, :], w[:, k, :], start=k < 4, stop=k >= 4)
                mm.then_inc(ev("units_used"), 1)

            def turn_mod(n):
                pe.wait_ge(ev("mod_row"), n + 1)
                for b in range(4):
                    mm = pe.matmul(ps[:, 3, 2 * b:2 * b + 2], mrow[:, b * P:b * P + P], cs("sel2"), start=True, stop=True)
                mm.then_inc(ev("mod_turned"), 1)

            def m2_turn_rows():
                pe.wait_ge(ev("m2_rows"), 1)
                for i, row in enumerate((1, 0, 3)):
                    for w, (t0, n) in enumerate(WINDOWS):
                        mm = pe.transpose(ps[0:n, 4, (w * 3 + i) * 16:(w * 3 + i) * 16 + 16], ch(row)[:, t0:t0 + n], ident[0:16, 0:16])
                mm.then_inc(ev("m2_rows_turned"), 1)

            def m2_turn(g):
                pe.wait_ge(ev("m2_conv"), 12)
                pe.wait_ge(ev("m2_tk"), 1)
                if g:
                    pe.wait_ge(ev("m2_out"), 4)
                for w, (t0, n) in enumerate(WINDOWS):
                    for c in range(4):
                        pe.transpose(ps[0:n, 4 + w, c * P:c * P + P], proj[:, TX + 4 * g + c, t0:t0 + n], ident)
                for w in range(2):
                    mm = pe.transpose(ps[:, 7, w * P:w * P + P], proj[:, TBM + g, w * P:w * P + P], ident)
                mm.then_inc(ev("m2_turned"), 1)

            def m2_states(g):
                pe.wait_ge(ev("m2_staged"), g + 1)
                for w in range(2):
                    s = slice(w * P, w * P + P)
                    pe.matmul(ps[:, 4, w * P:w * P + P], proj[:, TBM + g, s], proj[:, TCM + g, s], start=True, stop=True)
                pe.matmul(ps[0:16, 5, 0:16], proj[:, TBM + g, 256:T], proj[:, TCM + g, 256:T], start=True, stop=True)
                for w in range(2):
                    mm = pe.matmul(ps[:, 6 + w, :], m2_b[:, w, :], m2_xe[:, w, :], start=True, stop=True)
                mm.then_inc(ev("m2_update"), 1)

            def m2_spread(q):
                pe.wait_ge(ev("m2_group"), q // 2 + 1)
                pe.wait_ge(ev("m2_tk"), 1)
                if q % 2:
                    pe.wait_ge(ev("m2_out"), 2 * q)
                for w, (t0, n) in enumerate(WINDOWS):
                    for j in range(4):
                        hd = 4 * q + j
                        mm = pe.matmul(ps[:, (4, 5, 7)[w], j * n:j * n + n], ident[0:16, hd:hd + 1].to_broadcast([16, P]),
                                       ch(0)[:, t0:t0 + n], start=True, stop=True)
                mm.then_inc(ev("m2_a"), 1)

            def m2_heads(q):
                pe.wait_ge(ev("m2_pc"), q + 1)
                if q:
                    pe.wait_ge(ev("m2_out"), 2 * q)
                for pair in range(2):
                    for hh in range(2):
                        j = 2 * pair + hh
                        hc = (4 * (q % 2) + j) * M2P
                        o = ps[64 * hh:64 * hh + 64, 6 + pair, :]
                        pe.matmul(o[:, 0:128], m2_x[:, 0, hc:hc + M2P], m2P0[:, j, :], start=True, stop=True)
                        pe.matmul(o[:, 128:256], m2_x[:, 1, hc:hc + M2P], m2P1[:, j, :], start=True, stop=False)
                        pe.matmul(o[:, 128:256], m2_S[:, 0, hc:hc + M2P], m2C[:, j, 0:128], start=False, stop=True)
                        pe.matmul(o[:, 256:T], m2_x[0:16, 2, hc:hc + M2P], m2P2[:, j, :], start=True, stop=False)
                        mm = pe.matmul(o[:, 256:T], m2_S[:, 1, hc:hc + M2P], m2C[:, j, 128:144], start=False, stop=True)
                    mm.then_inc(ev("m2_y"), 1)

            def hg_turn(h):
                b = h % 2
                pe.wait_ge(ev("hg_staged"), h + 1)
                if h:
                    pe.wait_ge(ev("hg_head"), h)
                else:
                    pe.wait_ge(ev("m2_out"), 8)
                for w, (t0, n) in enumerate(WINDOWS):
                    pe.transpose(ps[0:n, 6, w * P:w * P + P], proj[:, TI + h, t0:t0 + n], ident)
                for w in range(2):
                    mm = pe.transpose(ps[:, 7, w * P:w * P + P], hg_D[:, b, 3, w * P:w * P + P], ident)
                mm.then_inc(ev("hg_turned"), 1)
                keys = [hg_K0[:, b], hg_D[:, b, 0, :], hg_D[:, b, 1, :], hg_D[:, b, 2, :]]
                for l in range(4):
                    q = hg_B[:, b, max(l - 1, 0), :]
                    for w in range(2):
                        s = slice(w * P, w * P + P)
                        pe.matmul(ps[:, 4 + l // 2, (l % 2) * 256 + w * P:(l % 2) * 256 + w * P + P], keys[l][:, s], q[:, s], start=True, stop=True)
                pe.wait_ge(ev("hg_v"), h + 1)
                pe.matmul(ps[0:16, 6, 384:400], hg_K0[:, b, 256:T], hg_B[:, b, 0, 256:T], start=True, stop=True).then_inc(ev("hg_scores"), 1)

            def hg_updates(h):
                pe.wait_ge(ev("hg_ke"), h + 1)
                for w in range(2):
                    mm = pe.matmul(ps[:, 7, w * P:w * P + P], hg_ke[:, w, :], hg_v[:, w, :], start=True, stop=True)
                mm.then_inc(ev("hg_update"), 1)

            def hg_out(h):
                b = h % 2
                pe.wait_ge(ev("hg_masked"), h + 1)
                pe.matmul(ps[:, 6, 0:128], hg_v[:, 0, :], hg_P[:, 0, :], start=True, stop=True)
                group([(hg_v[:, 1, :], hg_P[:, 1, :]), (hg_S[:, 0, :], hg_B[:, b, 3, 128:256])], ps[:, 6, 128:256])
                pe.matmul(ps[:, 6, 256:T], hg_v[0:16, 2, :], hg_P2[0:16, :], start=True, stop=False)
                pe.matmul(ps[:, 6, 256:T], hg_S[:, 1, :], hg_B[:, b, 3, 256:T], start=False, stop=True).then_inc(ev("hg_out"), 1)

            def hg_mean(h):
                pe.wait_ge(ev("hg_squared"), h + 1)
                pe.matmul(ps[:, 7, 0:T], ones1[:], hg_sq, start=True, stop=True).then_inc(ev("hg_mean"), 1)

            def hgrn(j):
                h = (j - 32) // 3
                if j >= 32 and h < HEADS:
                    (hg_turn, hg_updates, hg_mean)[(j - 32) % 3](h)

            def hgrn_inside(j):
                h = (j - 32) // 3
                if j >= 32 and h < HEADS and (j - 32) % 3 == 1:
                    hg_out(h)

            for j in range(NPROJ):
                n, m = divmod(j, 4)
                if j == 12:
                    pe.wait_ge(ev("small_loaded"), 16 * 8)
                    o = open_tile("dt")
                    done(group([(wsm[:, 0, k, :], f_(x[:, k, :])) for k in range(KT) for x in (uhi, uT)], o[0:16, 0:T]))
                if j == 3:
                    pe.wait_ge(ev("par2_loaded"), 16 * sum(PAR_LOADS[1:]))
                    turn_parameters([1, 2, 3])
                if j == 16:
                    m2_turn_rows()
                if j in (17, 24):
                    m2_turn((17, 24).index(j))
                if j in (18, 25):
                    m2_states((18, 25).index(j))
                if j in (21, 23, 28, 30):
                    m2_heads((21, 23, 28, 30).index(j))
                if j in (19, 21, 26, 28):
                    m2_spread((19, 21, 26, 28).index(j))
                hgrn(j)
                if j == 50:
                    norm_sum("mz0", T, lambda k: proj[:, TX + k, :], ones4, 4)
                if m == 2 and n:
                    turn_mod(n - 1)
                o = open_tile(f"p{j}")
                x, late_x = (lambda k: uhi[:, k, :], lambda k: uT[:, k, :]), None if j else 0
                split_products(f"p{j}", o[:, 0:T], *x, last=False, x_ready=late_x, ks=range(4))
                hgrn_inside(j)
                done(split_products(f"p{j}", o[:, 0:T], *x, first=False, x_ready=late_x, ks=range(4, KT)))
                if m == 3:
                    used()
                    if n < 12:
                        ada(n)
            hgrn(52)
            pe.wait_ge(ev("m2_normed"), 1)
            early = [open_tile(f"ob{k}") for k in range(3)]
            for k in range(3):
                split_products(f"ob{k}", early[k][:, 0:T], lambda i: proj[:, TX + i, :], lambda i: proj[:, TZ + i, :], last=False, ks=range(4))
            for k in range(4):
                squares[0] += 1
                pe.wait_ge(ev("squares"), squares[0])
                mm = pe.matmul(ps[:, 3, 0:T], ones4[:], proj[:, TX + 4 + k, :], start=k == 0, stop=k == 3)
            mm.then_inc(ev("mz1_done"), 1)
            for half in range(2):
                for k in range(KT):
                    cb, m = divmod(k, 4)
                    if half == 0 and k:
                        hgrn(52 + k)
                        hgrn_inside(52 + k)
                    if half == 1 and k == 0:
                        pe.wait_ge(ev("hg_lo"), HEADS)
                    if half == 0 and k == 0:
                        pe.wait_ge(ev("m2_normed"), 2)
                    late = half == 0 and k < 3
                    o = early[k] if late else open_tile(f"o{'ba'[half]}{k}")
                    thi, tlo = ((TX, TZ), (TF_, TQ))[half]
                    done(split_products(f"o{'ba'[half]}{k}", o[:, 0:T], lambda i: proj[:, thi + i, :], lambda i: proj[:, tlo + i, :],
                                        first=not late, ks=range(4, KT) if late else None))
                    if m == 3:
                        pe.wait_ge(ev("tiles_done"), TN[f"o{'ba'[half]}{k}"] + 1)
                        pe.nop().then_inc(ev("units_used"), 1)
            norm_sum("n2", T, lambda k: uT[:, k, :])
            pe.wait_ge(ev("tiles_freed"), opened[0] - 1)
            pe.nop().then_inc(ev("out_done"), 1)
            for i in range(FT):
                for s in range(2):
                    o = open_tile(f"f{2 * i + s}")
                    done(split_products(f"f{2 * i + s}", o[:, 0:T], lambda k: uhi2[:, k, :], lambda k: uT[:, k, :],
                                        x_ready=None if i or s else KT))
                if i % 2 == 1:
                    used()
                if 13 <= i <= 16:
                    c = i - 13
                    if c == 0:
                        pe.wait_ge(ev("ctx_loaded"), 16)
                    if c >= 2:
                        pe.wait_ge(ev("ctx_copied"), c - 1)
                    for kk in range(2):
                        for w_ in range(2):
                            mm = pe.transpose(ps[:, 4 + c % 2, kk * L + w_ * P:kk * L + w_ * P + P],
                                              ctok[:, w_, (2 * c + kk) * P:(2 * c + kk) * P + P], ident)
                    mm.then_inc(ev("ctx_turned"), 1)
                if i == 18:
                    pe.wait_ge(ev("ctx_squared"), 1)
                    group([(ones[:], hx[:, k, 0:L]) for k in range(KT)], ps[:, 6, 0:L]).then_inc(ev("ctx_mean"), 1)
            for k in range(KT):
                cb, m = divmod(k, 4)
                o = open_tile(f"d{k}")
                for i, (k0, k1) in enumerate(DK):
                    if k == 0:
                        pe.wait_ge(ev("ffn_act"), k1)
                    mm = split_products(f"d{k}.{i}", o[:, 0:T], lambda kk: act_hi[:, kk, :], lambda kk: act_[:, kk, :],
                                        k0, i == 0, i == 2)
                done(mm)
                if m == 3:
                    used(3)
            norm_sum("n3", T, lambda k: uT[:, k, :])
            norm_sum("n4", L, lambda k: uT[:, k, 0:L])

            def in2(r):
                n, m = divmod(r, 4)
                width = 2 * L if n in (1, 2) else L
                o = open_tile(f"q{r}")
                if r == 4:
                    pe.wait_ge(ev("u_tiles"), 2 * KT + 1)
                done(split_products(f"q{r}", o[:, 0:width], lambda k: hxhi[:, k, 0:width], lambda k: hx[:, k, 0:width],
                                    x_ready=None if r else 0, ready="mod_tiles"))
                if m == 3:
                    used()

            def rotate(j):
                pe.wait_ge(ev("qk_copied"), j + 1)
                if j >= 2:
                    pe.wait_ge(ev("rot_read"), j - 1)
                src, n = (pq[:, j, :], L) if j < RH else (pk[:, j - RH, :], 2 * L)
                pe.matmul(ps[:, 4 + j % 2, 0:n], cs("rot"), src, start=True, stop=True).then_inc(ev("rot_done"), 1)

            def turn_v(h):
                pe.wait_ge(ev("v_copied"), h + 1)
                if h >= 2:
                    pe.wait_ge(ev("v_turn_copied"), h - 1)
                for t in range(4):
                    mm = pe.transpose(ps[:, 6 + h % 2, t * P:t * P + P], pv[:, h, t * P:t * P + P], ident)
                mm.then_inc(ev("v_turned"), 1)

            def ret_scores(h):
                pe.wait_ge(ev("rotated"), RH + h + 1)
                pe.wait_ge(ev("rot_read"), 2 * RH)
                if h:
                    pe.wait_ge(ev("ret_p"), h)
                for t in range(4):
                    mm = pe.matmul(ps[:, 4 + t // 2, (t % 2) * L:(t % 2) * L + L], pk[:, h, t * P:t * P + P], pq[:, h, :], start=True, stop=True)
                mm.then_inc(ev("ret_s"), 1)

            def ret_out(h):
                pe.wait_ge(ev("ret_p"), h + 1)
                pe.wait_ge(ev("v_turn_copied"), RH)
                if h >= 2:
                    pe.wait_ge(ev("ret_y"), h - 1)
                group([(vtok[:, h, t, :], rP_[:, h % 2][:, t, :]) for t in range(4)], ps[:, 6 + h % 2, 0:L]).then_inc(ev("ret_o"), 1)

            def ret_mean(h, which):
                pe.wait_ge(ev("ret_y" if which == 0 else "ret_sq"), h + 1)
                if h or which:
                    pe.wait_ge(ev("ret_mean_read"), 2 * h + which)
                src = ry[:, h, :] if which == 0 else rr[:, 1, 0:L]
                pe.matmul(ps[:, 3, 0:L], ones1[:], src, start=True, stop=True).then_inc(ev("ret_mean"), 1)

            for r in range(28):
                in2(r)
                if 6 <= r < 14:
                    rotate(r - 6)
                if r in (13, 14, 15, 16):
                    turn_v(r - 13)
                if r in (15, 18, 21, 24):
                    ret_scores((r - 15) // 3)
                if r in (16, 19, 22, 25):
                    ret_out((r - 16) // 3)
                if r in (17, 20, 23, 26):
                    ret_mean((r - 17) // 3, 0)
                if r in (18, 21, 24, 27):
                    ret_mean((r - 18) // 3, 1)
            for k in range(KT):
                cb, m = divmod(k, 4)
                o = open_tile(f"w{k}")
                if m == 0:
                    weights(u_out2[cb])
                w = slot(u_out2[cb]).rearrange("p (k c) -> p k c", k=KT)
                order = [4, 5, 6, 0, 1, 2, 3, 7]
                for n, i in enumerate(order):
                    if k == 0:
                        pe.wait_ge(ev("conv_gated" if i < 4 else "ret_gated"), i % 4 + 1)
                    mixed_i = pcg[:, i, :] if i < 4 else ry[:, i - 4, :]
                    mm = pe.matmul(o[:, 0:L], w[:, i, m * P:m * P + P], mixed_i, start=n == 0, stop=n == KT - 1)
                done(mm)
                if m == 3:
                    used()
            norm_sum("n5", L, lambda k: uT[:, k, 0:L])
            norm_sum("n6", L, lambda k: uT[:, k, 0:L])
            pe.wait_ge(ev("ret_mean_read"), 2 * RH)
            for w in range(2):
                for k in range(KT):
                    if w == 0:
                        pe.wait_ge(ev("mod_tiles"), KT + k + 1)
                    mm = pe.matmul(ps[:, 3, w * 16:w * 16 + 16], h2[:, k, w * P:w * P + P], wsm[:, 1, k, :], start=k == 0, stop=k == KT - 1)
            mm.then_inc(ev("router_products"), 1)
            for w in range(2):
                for k in range(KT):
                    mm = pe.transpose(ps[:, 4 + 2 * w + k // 4, (k % 4) * P:(k % 4) * P + P], h2[:, k, w * P:w * P + P], ident)
            mm.then_inc(ev("router_products"), 1)
            pe.wait_ge(ev("router_steps"), 1 + 1)
            for w in range(2):
                mm = pe.transpose(ps[0:16, 3, 128 + w * P:128 + w * P + P], aff[:, w, :], ident)
            mm.then_inc(ev("router_products"), 1)
            pe.wait_ge(ev("gain7"), 1)
            for n in range(6):
                if n >= 3:
                    pe.wait_ge(ev("tok_copied"), n - 2)
                for m in range(4):
                    k = (n % 2) * 4 + m
                    o = ps[:, n % 3, m * P:m * P + P]
                    if n < 4:
                        mm = pe.transpose(o, hT[:, k, (n // 2) * P:(n // 2) * P + P], ident)
                    else:
                        mm = pe.matmul(o, small[:, 152 + k:153 + k].to_broadcast([P, P]), ident, start=True, stop=True)
                mm.then_inc(ev("tok_turned"), 1)
            pe.wait_ge(ev("h2tok_copied"), 4)
            pe.wait_ge(ev("zeros"), 1)
            zeros = uT[:].rearrange("p a b -> p (a b)")[:, 0:512]
            for b in range(4):
                pe.matmul(ps[:, 4 + b, :], ident, zeros, start=True, stop=False, skip_group_check=True)
            pe.wait_ge(ev("router_steps"), 2 + 1)
            for w in range(2):
                mm = pe.transpose(ps[:, 3, w * 16:w * 16 + 16], rtk[0:16, 3, w * P:w * P + P], ident[0:16, 0:16])
            mm.then_inc(ev("router_products"), 1)
            pe.wait_ge(ev("sel_ready"), 1)
            pe.wait_ge(ev("tok_copied"), 6)
            with pe.Fori(0, NE) as e:
                pe.wait_ge(ev("sg4_ready"), e + 1)
                for k in range(KT):
                    group([(h2tok[:, w, k * P:k * P + P], sel[:, w, e, :]) for w in range(2)], ps[:, 3, k * CAP:k * CAP + CAP])
                for w in range(2):
                    mm = pe.transpose(ps[:, 3, 256 + w * P:256 + w * P + P], sg4[:, w].rearrange("p j s -> p (j s)"), ident)
                mm.then_inc(ev("gathered"), 1)
                pe.wait_ge(ev("xs_ready"), e + 1)
                for half in range(2):
                    for i in range(4):
                        s = (4 * half + i) % RING
                        pe.wait_ge(ev(f"slot{s}_loaded"), e * 32 + (slot_count[s] + 16 * (1 + (4 * half + i) // RING)))
                        w = ring[:, s, :].rearrange("p (k c) -> p k c", k=2)
                        for k in range(2):
                            for j in range(4):
                                kt = 2 * i + k
                                mm = pe.matmul(ps[32 * j:32 * j + 32, half, :], xs[:, kt, :], w[:, k, 512 * j:512 * j + 512],
                                               start=kt == 0, stop=kt == KT - 1)
                        mm.then_inc(ev("units_used"), 1)
                pe.wait_ge(ev("hidden"), e + 1)
                for b in range(4):
                    mm = pe.transpose(ps[:, 2, b * P:b * P + P], he[:, b * P:b * P + P], ident)
                mm.then_inc(ev("hidden_turned"), 1)
                pe.wait_ge(ev("heT_ready"), e + 1)
                for i in range(4):
                    s = (8 + i) % RING
                    pe.wait_ge(ev(f"slot{s}_loaded"), e * 32 + (slot_count[s] + 16 * (1 + (8 + i) // RING)))
                    w = ring[:, s, :].rearrange("p (j c) -> p j c", j=4)
                    for half in range(2):
                        for j in range(4):
                            mm = pe.matmul(ps[32 * j:32 * j + 32, half, :], heT[:, i, 32 * j:32 * j + 32], w[:, j, 512 * half:512 * half + 512],
                                           start=i == 0, stop=i == 3)
                    mm.then_inc(ev("units_used"), 1)
                pe.wait_ge(ev("y_ready"), e + 1)
                for b in range(4):
                    w, half = divmod(b, 2)
                    mm = pe.matmul(ps[:, 4 + b, :], Gt[:, w * P:w * P + P], ye[:, half * 512:half * 512 + 512], start=False, stop=False, skip_group_check=True)
                mm.then_inc(ev("scattered"), 1)
            for b in range(4):
                mm = pe.matmul(ps[:, 4 + b, 0:2], ident, zeros[:, 0:2], start=False, stop=True, skip_group_check=True)
                mm.then_inc(ev("experts_done"), 1)

        @block.scalar
        def _(act):
            st = Steps(act, ev("act_steps"))

            def evict(name, dst, n, fn, rows=P, **kw):
                act.wait_ge(ev("tiles_done"), TN[name] + 1)
                act.activation(dst, bank_of(name)[0:rows, 0:n], fn, **kw).then_inc(ev("tiles_freed"), 1)

            hi_done = [0]

            def round_weights(upto):
                while hi_done[0] <= CH[upto]:
                    c = hi_done[0]
                    act.wait_ge(slot_ready(chunks[c][0]), ready_at[chunks[c][0]])
                    if c >= HB:
                        act.wait_ge(ev("hi_used"), c - HB + 1)
                    act.activation(r_(rounded(c)), chunks[c][1], ACT.Copy).then_inc(ev("w_hi"), 1)
                    hi_done[0] += 1

            def round_stream(dst, turn):
                for k in range(KT):
                    act.wait_ge(ev("u_full"), KT * turn + k + 1)
                    act.activation(r_(dst[:, k, :]), uT[:, k, :], ACT.Copy).then_inc(ev("u_hi"), 1)

            def root(name, n):
                act.wait_ge(ev("tiles_done"), TN[name] + 1)
                act.activation(bc[:, 0, 0:n], bank_of(name)[:, 0:n], ACT.Sqrt, bias=eps[:]).then_inc(ev("tiles_freed"), 1)
                act.wait_ge(ev("tiles_freed"), TN[name] + 1)
                act.nop().then_inc(ev("root"), 1)

            def load(dst, src, sem, **kw):
                act.dma_start(dst, src, **kw).then_inc(ev(sem), 16)

            def rows(name, src):
                b, r, n = PAR[name]
                n = src.shape[0]
                load(prow[r:r + n, b, :], src, "par2_loaded" if b else "par_loaded")

            def r1(w):
                return w.rearrange("o (k p) -> (o k) p", p=P)

            rows("norm1", r1(a["norm1_w"]))
            rows("lb0", r1(a["hg_lb_logits"][0:1]))
            rows("lb1", r1(a["hg_lb_logits"][1:2]))
            rows("hgn", r1(a["hg_norm_w"]))
            rows("m2cw", r1(a["m2_conv_w"][0]))
            rows("m2cb", r1(a["m2_conv_b"]))
            rows("m2n", r1(a["m2_norm_w"]))
            rows("norm2", r1(a["norm2_w"]))
            rows("c", r1(a["c_2"]))
            rows("cctx", a["c_ctx_2"].rearrange("(k p) -> k p", p=P))
            for k in range(KT):
                act.wait_ge(ev("stream_tiles"), k + 1)
                act.activation(uT[:, k, :], hT[:, k, :], ACT.Square).then_inc(ev("squares"), 1)
            act.wait_ge(ev("par_ready"), 1)
            act.wait_ge(ev("cond_cleared"), 1)
            st(act.activation(cond[:, :, 0], pc("c", 0, 8), ACT.Silu))
            st.link(act.activation(cond[:, :, 1], pc("cctx", 0, 8), ACT.Silu))
            act.nop().then_inc(ev("cond_ready"), 1)
            act.wait_ge(ev("lb_shift"), 1)
            act.activation(small[:, 0:16], small[:, 0:16], ACT.Exp).then_inc(ev("lb_exp"), 1)
            root("n1", T)
            round_weights("p0")
            round_stream(uhi, 0)
            round_weights("p1")

            def conv_silu(t):
                act.wait_ge(ev("m2_conv_sum"), t + 1)
                act.activation(proj[:, TX + t, :], m2_t[:, t % 2, :], ACT.Silu).then_inc(ev("m2_conv"), 1)

            def dt_first():
                act.wait_ge(ev("small_loaded"), 16 * 8)
                evict("dt", ch(1), T, ACT.Identity, rows=16, bias=chan[:, 0, 0:1])
                st.link(act.activation(chan[:, 0, 2:3], chan[:, 0, 1:2], ACT.Exp))
                act.wait_ge(ev("tiles_freed"), TN["dt"] + 1)
                act.nop().then_inc(ev("dt_in"), 1)
                act.wait_ge(ev("dt_abs"), 1)
                act.activation(ch(6), ch(5), ACT.Exp, scale=-1.0).then_inc(ev("dt_exp"), 1)
                act.wait_ge(ev("dt_one"), 1)
                act.activation(ch(8), ch(7), ACT.Ln).then_inc(ev("dt_log"), 1)

            def dt_end():
                act.wait_ge(ev("m2_end"), 1)
                act.activation(ch(3)[:, 0:256], ch(4)[:, 0:256], ACT.Exp).then_inc(ev("m2_end_exp"), 1)

            def m2_exp(q):
                act.wait_ge(ev("m2_a"), q + 1)
                if q:
                    act.wait_ge(ev("m2_y"), 2 * q)
                act.activation(m2C[:, :, 0:128], ps[:, 5, :].rearrange("p (h t) -> p h t", h=4), ACT.Exp).then_inc(ev("m2_ea"), 1)
                act.activation(m2C[:, :, 128:144], ps[:, 7, 0:64].rearrange("p (h t) -> p h t", h=4), ACT.Exp).then_inc(ev("m2_ea"), 1)
                for w, buf in enumerate((m2P0, m2P1, m2P2)):
                    act.wait_ge(ev("m2_seg"), 3 * q + w + 1)
                    act.activation(buf, buf, ACT.Exp).then_inc(ev("m2_seg_exp"), 1)

            def hg_log(h):
                act.wait_ge(ev("hg_f"), h + 1)
                act.activation(hg_lf, hg_f, ACT.Ln).then_inc(ev("hg_log"), 1)

            def hg_exps(h):
                b = h % 2
                act.wait_ge(ev("hg_b"), h + 1)
                st(act.activation(hg_K0[:, b], hg_B[:, b, 0, :], ACT.Exp, scale=-1.0))
                st.link(act.activation(hg_D[:, b], hg_D[:, b], ACT.Exp))
                act.activation(hg_B[:, b], hg_B[:, b], ACT.Exp).then_inc(ev("hg_exp"), 1)

            def hg_keys(h):
                act.wait_ge(ev("hg_turned"), h + 1)
                act.activation(hg_ke, ps[:, 7, 0:256].rearrange("p (w c) -> p w c", w=2), ACT.Copy).then_inc(ev("hg_ke"), 1)

            def hgrn(j):
                h = (j - 32) // 3
                if (j - 32) % 3 == 0 and 1 <= h <= HEADS:
                    act.wait_ge(ev("hg_head"), h)
                    act.activation(r_(proj[:, TF_ + h - 1, :]), proj[:, TQ + h - 1, :], ACT.Copy).then_inc(ev("hg_hi"), 1)
                if j < 32 or h >= HEADS:
                    return
                if (j - 32) % 3 == 0:
                    hg_keys(h)
                    if h + 1 < HEADS:
                        hg_log(h + 1)
                    if h + 1 < HEADS:
                        hg_exps(h + 1)
                if (j - 32) % 3 == 1:
                    act.wait_ge(ev("hg_out"), h + 1)
                    act.activation(hg_sq, ps[:, 6, 0:T], ACT.Square).then_inc(ev("hg_squared"), 1)
                if (j - 32) % 3 == 2:
                    act.wait_ge(ev("hg_mean"), h + 1)
                    act.activation(hg_lf, ps[:, 7, 0:T], ACT.Sqrt, bias=eps[:]).then_inc(ev("hg_root"), 1)

            def m2_round(g):
                act.wait_ge(ev("m2_full"), g + 1)
                act.activation(r_(proj[:, TX + 4 * g:TX + 4 * g + 4, :]), proj[:, TZ + 4 * g:TZ + 4 * g + 4, :], ACT.Copy).then_inc(ev("m2_hi"), 1)

            def gate_squares(g):
                act.wait_ge(ev("m2_gated"), g + 1)
                for k in range(4):
                    act.activation(proj[:, TX + 4 * g + k, :], proj[:, TZ + 4 * g + k, :], ACT.Square).then_inc(ev("squares"), 1)

            for j in range(NPROJ):
                n, m = divmod(j, 4)
                round_weights(f"p{j + 2}" if j + 2 < NPROJ else f"ob{j + 2 - NPROJ}")
                if 2 <= j <= 13:
                    conv_silu(j - 2)
                if j == 12:
                    dt_first()
                if j == 14:
                    dt_end()
                if j in (19, 21, 26, 28):
                    m2_exp((19, 21, 26, 28).index(j))
                if j == 30:
                    hg_log(0)
                    hg_exps(0)
                hgrn(j)
                if j == 49:
                    gate_squares(0)
                if j == 50:
                    root("mz0", T)
                unit_ = ORDER[n]
                fn = {0: ACT.Silu, 1: ACT.Sigmoid, 2: ACT.Copy, 3: ACT.Silu, 4: ACT.Silu}.get(unit_ // 2, ACT.Copy)
                evict(f"p{j}", proj[:, 4 * unit_ + m, :], T, fn)
                act.wait_ge(ev("tiles_freed"), TN[f"p{j}"] + 1)
                act.nop().then_inc(ev("proj_tiles"), 1)
            m2_round(0)
            gate_squares(1)
            round_weights("ob2")
            act.wait_ge(ev("mz1_done"), 1)
            act.activation(bc[:, 0, 0:T], ps[:, 3, 0:T], ACT.Sqrt, bias=eps[:]).then_inc(ev("root"), 1)
            m2_round(1)
            hgrn(52)
            for j in range(53, 57):
                round_weights(f"ob{j - 50}")
                hgrn(j)
            round_weights("ob7")
            for k in range(KT):
                round_weights(f"oa{k}")
            for k in range(KT):
                act.wait_ge(ev("stream_tiles"), 2 * KT + k + 1)
                act.activation(uT[:, k, :], hT[:, k, :], ACT.Square).then_inc(ev("squares"), 1)
            root("n2", T)
            round_weights("f1")
            act.wait_ge(ev("out_done"), 1)
            round_stream(uhi2, 1)
            def act_round(i):
                act.wait_ge(ev("act_full"), i + 1)
                act.activation(r_(act_hi[:, i, :]), act_[:, i, :], ACT.Copy).then_inc(ev("act_hi"), 1)

            for i in range(FT):
                for s in range(2):
                    m = s * FT + i
                    round_weights((f"f{2 * i + s + 2}", f"d0.{s}")[i == FT - 1])
                    act.wait_ge(ev("tiles_done"), TN[f"f{2 * i + s}"] + 1)
                    if i >= 2:
                        act.wait_ge(ev("act_full"), i - 1)
                    act.activation(fc[:, i % 2, s, :], bank_of(f"f{2 * i + s}")[:, 0:T], ACT.Identity, scale=pc("ffw2", m),
                                   bias=pc("ffb", m)).then_inc(ev("ffn_tap"), 1)
                act.wait_ge(ev("ffn_conv"), 2 * i + 1)
                act.activation(fc[:, i % 2, 0, :], fc[:, i % 2, 0, :], ACT.Silu).then_inc(ev("ffn_silu"), 1)
                if i:
                    act_round(i - 1)
                if i == 17:
                    act.wait_ge(ev("ctx_copied"), 4)
                    act.activation(hx[:, :, 0:L], hx[:, :, L:2 * L], ACT.Square).then_inc(ev("ctx_squared"), 1)
                if i == 18:
                    act.wait_ge(ev("ctx_mean"), 1)
                    act.activation(bc[:, 0, L:2 * L], ps[:, 6, 0:L], ACT.Sqrt, bias=eps[:]).then_inc(ev("ctx_root"), 1)
                if i == 19:
                    act.wait_ge(ev("lg_abs"), 1)
                    act.activation(small[:, 40:48], small[:, 32:40], ACT.Exp, scale=-1.0).then_inc(ev("lg_exp"), 1)
                    act.wait_ge(ev("lg_one"), 1)
                    act.activation(small[:, 56:64], small[:, 48:56], ACT.Ln).then_inc(ev("lg_log"), 1)
            act_round(FT - 1)
            round_weights("d0.2")
            for k in range(KT):
                if k < KT - 1:
                    round_weights(f"d{k + 1}.1")
                act.wait_ge(ev("stream_tiles"), 3 * KT + k + 1)
                act.activation(uT[:, k, :], hT[:, k, :], ACT.Square).then_inc(ev("squares"), 1)
                if k < KT - 1:
                    round_weights(f"d{k + 1}.2")
            root("n3", T)
            act.activation(r_(hxhi[:, :, L:2 * L]), hx[:, :, L:2 * L], ACT.Copy).then_inc(ev("u_hi"), 1)
            round_weights("q1")
            for k in range(KT):
                act.wait_ge(ev("x_tiles"), k + 1)
                act.activation(uT[:, k, 0:L], hT[:, k, 0:L], ACT.Square).then_inc(ev("squares"), 1)
            root("n4", L)
            for k in range(KT):
                act.wait_ge(ev("mod_scaled"), k + 1)
                act.activation(r_(hxhi[:, k, 0:L]), hx[:, k, 0:L], ACT.Identity, bias=mod[:, k, 0:1]).then_inc(ev("u_hi"), 1)

            def ret_powers(h):
                act.wait_ge(ev("ret_arg"), h + 1)
                st(act.activation(rD[:, h % 2, 0:2, :], rD[:, h % 2, 0:2, :], ACT.Exp))
                st(act.activation(rD[:, h % 2, 2:4, :], dist[:, 4:6, :], ACT.Exp, scale=small[:, 80 + h:81 + h]))
                st.link(act.activation(rr[:, 0, :], dist[:, 6:8, :].rearrange("p a b -> p (a b)"), ACT.Exp, scale=small[:, 84 + h:85 + h]))
                act.nop().then_inc(ev("ret_pow"), 1)

            def ret_square(h):
                act.wait_ge(ev("ret_centred"), h + 1)
                act.activation(rr[:, 1, 0:L], ry[:, h, :], ACT.Square).then_inc(ev("ret_sq"), 1)

            def ret_root(h):
                act.wait_ge(ev("ret_mean"), 2 * h + 2)
                if h:
                    act.wait_ge(ev("ret_normed"), h)
                act.activation(bc[:, 0, 0:L], ps[:, 3, 0:L], ACT.Sqrt, bias=eps[:]).then_inc(ev("ret_mean_read"), 1)
                act.wait_ge(ev("ret_mean_read"), 2 * h + 2)
                act.nop().then_inc(ev("ret_root"), 1)

            for r in range(28):
                n, m = divmod(r, 4)
                width = 2 * L if n in (1, 2) else L
                dst = (pq, pk, pv, pcg, pu, pg, pb)[n][:, m, :]
                round_weights(f"q{min(r + 2, 27)}")
                evict(f"q{r}", dst, width, ACT.Silu if n == 5 else ACT.Copy)
                act.wait_ge(ev("tiles_freed"), TN[f"q{r}"] + 1)
                act.nop().then_inc(ev("qk_copied" if n < 2 else "v_copied" if n == 2 else "cgx_copied"), 1)
                if r == 13:
                    ret_powers(0)
                if r in (16, 19, 22):
                    ret_powers((r - 16) // 3 + 1)
                if r in (17, 20, 23, 26):
                    ret_square((r - 17) // 3)
                if r in (18, 21, 24, 27):
                    ret_root((r - 18) // 3)
            for k in range(KT):
                act.wait_ge(ev("mx_tiles"), k + 1)
                act.activation(uT[:, k, 0:L], mx[:, k, :], ACT.Square).then_inc(ev("squares"), 1)
            root("n5", L)
            for k in range(KT):
                act.wait_ge(ev("x_tiles"), KT + k + 1)
                act.activation(uT[:, k, 0:L], hT[:, k, 0:L], ACT.Square).then_inc(ev("squares"), 1)
            root("n6", L)
            for k in range(KT):
                act.wait_ge(ev("mod_scaled"), KT + k + 1)
                act.activation(h2[:, k, :], h2[:, k, :], ACT.Identity, bias=mod[:, 24 + k, 0:1]).then_inc(ev("mod_tiles"), 1)
            act.wait_ge(ev("router_steps"), 1)
            act.activation(aff[:], aff[:], ACT.Exp).then_inc(ev("soft_exp"), 1)
            act.wait_ge(ev("router_products"), 1 + 1)
            for i in range(4):
                act.activation(h2tok[:, i // 2, (i % 2) * 512:(i % 2) * 512 + 512], ps[:, 4 + i, :], ACT.Copy).then_inc(ev("h2tok_copied"), 1)
            for n in range(6):
                dst = otok[:, n // 2, (n % 2) * 512:(n % 2) * 512 + 512] if n < 4 else gtok[:, (n - 4) * 512:(n - 4) * 512 + 512]
                act.wait_ge(ev("tok_turned"), n + 1)
                act.activation(dst, ps[:, n % 3, :], ACT.Copy).then_inc(ev("tok_copied"), 1)
            with act.Fori(0, NE) as e:
                act.wait_ge(ev("units_used"), e * 12 + (U0 + 4))
                act.activation(sa, ps[:, 0, :], ACT.Silu).then_inc(ev("gate_silu"), 1)
                act.wait_ge(ev("hidden_turned"), e + 1)
                act.activation(heT[:], ps[:, 2, :].rearrange("p (b c) -> p b c", b=4), ACT.Copy).then_inc(ev("heT_ready"), 1)
                act.wait_ge(ev("units_used"), e * 12 + (U0 + 12))
                act.activation(ye[:, 0:512], ps[:, 0, :], ACT.Copy).then_inc(ev("y_half"), 1)
            for w in range(2):
                act.wait_ge(ev("experts_done"), 2 * w + 2)
                if w:
                    act.wait_ge(ev("y_squared"), 1)
                act.activation(ysq.rearrange("p (a b) -> p a b", a=2), ps[:, 4 + 2 * w:6 + 2 * w, :], ACT.Square,
                               accum_out=small[:, 200 + w:201 + w]).then_inc(ev("y_squared"), 1)
                act.wait_ge(ev("y_squared"), w + 1)
                act.activation(small[:, 202 + w:203 + w], small[:, 200 + w:201 + w], ACT.Sqrt, scale=1.0 / D, bias=eps[:]).then_inc(ev("y_root"), 1)

        @block.gpsimd
        def _(pool):
            for c, (_, w) in enumerate(chunks):
                pool.wait_ge(ev("w_hi"), c + 1)
                pool.tensor_tensor(r_(w), w, f_(rounded(c)), ALU.subtract).then_inc(ev("w_lo"), 1)

        @block.vector
        def _(dve):
            st = Steps(dve, ev("dve_steps"))
            tt, ts, stt = dve.tensor_tensor, dve.tensor_scalar, dve.scalar_tensor_tensor
            roots = [0]

            def inverse_root(n):
                roots[0] += 1
                dve.wait_ge(ev("root"), roots[0])
                st.link(dve.reciprocal(bc[:, 1, 0:n], bc[:, 0, 0:n]))

            st(dve.memset(ones[:], 1.0 / D))
            st(dve.memset(ones4[:], 1.0 / 512))
            st(dve.memset(ones1[:], 1.0 / P))
            st(dve.memset(eps[:], 1e-6))
            st.wait()
            dve.memset(cond[:], 0.0).then_inc(ev("cond_cleared"), 1)
            for k in range(KT):
                dve.wait_ge(ev("tiles_done"), k + 1)
                dve.tensor_copy(hT[:, k, :], bank_of(f"x{k}")[:, 0:T]).then_inc(ev("tiles_freed"), 1)
                dve.wait_ge(ev("tiles_freed"), k + 1)
                dve.nop().then_inc(ev("stream_tiles"), 1)
            dve.wait_ge(ev("par_turned"), 1)
            dve.tensor_copy(par[:, 0:PAR_ROWS[0]], ps[:, 3, 0:PAR_ROWS[0]]).then_inc(ev("par_ready"), 1)
            dve.wait_ge(ev("par_ready"), 1)
            st.link(tt(small[:, 16:24], pc("lb0", 0, 8), pc("lb1", 0, 8), ALU.max))
            st(tt(small[:, 0:8], pc("lb0", 0, 8), small[:, 16:24], ALU.subtract))
            st.link(tt(small[:, 8:16], pc("lb1", 0, 8), small[:, 16:24], ALU.subtract))
            dve.nop().then_inc(ev("lb_shift"), 1)
            dve.wait_ge(ev("lb_exp"), 1)
            st.link(tt(small[:, 16:24], small[:, 0:8], small[:, 8:16], ALU.add))
            st.link(dve.reciprocal(small[:, 24:32], small[:, 16:24]))
            lb, oml = small[:, 96:104], small[:, 104:112]
            st.link(tt(lb, small[:, 0:8], small[:, 24:32], ALU.mult))
            st.link(ts(oml, lb, -1.0, 1.0, ALU.mult, ALU.add))

            def normed(name, turn, hi):
                inverse_root(T)
                for k in range(KT + 1):
                    if k < KT:
                        stt(uT[:, k, :], hT[:, k, :], pc(name, k), bc[:, 1, 0:T], ALU.mult, ALU.mult).then_inc(ev("u_full"), 1)
                    if k:
                        dve.wait_ge(ev("u_hi"), KT * turn + k)
                        tt(r_(uT[:, k - 1, :]), uT[:, k - 1, :], f_(hi[:, k - 1, :]), ALU.subtract).then_inc(ev("u_tiles"), 1)

            normed("norm1", 0, uhi)

            def mod_row(n):
                dve.wait_ge(ev("units_used"), 2 * n + 2)
                dve.tensor_copy(mrow, ps[:, 3, :]).then_inc(ev("mod_row"), 1)

            def mod_add(n):
                dve.wait_ge(ev("mod_turned"), n + 1)
                tt(mod[:, 4 * n:4 * n + 4, :], ps[:, 3, 0:8].rearrange("p (b c) -> p b c", c=2),
                   pc("bada", 4 * n, 4).unsqueeze(2).to_broadcast([P, 4, 2]), ALU.add).then_inc(ev("mod_done"), 1)

            def conv(t):
                dve.wait_ge(ev("proj_tiles"), t + 1)
                x, o = proj[:, TX + t, :], m2_t[:, t % 2, :]
                if t == 0:
                    dve.wait_ge(ev("tiles_done"), TN["n1"] + 1)
                if t >= 2:
                    dve.wait_ge(ev("m2_conv"), t - 1)
                st.link(ts(o, x, pc("m2cw", 36 + t), pc("m2cb", t), ALU.mult, ALU.add))
                for s in (1, 2, 3):
                    ins = stt(o[:, s:T], x[:, 0:T - s], pc("m2cw", 12 * (3 - s) + t), o[:, s:T], ALU.mult, ALU.add)
                    if s < 3:
                        st.link(ins)
                ins.then_inc(ev("m2_conv_sum"), 1)

            def log1p_of_exp(u, e, one, lg, tmp, ev_abs, ev_exp, ev_one, ev_log):
                st.link(stt(tmp, u, -1.0, u, ALU.mult, ALU.max))
                dve.nop().then_inc(ev(ev_abs), 1)
                dve.wait_ge(ev(ev_exp), 1)
                st.link(ts(one, e, 1.0, None, ALU.add))
                dve.nop().then_inc(ev(ev_one), 1)
                dve.wait_ge(ev(ev_log), 1)
                st.link(tt(lg, lg, e, ALU.mult))
                st.link(ts(tmp, one, -1.0, 1e-30, ALU.add, ALU.max))
                st.link(dve.reciprocal(tmp, tmp))
                st.link(tt(lg, lg, tmp, ALU.mult))
                st.link(ts(tmp, one, 1.0, None, ALU.is_equal))
                st.link(tt(tmp, tmp, e, ALU.mult))
                st.link(tt(lg, lg, tmp, ALU.add))

            def dt_rows():
                dve.wait_ge(ev("dt_in"), 1)
                log1p_of_exp(ch(1), ch(6), ch(7), ch(8), ch(5), "dt_abs", "dt_exp", "dt_one", "dt_log")
                st.link(stt(ch(1), ch(1), 0.0, ch(8), ALU.max, ALU.add))
                st.link(ts(ch(4), ch(1), chan[:, 0, 2:3], -1.0, ALU.mult, ALU.mult))
                st.link(dve.tensor_tensor_scan(ch(0), cs("reset", 16)[:, 3 * T:4 * T], ch(4), 0.0, ALU.mult, ALU.add))
                for w in range(2):
                    s = slice(w * P, w * P + P)
                    st(tt(ch(4)[:, s], ch(0)[:, w * P + 127:w * P + 128].to_broadcast([16, P]), ch(0)[:, s], ALU.subtract))
                st(dve.memset(ch(3)[:, 256:T], 1.0))
                st.wait()
                dve.nop().then_inc(ev("m2_end"), 1)
                dve.wait_ge(ev("m2_end_exp"), 1)
                dve.nop().then_inc(ev("m2_rows"), 1)

            def m2_tokens():
                dve.wait_ge(ev("m2_rows_turned"), 1)
                pr = ps[:, 4, 0:144].rearrange("p (w i h) -> p w i h", w=3, i=3)
                st(dve.tensor_copy(tkq[:, 0:2], pr[:, 0:2]))
                st(dve.tensor_copy(tkq[0:16, 2], pr[0:16, 2]))
                st.wait()
                dve.nop().then_inc(ev("m2_tk"), 1)

            def m2_stage(g):
                dve.wait_ge(ev("m2_turned"), g + 1)
                hs = slice(8 * g, 8 * g + 8)
                for w, (t0, n) in enumerate(WINDOWS):
                    st(tt(m2_x[0:n, w, :].rearrange("p (h c) -> p h c", h=8), ps[0:n, 4 + w, :].rearrange("p (h c) -> p h c", h=8),
                          tkq[0:n, w, 0, hs].unsqueeze(2).to_broadcast([n, 8, 64]), ALU.mult))
                st(dve.tensor_copy(m2_b, ps[:, 7, 0:256].rearrange("p (w c) -> p w c", w=2)))
                st.wait()
                for w in range(2):
                    st(tt(m2_xe[:, w, :].rearrange("p (h c) -> p h c", h=8), m2_x[:, w, :].rearrange("p (h c) -> p h c", h=8),
                          tkq[:, w, 2, hs].unsqueeze(2).to_broadcast([P, 8, 64]), ALU.mult))
                st.wait()
                dve.nop().then_inc(ev("m2_staged"), 1)

            def m2_masks(g):
                dve.wait_ge(ev("m2_update"), g + 1)
                st(tt(m2_cb, ps[:, 4, 0:256].rearrange("p (w c) -> p w c", w=2),
                      cs("causal").unsqueeze(1).to_broadcast([P, 2, P]), ALU.mult))
                st(tt(m2_cb2[0:16], ps[0:16, 5, 0:16], cs("causal", 16)[:, 0:16], ALU.mult))
                for w in range(2):
                    st(dve.tensor_copy(m2_S[:, w, :], ps[:, 6 + w, :]))
                st.wait()
                dve.nop().then_inc(ev("m2_group"), 1)

            def m2_scores(q):
                g = q // 2
                dve.wait_ge(ev("m2_a"), q + 1)
                if q:
                    dve.wait_ge(ev("m2_y"), 2 * q)
                bufs = ((m2P0, P), (m2P1, P), (m2P2, 16))
                for w, (buf, n) in enumerate(bufs):
                    if w:
                        dve.wait_ge(ev("m2_ea"), 2 * q + w)
                    st.link(tt(buf, ps[0:n, (4, 5, 7)[w], 0:4 * n].rearrange("p (h t) -> p h t", h=4),
                               tkq[0:n, w, 1, 4 * q:4 * q + 4].unsqueeze(2).to_broadcast([n, 4, n]), ALU.subtract))
                    ts(buf, buf, 0.0, None, ALU.min).then_inc(ev("m2_seg"), 1)
                hs = slice(256 * (q % 2), 256 * (q % 2) + 256)
                s0 = m2_S[:, 0, hs].rearrange("p (h c) -> p h c", h=4)
                s1 = m2_S[:, 1, hs].rearrange("p (h c) -> p h c", h=4)
                tmp = m2_seg.rearrange("p (h c) -> p h c", h=4)
                st.link(tt(tmp, s0, m2C[:, :, 127:128].to_broadcast([P, 4, 64]), ALU.mult))
                st.link(tt(s1, s1, tmp, ALU.add))
                st(tt(m2C, m2C, proj[:, TCM + g, 128:T].unsqueeze(1).to_broadcast([P, 4, 144]), ALU.mult))
                for w, (buf, n) in enumerate(bufs):
                    dve.wait_ge(ev("m2_seg_exp"), 3 * q + w + 1)
                    cb = m2_cb[:, w, :] if w < 2 else m2_cb2[0:16]
                    st(tt(buf, buf, cb.unsqueeze(1).to_broadcast([n, 4, n]), ALU.mult))
                st.wait()
                dve.nop().then_inc(ev("m2_pc"), 1)

            def m2_outputs(q):
                for pair in range(2):
                    c = 2 * q + pair
                    dve.wait_ge(ev("m2_y"), c + 1)
                    stt(proj[:, TX + c, :], proj[:, TX + c, :], bcast8[:, c:c + 1], ps[:, 6 + pair, 0:T], ALU.mult, ALU.add).then_inc(ev("m2_out"), 1)

            def m2_gate(g):
                dve.wait_ge(ev("m2_out"), 8)
                dve.wait_ge(ev("proj_tiles"), 48 + 4 * g)
                z = proj[:, TZ + 4 * g:TZ + 4 * g + 4, :]
                tt(z, z, proj[:, TX + 4 * g:TX + 4 * g + 4, :], ALU.mult).then_inc(ev("m2_gated"), 1)

            def m2_norm(g):
                inverse_root(T)
                dve.wait_ge(ev("m2_gated"), g + 1)
                for k in range(4):
                    m = TZ + 4 * g + k
                    st(stt(proj[:, m, :], proj[:, m, :], pc("m2n", 4 * g + k), bc[:, 1, 0:T], ALU.mult, ALU.mult))
                st.wait()
                dve.nop().then_inc(ev("m2_full"), 1)

            def m2_rest(g):
                dve.wait_ge(ev("m2_hi"), g + 1)
                z = proj[:, TZ + 4 * g:TZ + 4 * g + 4, :]
                tt(r_(z), z, f_(proj[:, TX + 4 * g:TX + 4 * g + 4, :]), ALU.subtract).then_inc(ev("m2_normed"), 1)

            reset = cs("reset").rearrange("p (l t) -> p l t", l=4)
            mask = cs("mask").bitcast(U32).rearrange("p (l r) -> p l r", l=4)

            def hg_cumulate(h):
                b = h % 2
                dve.wait_ge(ev("proj_tiles"), 16 if h < 4 else 32)
                st.link(ts(hg_f, proj[:, h + TF_, :], oml[:, h:h + 1], lb[:, h:h + 1], ALU.mult, ALU.add))
                dve.nop().then_inc(ev("hg_f"), 1)
                st(ts(hg_k, hg_f, -1.0, 1.0, ALU.mult, ALU.add))
                dve.wait_ge(ev("hg_log"), h + 1)
                for l in range(4):
                    st(dve.tensor_tensor_scan(hg_B[:, b, l, :], reset[:, l, :], hg_lf, 0.0, ALU.mult, ALU.add))
                st.wait()
                for l, w in enumerate(LEVELS):
                    B = hg_B[:, b, l, 0:256].rearrange("p (c w) -> p c w", w=w)
                    st(tt(hg_D[:, b, l, :].rearrange("p (c w) -> p c w", w=w),
                          B[:, :, w - 1:w].to_broadcast([P, 256 // w, w]), B, ALU.subtract))
                st.wait()
                dve.nop().then_inc(ev("hg_b"), 1)

            def hg_decay(h):
                b = h % 2
                dve.wait_ge(ev("hg_exp"), h + 1)
                st(dve.tensor_copy(small[:, 120 + b:121 + b], hg_B[:, b, 3, 255:256]))
                st(tt(hg_K0[:, b], hg_K0[:, b], hg_k, ALU.mult))
                st(tt(hg_D[:, b], hg_D[:, b], hg_k[:, 0:256].unsqueeze(1).to_broadcast([P, 4, 256]), ALU.mult))
                st.wait()
                dve.wait_ge(ev("proj_tiles"), 24 if h < 4 else 40)
                st.link(tt(hg_B[:, b], hg_B[:, b], proj[:, h + TQ, :].unsqueeze(1).to_broadcast([P, 4, T]), ALU.mult))
                dve.nop().then_inc(ev("hg_staged"), 1)

            def hg_values(h):
                dve.wait_ge(ev("hg_turned"), h + 1)
                st(dve.tensor_copy(hg_v[:, 0:2, :], ps[:, 6, 0:256].rearrange("p (w c) -> p w c", w=2)))
                st(dve.tensor_copy(hg_v[0:16, 2, :], ps[0:16, 6, 256:384]))
                st.wait()
                dve.nop().then_inc(ev("hg_v"), 1)

            def hg_mask(h):
                dve.wait_ge(ev("hg_scores"), h + 1)
                for l in range(4):
                    st.link(dve.copy_predicated(hg_P, mask[:, l, :].unsqueeze(1).to_broadcast([P, 2, P]),
                                                ps[:, 4 + l // 2, (l % 2) * 256:(l % 2) * 256 + 256].rearrange("p (w r) -> p w r", w=2)))
                st.link(dve.copy_predicated(hg_P2[0:16, :], mask[0:16, 0, 0:16], ps[0:16, 6, 384:400]))

            def hg_states(h):
                dve.wait_ge(ev("hg_update"), h + 1)
                st.link(dve.tensor_copy(hg_S[:, 0, :], ps[:, 7, 0:128]))
                st.link(stt(hg_S[:, 1, :], hg_S[:, 0, :], small[:, 120 + h % 2:121 + h % 2], ps[:, 7, 128:256], ALU.mult, ALU.add))
                dve.nop().then_inc(ev("hg_masked"), 1)

            def hg_finish(h):
                dve.wait_ge(ev("hg_root"), h + 1)
                dve.wait_ge(ev("proj_tiles"), 28 if h < 4 else 44)
                st.link(dve.reciprocal(hg_f, hg_lf))
                st.link(stt(hg_o, ps[:, 6, 0:T], pc("hgn", h), hg_f, ALU.mult, ALU.mult))
                tt(proj[:, h + TQ, :], hg_o, proj[:, h + TG, :], ALU.mult).then_inc(ev("hg_head"), 1)
                dve.wait_ge(ev("hg_head"), h + 1)

            def hgrn(j):
                h = (j - 32) // 3
                if (j - 32) % 3 == 0 and 1 <= h <= HEADS:
                    dve.wait_ge(ev("hg_hi"), h)
                    tt(r_(proj[:, TQ + h - 1, :]), proj[:, TQ + h - 1, :], f_(proj[:, TF_ + h - 1, :]), ALU.subtract).then_inc(ev("hg_lo"), 1)
                if j < 32 or h >= HEADS:
                    return
                if (j - 32) % 3 == 0:
                    hg_values(h)
                    hg_mask(h)
                    if h + 1 < HEADS:
                        hg_cumulate(h + 1)
                if (j - 32) % 3 == 1:
                    hg_states(h)
                    if j == 51:
                        m2_norm(0)
                    if h + 1 < HEADS:
                        hg_decay(h + 1)
                if (j - 32) % 3 == 2:
                    hg_finish(h)

            for j in range(NPROJ):
                n, m = divmod(j, 4)
                if 1 <= j <= 12:
                    conv(j - 1)
                if m == 0 and n:
                    mod_row(n - 1)
                if m == 3 and n:
                    mod_add(n - 1)
                if j == 4:
                    dve.wait_ge(ev("par_turned"), 2)
                    for b in (1, 2, 3):
                        st(dve.tensor_copy(par[:, b * P:b * P + PAR_ROWS[b]], ps[:, 4, b * P:b * P + PAR_ROWS[b]]))
                    st.wait()
                if j == 12:
                    dt_rows()
                if j == 16:
                    m2_tokens()
                if j in (17, 24):
                    m2_stage((17, 24).index(j))
                if j in (18, 25):
                    m2_masks((18, 25).index(j))
                if j in (21, 23, 28, 30):
                    m2_outputs((21, 23, 28, 30).index(j))
                if j in (19, 21, 26, 28):
                    m2_scores((19, 21, 26, 28).index(j))
                if j == 30:
                    dve.wait_ge(ev("m2_out"), 8)
                    st(dve.memset(hg_P, 0.0))
                    st.link(dve.memset(hg_P2, 0.0))
                    hg_cumulate(0)
                    hg_decay(0)
                hgrn(j)
                if j == 48:
                    m2_gate(0)
            m2_rest(0)
            m2_gate(1)
            m2_norm(1)
            m2_rest(1)
            hgrn(52)

            def add_tile(name, k, n=T):
                dve.wait_ge(ev("tiles_done"), TN[name] + 1)
                if name == "ob0":
                    dve.wait_ge(ev("tiles_freed"), TN[name])
                tt(hT[:, k, 0:n], hT[:, k, 0:n], bank_of(name)[:, 0:n], ALU.add).then_inc(ev("tiles_freed"), 1)
                dve.wait_ge(ev("tiles_freed"), TN[name] + 1)
                dve.nop().then_inc(ev("stream_tiles"), 1)

            for k in range(KT):
                if 1 <= k <= 5:
                    hgrn(52 + k)
                add_tile(f"ob{k}", k)
            for k in range(KT):
                add_tile(f"oa{k}", k)
            normed("norm2", 1, uhi2)
            gain = small[:, 128:144].rearrange("p (k c) -> p k c", c=2)

            def act_rest(i):
                dve.wait_ge(ev("act_hi"), i + 1)
                tt(r_(act_[:, i, :]), act_[:, i, :], f_(act_hi[:, i, :]), ALU.subtract).then_inc(ev("ffn_act"), 1)

            for i in range(FT):
                for s in range(2):
                    m = s * FT + i
                    dve.wait_ge(ev("ffn_tap"), 2 * i + s + 1)
                    o, x = fc[:, i % 2, s, :], bank_of(f"f{2 * i + s}")
                    st.link(stt(o[:, 1:T], x[:, 0:T - 1], pc("ffw01", 44 + m), o[:, 1:T], ALU.mult, ALU.add))
                    st.link(stt(o[:, 2:T], x[:, 0:T - 2], pc("ffw01", m), o[:, 2:T], ALU.mult, ALU.add))
                    dve.nop().then_inc(ev("tiles_freed"), 1)
                    dve.nop().then_inc(ev("ffn_conv"), 1)
                dve.wait_ge(ev("ffn_silu"), i + 1)
                tt(act_[:, i, :], fc[:, i % 2, 0, :], fc[:, i % 2, 1, :], ALU.mult).then_inc(ev("act_full"), 1)
                if i:
                    act_rest(i - 1)
                if 14 <= i <= 17:
                    c = i - 14
                    dve.wait_ge(ev("ctx_turned"), c + 1)
                    dve.tensor_copy(hx[:, 2 * c:2 * c + 2, L:2 * L], ps[:, 4 + c % 2, :].rearrange("p (k c) -> p k c", k=2)).then_inc(ev("ctx_copied"), 1)
                if i == 18:
                    for c in range(2):
                        st(stt(gain[:, :, c], mod[:, 8:16, c], 1.0, pc("prem", 0, 8), ALU.add, ALU.mult))
                if i == 19:
                    lgt = bcast8[:, 24:32]
                    log1p_of_exp(lgt, small[:, 40:48], small[:, 48:56], small[:, 56:64], small[:, 32:40], "lg_abs", "lg_exp", "lg_one", "lg_log")
                    st.link(stt(small[:, 80:88], lgt, 0.0, small[:, 56:64], ALU.min, ALU.subtract))
                if i == 20:
                    dve.wait_ge(ev("ctx_root"), 1)
                    st.link(dve.reciprocal(bc[:, 1, L:2 * L], bc[:, 0, L:2 * L]))
                    for k in range(KT):
                        st(stt(hx[:, k, L:2 * L], hx[:, k, L:2 * L], gain[:, k, 1:2], bc[:, 1, L:2 * L], ALU.mult, ALU.mult))
                    st.wait()
                    st.link(tt(hx[:, :, L:2 * L], hx[:, :, L:2 * L], mod[:, 0:8, 1:2].to_broadcast([P, KT, L]), ALU.add))

            act_rest(FT - 1)

            def ret_args(h):
                if h >= 2:
                    dve.wait_ge(ev("ret_p"), h - 1)
                st.link(ts(rD[:, h % 2, 0:2, :], dist[:, 0:2, :], small[:, 80 + h:81 + h], None, ALU.mult))
                st.link(stt(rD[:, h % 2, 0:2, :], dist[:, 2:4, :], small[:, 84 + h:85 + h], rD[:, h % 2, 0:2, :], ALU.mult, ALU.add))
                dve.nop().then_inc(ev("ret_arg"), 1)

            for k in range(KT):
                add_tile(f"d{k}", k)
            inverse_root(T)
            for k in range(KT):
                st.link(stt(hT[:, k, :], hT[:, k, :], pc("fin", k), bc[:, 1, 0:T], ALU.mult, ALU.mult))
                st.link(dve.tensor_copy(uT[:, k, 0:L], hT[:, k, META:T]))
                dve.tensor_copy(hT[:, k, 0:L], uT[:, k, 0:L]).then_inc(ev("x_tiles"), 1)
            inverse_root(L)
            dve.wait_ge(ev("ctx_mean"), 1)
            for k in range(KT + 1):
                if k < KT:
                    stt(hx[:, k, 0:L], hT[:, k, 0:L], gain[:, k, 0:1], bc[:, 1, 0:L], ALU.mult, ALU.mult).then_inc(ev("mod_scaled"), 1)
                if k:
                    dve.wait_ge(ev("u_hi"), 2 * KT + 1 + k)
                    x = hx[:, k - 1, 0:L]
                    stt(r_(x), x, mod[:, k - 1, 0:1], f_(hxhi[:, k - 1, 0:L]), ALU.add, ALU.subtract).then_inc(ev("mod_tiles"), 1)
            x = hx[:, :, L:2 * L]
            tt(r_(x), x, f_(hxhi[:, :, L:2 * L]), ALU.subtract).then_inc(ev("u_tiles"), 1)

            dve.wait_ge(ev("dist_loaded"), 16)
            cos = dist[:, 8:10, :].rearrange("p a b -> p (a b)")
            sin = dist[:, 10:12, :].rearrange("p a b -> p (a b)")

            def rotate(j):
                src, n = (pq[:, j, :], L) if j < RH else (pk[:, j - RH, :], 2 * L)
                dve.wait_ge(ev("rot_done"), j + 1)
                tt(rr[:, 1, 0:n], ps[:, 4 + j % 2, 0:n], sin[:, 0:n], ALU.mult).then_inc(ev("rot_read"), 1)
                st(tt(src, src, cos[:, 0:n], ALU.mult))
                st.wait()
                dve.wait_ge(ev("rot_read"), j + 1)
                tt(src, src, rr[:, 1, 0:n], ALU.add).then_inc(ev("rotated"), 1)
                dve.wait_ge(ev("rotated"), j + 1)

            def turn_v(h):
                dve.wait_ge(ev("v_turned"), h + 1)
                dve.tensor_copy(vtok[:, h], ps[:, 6 + h % 2, :].rearrange("p (t c) -> p t c", t=4)).then_inc(ev("v_turn_copied"), 1)

            def ret_decayed(h):
                b = h % 2
                dve.wait_ge(ev("ret_pow"), h + 1)
                st.link(tt(rD[:, b, 2:4, :], rD[:, b, 2:4, :], rr[:, 0, :].rearrange("p (a b) -> p a b", a=2), ALU.add))
                dve.wait_ge(ev("ret_s"), h + 1)
                if h >= 2:
                    dve.wait_ge(ev("ret_o"), h - 1)
                for i in range(2):
                    st(stt(rP_[:, h % 2][:, 2 * i:2 * i + 2, :], ps[:, 4 + i, :].rearrange("p (a b) -> p a b", a=2), float(P) ** -0.5,
                           rD[:, b, 2 * i:2 * i + 2, :], ALU.mult, ALU.mult))
                st.wait()
                dve.nop().then_inc(ev("ret_p"), 1)

            def ret_output(h):
                dve.wait_ge(ev("ret_o"), h + 1)
                dve.tensor_copy(ry[:, h, :], ps[:, 6 + h % 2, 0:L]).then_inc(ev("ret_y"), 1)

            def ret_centre(h):
                dve.wait_ge(ev("ret_mean"), 2 * h + 1)
                dve.wait_ge(ev("ret_y"), h + 1)
                tt(ry[:, h, :], ry[:, h, :], ps[:, 3, 0:L], ALU.subtract).then_inc(ev("ret_mean_read"), 1)
                dve.wait_ge(ev("ret_mean_read"), 2 * h + 1)
                dve.nop().then_inc(ev("ret_centred"), 1)

            def ret_norm(h):
                dve.wait_ge(ev("ret_root"), h + 1)
                st.link(dve.reciprocal(bc[:, 1, 0:L], bc[:, 0, 0:L]))
                dve.nop().then_inc(ev("ret_normed"), 1)
                st.link(stt(ry[:, h, :], ry[:, h, :], pc("retn", h), bc[:, 1, 0:L], ALU.mult, ALU.mult))

            def ret_gate(h):
                dve.wait_ge(ev("cgx_copied"), 9 + h)
                tt(ry[:, h, :], ry[:, h, :], pg[:, h, :], ALU.mult).then_inc(ev("ret_gated"), 1)

            def conv_rows(k):
                dve.wait_ge(ev("cgx_copied"), 5 + k)
                st.link(tt(pu[:, k, :], pu[:, k, :], pcg[:, k, :], ALU.mult))
                st.link(ts(pcg[:, k, :], pu[:, k, :], pc("cw2", 4 + k), pc("cb2", k), ALU.mult, ALU.add))
                o = pcg[:, k, :].rearrange("p (r c) -> p r c", c=64)
                x = pu[:, k, :].rearrange("p (r c) -> p r c", c=64)
                st.link(stt(o[:, :, 1:64], x[:, :, 0:63], pc("cw2", k), o[:, :, 1:64], ALU.mult, ALU.add))
                st.link(stt(o[:, :, 0:63], x[:, :, 1:64], pc("cw2", 8 + k), o[:, :, 0:63], ALU.mult, ALU.add))

            def conv_gate(k):
                dve.wait_ge(ev("cgx_copied"), 13 + k)
                tt(pcg[:, k, :], pcg[:, k, :], pb[:, k, :], ALU.mult).then_inc(ev("conv_gated"), 1)

            for r in range(28):
                if 6 <= r < 14:
                    rotate(r - 6)
                if r == 13:
                    ret_args(0)
                if r in (13, 14, 15, 16):
                    turn_v(r - 13)
                if r in (15, 18, 21, 24):
                    ret_decayed((r - 15) // 3)
                if r in (16, 19, 22, 25):
                    ret_output((r - 16) // 3)
                    if r < 25:
                        ret_args((r - 16) // 3 + 1)
                if r in (17, 20, 23, 26):
                    ret_centre((r - 17) // 3)
                if 20 <= r < 24:
                    conv_rows(r - 20)
                if 25 <= r < 28:
                    conv_gate(r - 25)
                if r in (18, 21, 24, 27):
                    ret_norm((r - 18) // 3)
                if r == 24:
                    for h in range(3):
                        ret_gate(h)
            ret_gate(3)
            conv_gate(3)
            for k in range(KT):
                dve.wait_ge(ev("tiles_done"), TN[f"w{k}"] + 1)
                if k == 0:
                    dve.wait_ge(ev("tiles_freed"), TN["w0"])
                dve.tensor_copy(mx[:, k, :], bank_of(f"w{k}")[:, 0:L]).then_inc(ev("tiles_freed"), 1)
                dve.wait_ge(ev("tiles_freed"), TN[f"w{k}"] + 1)
                dve.nop().then_inc(ev("mx_tiles"), 1)

            def onto_stream():
                for k in range(KT):
                    st.link(stt(mx[:, k, :], mx[:, k, :], small[:, 128 + k:129 + k], bc[:, 1, 0:L], ALU.mult, ALU.mult))
                    tt(hT[:, k, 0:L], hT[:, k, 0:L], mx[:, k, :], ALU.add).then_inc(ev("x_tiles"), 1)

            st(tt(small[:, 128:136], mod[:, 16:24, 0], pc("postm", 0, 8), ALU.mult))
            st.link(tt(small[:, 152:160], mod[:, 40:48, 0], pc("postf", 0, 8), ALU.mult))
            dve.nop().then_inc(ev("gain7"), 1)
            st(stt(small[:, 144:152], mod[:, 32:40, 0], 1.0, pc("pref", 0, 8), ALU.add, ALU.mult))
            inverse_root(L)
            onto_stream()
            inverse_root(L)
            dve.wait_ge(ev("x_tiles"), KT + KT)
            for k in range(KT):
                stt(h2[:, k, :], hT[:, k, 0:L], small[:, 144 + k:145 + k], bc[:, 1, 0:L], ALU.mult, ALU.mult).then_inc(ev("mod_scaled"), 1)
            dve.wait_ge(ev("router_products"), 1)
            st.link(tt(aff, ps[:, 3, 0:32].rearrange("p (w e) -> p w e", w=2), bcast8[:, 8:24].unsqueeze(1).to_broadcast([P, 2, NE]), ALU.add))
            st.link(dve.tensor_reduce(small[:, 160:162], aff, AX, ALU.max))
            st.link(tt(aff, aff, small[:, 160:162].unsqueeze(2).to_broadcast([P, 2, NE]), ALU.subtract))
            dve.nop().then_inc(ev("router_steps"), 1)
            dve.wait_ge(ev("soft_exp"), 1)
            st.link(dve.tensor_reduce(small[:, 162:164], aff, AX, ALU.add))
            st.link(dve.reciprocal(small[:, 164:166], small[:, 162:164]))
            st.link(tt(aff, aff, small[:, 164:166].unsqueeze(2).to_broadcast([P, 2, NE]), ALU.mult))
            dve.nop().then_inc(ev("router_steps"), 1)
            dve.memset(uT[:], 0.0).then_inc(ev("zeros"), 1)
            dve.wait_ge(ev("router_products"), 2 + 1)
            st.link(dve.tensor_copy(rtk[0:16, 0, :], ps[0:16, 3, 128:384]))
            for i in range(4):
                st.link(dve.max(rtk[0:16, 4, 8 * i:8 * i + 8], rtk[0:16, i % 2, :]))
                st.link(dve.match_replace(rtk[0:16, (i + 1) % 2, :], rtk[0:16, 4, 8 * i:8 * i + 8], rtk[0:16, i % 2, :], -1.0))
            st(ts(rtk[0:16, 1, :], rtk[0:16, 0, :], 0.0, None, ALU.is_lt))
            st.link(dve.memset(rtk[0:16, 5, :], 1.0))
            st.link(dve.tensor_tensor_scan(rtk[0:16, 2, :], rtk[0:16, 5, :], rtk[0:16, 1, :], 0.0, ALU.mult, ALU.add))
            st.link(tt(rtk[0:16, 3, :], rtk[0:16, 2, :], rtk[0:16, 1, :], ALU.mult))
            dve.nop().then_inc(ev("router_steps"), 1)
            dve.wait_ge(ev("router_products"), 3 + 1)
            st.link(dve.tensor_copy(small[:, 168:200], ps[:, 3, 0:32]))
            for w in range(2):
                st(tt(sel[:, w], small[:, 168 + 16 * w:184 + 16 * w].unsqueeze(2).to_broadcast([P, NE, CAP]),
                      cs("slot").unsqueeze(1).to_broadcast([P, NE, CAP]), ALU.is_equal))
            st.wait()
            for w in range(2):
                st(tt(selg[:, w], sel[:, w], aff[:, w, :].unsqueeze(2).to_broadcast([P, NE, CAP]), ALU.mult))
            st.wait()
            dve.wait_ge(ev("h2tok_copied"), 4)
            dve.nop().then_inc(ev("sel_ready"), 1)
            SX = 4
            with dve.Fori(0, NE) as e:
                st.loop(e, SX)
                for w in range(2):
                    st(dve.tensor_copy(sg4[:, w], selg[:, w, e, :].unsqueeze(1).to_broadcast([P, 4, CAP])))
                st.wait()
                dve.nop().then_inc(ev("sg4_ready"), 1)
                dve.wait_ge(ev("gathered"), e + 1)
                st(dve.tensor_copy(xs, ps[:, 3, 0:256].rearrange("p (k s) -> p k s", k=KT)))
                st(dve.tensor_copy(Gt, ps[:, 3, 256:512]))
                st.wait()
                dve.nop().then_inc(ev("xs_ready"), 1)
                dve.wait_ge(ev("gate_silu"), e + 1)
                dve.wait_ge(ev("units_used"), e * 12 + (U0 + 8))
                tt(he, sa, ps[:, 1, :], ALU.mult).then_inc(ev("hidden"), 1)
                dve.wait_ge(ev("units_used"), e * 12 + (U0 + 12))
                dve.tensor_copy(ye[:, 512:1024], ps[:, 1, :]).then_inc(ev("y_other"), 1)
                dve.wait_ge(ev("y_other"), e + 1)
                dve.wait_ge(ev("y_half"), e + 1)
                dve.nop().then_inc(ev("y_ready"), 1)
                dve.wait_ge(ev("scattered"), e + 1)
            st.close(NE, SX)
            for w in range(2):
                dve.wait_ge(ev("y_root"), w + 1)
                st.link(dve.reciprocal(small[:, 204 + w:205 + w], small[:, 202 + w:203 + w]))
                y = ps[:, 4 + 2 * w:6 + 2 * w, :]
                t = mx.rearrange("p k l -> p (k l)")[:, w * D:w * D + D].rearrange("p (a b) -> p a b", a=2)
                st.link(stt(t, y, small[:, 204 + w:205 + w], gtok.rearrange("p (a b) -> p a b", a=2), ALU.mult, ALU.mult))
                o = otok[:, w, :].rearrange("p (a b) -> p a b", a=2)
                tt(o, o, t, ALU.add).then_inc(ev("out_ready"), 1)


NAMES = ["x", "meta_tokens", "norm1_w", "w_in", "hg_lb_logits", "hg_norm_w", "m2_conv_w", "m2_conv_b", "m2_dt_bias",
         "m2_a_log", "m2_d", "m2_norm_w", "w_out", "norm2_w", "ffn_w_up", "ffn_conv_w", "ffn_conv_b", "ffn_w_down",
         "final_norm_w", "c_2", "ctx_2", "c_ctx_2", "w_ada_2", "b_ada_2", "pre_mix_g_2", "post_mix_g_2", "pre_ffn_g_2",
         "post_ffn_g_2", "w_in_2", "conv_w_2", "conv_b_2", "ret_decay_logit_2", "ret_norm_g_2", "w_out_2",
         "w_router_2", "b_router_2", "w_gate_2", "w_up_2", "w_down_2"]


def kernel(**inputs):
    import concourse.bacc as bacc
    from concourse.bass_utils import run_bass_kernel_spmd

    nc = bacc.Bacc("TRN2", target_bir_lowering=False, num_devices=1, dynamic_dma_scratch_size=1024)
    arrays = {n: np.ascontiguousarray(inputs[n]) for n in NAMES}
    arrays["cst"], arrays["dist"] = constants()
    aps = {n: nc.dram_tensor("in_" + n, v.shape, mybir.dt.from_np(v.dtype), kind="ExternalInput").ap() for n, v in arrays.items()}
    out = nc.dram_tensor("out_y", (1, SEQ, D), F32, kind="ExternalOutput").ap()
    build(nc, aps, out)
    r = run_bass_kernel_spmd(nc, [{"in_" + n: v for n, v in arrays.items()}], core_ids=[0])
    return r.results[0]["out_y"]
```
